# Optimizing a Trainium2 kernel written in Bass

```python
import jax
import jax.numpy as jnp
from jax import lax
import numpy as np
import jax, jax.numpy as jnp

D_MODEL = 1024
BATCH = 1
SEQ = 1024
DEPTH = 1

GRID_W = 64
EPS = 1e-6
ATTN_HEADS = 8
ATTN_KV_HEADS = 2
ATTN_HEAD_DIM = 64
ATTN_WIDTH = ATTN_HEADS * ATTN_HEAD_DIM
KV_WIDTH = ATTN_KV_HEADS * ATTN_HEAD_DIM
Q_BLOCK = 128
ROPE_THETA = 10000.0
MLSTM_HEADS = 4
MLSTM_HEAD_DIM = 128
MLSTM_WIDTH = MLSTM_HEADS * MLSTM_HEAD_DIM
MLSTM_CHUNK = 64
CONV_WIDTH = 5
N_GATES = 4 * MLSTM_HEADS
FORGET_BIAS_LO = 3.0
FORGET_BIAS_HI = 6.0
MIX_WIDTH = ATTN_WIDTH + MLSTM_WIDTH
IN_PROJ_WIDTH = ATTN_WIDTH + 2 * KV_WIDTH + 4 * MLSTM_WIDTH + N_GATES
FFN_HIDDEN = 256 * ((8 * D_MODEL + 3 * 256 - 1) // (3 * 256))


def rms_norm(x, g):
    xf = x.astype(jnp.float32)
    y = xf * lax.rsqrt(jnp.mean(xf * xf, axis=-1, keepdims=True) + EPS)
    return (y * g.astype(jnp.float32)).astype(x.dtype)

def modulate(h, shift, scale):
    return h * (1.0 + scale[:, None, :]) + shift[:, None, :]

def axial_rope_tables(seq):
    rows = seq // GRID_W
    row = jnp.repeat(jnp.arange(rows, dtype=jnp.float32), GRID_W)
    col = jnp.tile(jnp.arange(GRID_W, dtype=jnp.float32), rows)
    axis_dim = ATTN_HEAD_DIM // 2
    inv_freq = ROPE_THETA ** (-jnp.arange(0, axis_dim, 2, dtype=jnp.float32) / axis_dim)
    ang_row = row[:, None] * inv_freq[None, :]
    ang_col = col[:, None] * inv_freq[None, :]
    return (jnp.cos(ang_row), jnp.sin(ang_row), jnp.cos(ang_col), jnp.sin(ang_col))

def rotate_pairs(x, cos, sin):
    x1, x2 = jnp.split(x, 2, axis=-1)
    cos = cos[:, None, :]
    sin = sin[:, None, :]
    return jnp.concatenate([x1 * cos - x2 * sin, x2 * cos + x1 * sin], axis=-1)

def apply_axial_rope(x, tables):
    cos_r, sin_r, cos_c, sin_c = tables
    x_row, x_col = jnp.split(x.astype(jnp.float32), 2, axis=-1)
    out = jnp.concatenate([rotate_pairs(x_row, cos_r, sin_r), rotate_pairs(x_col, cos_c, sin_c)], axis=-1)
    return out.astype(x.dtype)

def axial_gqa_attention(q, k, v, q_g, k_g, tables):
    B, S, _ = q.shape
    G = ATTN_HEADS // ATTN_KV_HEADS
    q = q.reshape(B, S, ATTN_HEADS, ATTN_HEAD_DIM)
    k = k.reshape(B, S, ATTN_KV_HEADS, ATTN_HEAD_DIM)
    v = v.reshape(B, S, ATTN_KV_HEADS, ATTN_HEAD_DIM)
    q = apply_axial_rope(rms_norm(q, q_g), tables)
    k = apply_axial_rope(rms_norm(k, k_g), tables)
    n_blocks = S // Q_BLOCK
    qb = q.reshape(B, n_blocks, Q_BLOCK, ATTN_KV_HEADS, G, ATTN_HEAD_DIM).transpose(1, 0, 3, 4, 2, 5)
    kt = k.transpose(0, 2, 1, 3)
    vt = v.transpose(0, 2, 1, 3)
    scale = ATTN_HEAD_DIM ** -0.5

    def one_block(q_blk):
        s = jnp.einsum('bkgqd,bksd->bkgqs', q_blk, kt).astype(jnp.float32) * scale
        p = jax.nn.softmax(s, axis=-1).astype(vt.dtype)
        return jnp.einsum('bkgqs,bksd->bkgqd', p, vt)

    o = lax.map(one_block, qb)
    return o.transpose(1, 0, 4, 2, 3, 5).reshape(B, S, ATTN_WIDTH)

def mlstm_chunkwise(q, k, v, i_pre, log_f):
    B, H, S, D = q.shape
    L = MLSTM_CHUNK
    nc = S // L

    def to_chunks(a):
        return jnp.moveaxis(a.reshape((B, H, nc, L) + a.shape[3:]), 2, 0)

    xs = (to_chunks(q), to_chunks(k), to_chunks(v), to_chunks(i_pre), to_chunks(log_f))
    tril = jnp.tril(jnp.ones((L, L), dtype=bool))

    def step(carry, chunk):
        C, n, m = carry
        qc, kc, vc, ic, fc = chunk
        b = jnp.cumsum(fc, axis=-1)
        g = b[..., -1]
        d = b[..., :, None] - b[..., None, :] + ic[..., None, :]
        d = jnp.where(tril, d, -jnp.inf)
        m_inter = b + m[..., None]
        m_t = jnp.maximum(m_inter, jnp.max(d, axis=-1))
        w_inter = jnp.exp(m_inter - m_t)
        p = jnp.exp(d - m_t[..., None])
        s = jnp.einsum('bhtd,bhsd->bhts', qc, kc) * p
        num = w_inter[..., None] * jnp.einsum('bhvd,bhtd->bhtv', C, qc) + jnp.einsum('bhts,bhsv->bhtv', s, vc)
        den = w_inter * jnp.einsum('bhd,bhtd->bht', n, qc) + jnp.sum(s, axis=-1)
        h = num / jnp.maximum(jnp.abs(den), jnp.exp(-m_t))[..., None]
        a = g[..., None] - b + ic
        m_new = jnp.maximum(g + m, jnp.max(a, axis=-1))
        decay = jnp.exp(g + m - m_new)
        w = jnp.exp(a - m_new[..., None])
        C = decay[..., None, None] * C + jnp.einsum('bhs,bhsv,bhsd->bhvd', w, vc, kc)
        n = decay[..., None] * n + jnp.einsum('bhs,bhsd->bhd', w, kc)
        return (C, n, m_new), h

    init = (jnp.zeros((B, H, D, D), jnp.float32), jnp.zeros((B, H, D), jnp.float32), jnp.zeros((B, H), jnp.float32))
    _, h = lax.scan(step, init, xs)
    return jnp.moveaxis(h, 0, 2).reshape(B, H, S, D)

def centred_depthwise_conv(x, w, b):
    ch = x.shape[-1]
    y = lax.conv_general_dilated(x, w[:, None, :].astype(x.dtype), window_strides=(1,),
                                 padding=[(CONV_WIDTH // 2, CONV_WIDTH // 2)],
                                 dimension_numbers=('NWC', 'WIO', 'NWC'), feature_group_count=ch)
    return y + b.astype(x.dtype)

def bidirectional_mlstm(qk_pre, v, o_pre, gate_pre, conv_w, conv_b, gate_b, norm_g):
    B, S, _ = v.shape
    qk = jax.nn.silu(centred_depthwise_conv(qk_pre, conv_w, conv_b))
    q, k = jnp.split(qk, 2, axis=-1)

    def heads(a):
        return a.astype(jnp.float32).reshape(B, S, MLSTM_HEADS, MLSTM_HEAD_DIM).transpose(0, 2, 1, 3)

    qh = heads(q)
    kh = heads(k) * MLSTM_HEAD_DIM ** -0.5
    vh = heads(v)
    g = (gate_pre.astype(jnp.float32) + gate_b.astype(jnp.float32)).reshape(B, S, 4, MLSTM_HEADS)
    g = g.transpose(2, 0, 3, 1)
    i_fw, f_fw, i_bw, f_bw = g[0], g[1], g[2], g[3]
    h_fw = mlstm_chunkwise(qh, kh, vh, i_fw, jax.nn.log_sigmoid(f_fw))
    flip = lambda a: jnp.flip(a, axis=2)
    h_bw = flip(mlstm_chunkwise(flip(qh), flip(kh), flip(vh), flip(i_bw), flip(jax.nn.log_sigmoid(f_bw))))
    h = (h_fw + h_bw).transpose(0, 2, 1, 3)
    h = h * lax.rsqrt(jnp.mean(h * h, axis=-1, keepdims=True) + EPS)
    h = h * norm_g.astype(jnp.float32).reshape(MLSTM_HEADS, MLSTM_HEAD_DIM)
    h = h.reshape(B, S, MLSTM_WIDTH) * jax.nn.sigmoid(o_pre.astype(jnp.float32))
    return h.astype(v.dtype)

def first_inputs(seed: int = 0) -> dict:
    key = jax.random.key(seed)
    ks = jax.random.split(key, 18)
    nrm = lambda k, shape, s: jax.random.normal(k, shape, jnp.float32) * s
    gain = lambda k, shape: 1.0 + nrm(k, shape, 0.02)
    f_bias = jnp.linspace(FORGET_BIAS_LO, FORGET_BIAS_HI, MLSTM_HEADS, dtype=jnp.float32)
    gate_offset = jnp.zeros((4, MLSTM_HEADS), jnp.float32).at[1].set(f_bias).at[3].set(f_bias)
    gate_b = (nrm(ks[10], (DEPTH, 4, MLSTM_HEADS), 0.1) + gate_offset).reshape(DEPTH, N_GATES)
    return {
        'x': nrm(ks[0], (BATCH, SEQ, D_MODEL), 1.0),
        'c': nrm(ks[1], (BATCH, D_MODEL), 1.0),
        'w_ada': nrm(ks[2], (DEPTH, D_MODEL, 6 * D_MODEL), D_MODEL ** -0.5),
        'b_ada': nrm(ks[3], (DEPTH, 6 * D_MODEL), 0.02),
        'norm_mix_g': gain(ks[4], (DEPTH, D_MODEL)),
        'w_in': nrm(ks[5], (DEPTH, D_MODEL, IN_PROJ_WIDTH), D_MODEL ** -0.5),
        'q_norm_g': gain(ks[6], (DEPTH, ATTN_HEAD_DIM)),
        'k_norm_g': gain(ks[7], (DEPTH, ATTN_HEAD_DIM)),
        'conv_w': nrm(ks[8], (DEPTH, CONV_WIDTH, 2 * MLSTM_WIDTH), CONV_WIDTH ** -0.5),
        'conv_b': nrm(ks[9], (DEPTH, 2 * MLSTM_WIDTH), 0.02),
        'gate_b': gate_b,
        'mlstm_norm_g': gain(ks[11], (DEPTH, MLSTM_WIDTH)),
        'w_out': nrm(ks[12], (DEPTH, MIX_WIDTH, D_MODEL), MIX_WIDTH ** -0.5),
        'norm_ffn_g': gain(ks[13], (DEPTH, D_MODEL)),
        'w_gate': nrm(ks[14], (DEPTH, D_MODEL, FFN_HIDDEN), D_MODEL ** -0.5),
        'w_up': nrm(ks[15], (DEPTH, D_MODEL, FFN_HIDDEN), D_MODEL ** -0.5),
        'w_down': nrm(ks[16], (DEPTH, FFN_HIDDEN, D_MODEL), FFN_HIDDEN ** -0.5),
        'final_norm_g': gain(ks[17], (D_MODEL,)),
    }

def first_block(x, c, w_ada, b_ada, norm_mix_g, w_in, q_norm_g, k_norm_g, conv_w, conv_b, gate_b,
              mlstm_norm_g, w_out, norm_ffn_g, w_gate, w_up, w_down, final_norm_g):
    S = x.shape[1]
    tables = axial_rope_tables(S)
    cond = jax.nn.silu(c)
    splits = [ATTN_WIDTH,
              ATTN_WIDTH + KV_WIDTH,
              ATTN_WIDTH + 2 * KV_WIDTH,
              ATTN_WIDTH + 2 * KV_WIDTH + 2 * MLSTM_WIDTH,
              ATTN_WIDTH + 2 * KV_WIDTH + 3 * MLSTM_WIDTH,
              ATTN_WIDTH + 2 * KV_WIDTH + 4 * MLSTM_WIDTH]
    for l in range(DEPTH):
        mod = cond @ w_ada[l] + b_ada[l]
        sh1, sc1, g1, sh2, sc2, g2 = jnp.split(mod, 6, axis=-1)
        h = modulate(rms_norm(x, norm_mix_g[l]), sh1, sc1)
        proj = h @ w_in[l]
        q_a, k_a, v_a, qk_m, v_m, o_m, gates = jnp.split(proj, splits, axis=-1)
        y_attn = axial_gqa_attention(q_a, k_a, v_a, q_norm_g[l], k_norm_g[l], tables)
        y_mem = bidirectional_mlstm(qk_m, v_m, o_m, gates, conv_w[l], conv_b[l], gate_b[l], mlstm_norm_g[l])
        mix = jnp.concatenate([y_attn, y_mem], axis=-1) @ w_out[l]
        x = x + g1[:, None, :] * mix
        h = modulate(rms_norm(x, norm_ffn_g[l]), sh2, sc2)
        ffn = (jax.nn.silu(h @ w_gate[l]) * (h @ w_up[l])) @ w_down[l]
        x = x + g2[:, None, :] * ffn
    return rms_norm(x, final_norm_g)


HEAD_DIM = 64
MIX_WIDTH_2 = D_MODEL
FOX_HEADS = (MIX_WIDTH_2 // 2) // HEAD_DIM
SWA_Q_HEADS = (MIX_WIDTH_2 // 2) // HEAD_DIM
SWA_KV_HEADS = 2
SWA_GROUP = SWA_Q_HEADS // SWA_KV_HEADS
WINDOW = 128
RMS_EPS = 1e-6
FOX_W = FOX_HEADS * HEAD_DIM
SWA_W = SWA_Q_HEADS * HEAD_DIM
SWA_KV_W = SWA_KV_HEADS * HEAD_DIM
IN_SIZES = (FOX_W, FOX_W, FOX_W, FOX_HEADS, FOX_W, SWA_W, SWA_KV_W, SWA_KV_W, SWA_W)
IN_WIDTH = FOX_W * 4 + FOX_HEADS + SWA_W * 2 + SWA_KV_W * 2


def rms_norm_2(x, g):
    xf = x.astype(jnp.float32)
    y = xf * lax.rsqrt(jnp.mean(xf * xf, axis=-1, keepdims=True) + RMS_EPS)
    return (y * g.astype(jnp.float32)).astype(x.dtype)

def rope(x, positions):
    half = HEAD_DIM // 2
    inv_freq = ROPE_THETA ** (-jnp.arange(half, dtype=jnp.float32) / half)
    ang = positions.astype(jnp.float32)[..., None] * inv_freq
    cos = jnp.cos(ang)[:, :, None, :]
    sin = jnp.sin(ang)[:, :, None, :]
    xf = x.astype(jnp.float32)
    x1, x2 = xf[..., :half], xf[..., half:]
    return jnp.concatenate([x1 * cos - x2 * sin, x2 * cos + x1 * sin], axis=-1).astype(x.dtype)

def forgetting_attention(q, k, v, f_logit):
    B, S, H, d = q.shape
    nb = S // Q_BLOCK
    cum = jnp.cumsum(jax.nn.log_sigmoid(f_logit.astype(jnp.float32)), axis=1)
    cum = cum.transpose(0, 2, 1)
    kh = k.transpose(0, 2, 1, 3)
    vh = v.transpose(0, 2, 1, 3)
    q_blocks = q.transpose(0, 2, 1, 3).reshape(B, H, nb, Q_BLOCK, d).transpose(2, 0, 1, 3, 4)
    c_blocks = cum.reshape(B, H, nb, Q_BLOCK).transpose(2, 0, 1, 3)
    key_pos = jnp.arange(S)
    scale = d ** -0.5

    def one_block(args):
        qb, cb, n = args
        s = jnp.einsum('bhqd,bhkd->bhqk', qb, kh, preferred_element_type=jnp.float32) * scale
        s = s + cb[..., None] - cum[:, :, None, :]
        q_pos = n * Q_BLOCK + jnp.arange(Q_BLOCK)
        causal = key_pos[None, :] <= q_pos[:, None]
        s = jnp.where(causal, s, -jnp.inf)
        p = jax.nn.softmax(s, axis=-1)
        return jnp.einsum('bhqk,bhkd->bhqd', p.astype(vh.dtype), vh)

    out = lax.map(one_block, (q_blocks, c_blocks, jnp.arange(nb)))
    return out.transpose(1, 0, 3, 2, 4).reshape(B, S, H * d)

def sliding_window_sink_attention(q, k, v, sinks):
    B, S, _, d = q.shape
    nb = S // Q_BLOCK
    qb = q.reshape(B, nb, Q_BLOCK, SWA_KV_HEADS, SWA_GROUP, d)

    def with_prev(t):
        t = t.reshape(B, nb, Q_BLOCK, SWA_KV_HEADS, d)
        prev = jnp.pad(t[:, :-1], ((0, 0), (1, 0), (0, 0), (0, 0), (0, 0)))
        return jnp.concatenate([prev, t], axis=2)

    kk, vv = with_prev(k), with_prev(v)
    s = jnp.einsum('bnqhgd,bnshd->bnhgqs', qb, kk, preferred_element_type=jnp.float32) * (d ** -0.5)
    i = jnp.arange(Q_BLOCK)[:, None]
    j = jnp.arange(2 * Q_BLOCK)[None, :]
    rel = i + Q_BLOCK - j
    band = (rel >= 0) & (rel < WINDOW)
    valid_blk = (jnp.arange(nb)[:, None, None] > 0) | (j[None] >= Q_BLOCK)
    mask = band[None] & valid_blk
    s = jnp.where(mask[None, :, None, None], s, -jnp.inf)
    sink = jnp.broadcast_to(
        sinks.astype(jnp.float32).reshape(SWA_KV_HEADS, SWA_GROUP)[None, None, :, :, None, None],
        s.shape[:-1] + (1,))
    p = jax.nn.softmax(jnp.concatenate([s, sink], axis=-1), axis=-1)[..., :-1]
    out = jnp.einsum('bnhgqs,bnshd->bnqhgd', p.astype(vv.dtype), vv)
    return out.reshape(B, S, SWA_Q_HEADS * d)

def second_inputs(seed: int = 0) -> dict:
    key = jax.random.key(seed)
    ks = jax.random.split(key, 12)
    x = jax.random.normal(ks[0], (BATCH, SEQ, D_MODEL), jnp.float32)
    c = jax.random.normal(ks[1], (BATCH, D_MODEL), jnp.float32)
    positions = jnp.broadcast_to(jnp.arange(SEQ, dtype=jnp.int32)[None, :], (BATCH, SEQ))
    w_ada = jax.random.normal(ks[2], (DEPTH, D_MODEL, 3 * D_MODEL), jnp.float32) * (0.5 * D_MODEL ** -0.5)
    b_ada = jax.random.normal(ks[3], (DEPTH, 3 * D_MODEL), jnp.float32) * 0.02
    g_pre = 1.0 + 0.1 * jax.random.normal(ks[4], (DEPTH, D_MODEL), jnp.float32)
    w_in = jax.random.normal(ks[5], (DEPTH, D_MODEL, IN_WIDTH), jnp.float32) * D_MODEL ** -0.5
    b_fgate = jax.random.uniform(ks[6], (DEPTH, FOX_HEADS), jnp.float32, 1.0, 4.0)
    sinks = jax.random.normal(ks[7], (DEPTH, SWA_Q_HEADS), jnp.float32)
    w_out = jax.random.normal(ks[8], (DEPTH, MIX_WIDTH_2, D_MODEL), jnp.float32) * MIX_WIDTH_2 ** -0.5
    g_post = 1.0 + 0.1 * jax.random.normal(ks[9], (DEPTH, D_MODEL), jnp.float32)
    return {"x": x, "c": c, "positions": positions, "w_ada": w_ada, "b_ada": b_ada,
            "g_pre": g_pre, "w_in": w_in, "b_fgate": b_fgate, "sinks": sinks,
            "w_out": w_out, "g_post": g_post}

def second_block(x, c, positions, w_ada, b_ada, g_pre, w_in, b_fgate, sinks, w_out, g_post):
    B, S, _ = x.shape
    split_points = [int(v) for v in np.cumsum(IN_SIZES)[:-1]]
    for l in range(DEPTH):
        mod = jax.nn.silu(c) @ w_ada[l] + b_ada[l]
        shift, scale, gate = jnp.split(mod, 3, axis=-1)
        h = rms_norm_2(x, g_pre[l]) * (1.0 + scale[:, None, :]) + shift[:, None, :]
        proj = h @ w_in[l]
        qa, ka, va, fa, za, qb, kb, vb, zb = jnp.split(proj, split_points, axis=-1)
        oa = forgetting_attention(
            qa.reshape(B, S, FOX_HEADS, HEAD_DIM),
            ka.reshape(B, S, FOX_HEADS, HEAD_DIM),
            va.reshape(B, S, FOX_HEADS, HEAD_DIM),
            fa + b_fgate[l])
        oa = oa * jax.nn.silu(za)
        qb = rope(qb.reshape(B, S, SWA_Q_HEADS, HEAD_DIM), positions)
        kb = rope(kb.reshape(B, S, SWA_KV_HEADS, HEAD_DIM), positions)
        ob = sliding_window_sink_attention(qb, kb, vb.reshape(B, S, SWA_KV_HEADS, HEAD_DIM), sinks[l])
        ob = ob * jax.nn.silu(zb)
        y = jnp.concatenate([oa, ob], axis=-1) @ w_out[l]
        x = x + gate[:, None, :] * rms_norm_2(y, g_post[l])
    return x


def setup_inputs(seed=0):
    out = dict(first_inputs(seed))
    for name, value in second_inputs(seed + 1).items():
        if name != "x":
            out[name + "_2"] = value
    return out


def reference(
    x, c, w_ada, b_ada, norm_mix_g, w_in, q_norm_g, k_norm_g, conv_w, conv_b, gate_b,
    mlstm_norm_g, w_out, norm_ffn_g, w_gate, w_up, w_down, final_norm_g, c_2, positions_2,
    w_ada_2, b_ada_2, g_pre_2, w_in_2, b_fgate_2, sinks_2, w_out_2, g_post_2,
):
    x = first_block(
        x, c, w_ada, b_ada, norm_mix_g, w_in, q_norm_g, k_norm_g, conv_w, conv_b, gate_b,
        mlstm_norm_g, w_out, norm_ffn_g, w_gate, w_up, w_down, final_norm_g,
    )
    return second_block(
        x, c_2, positions_2, w_ada_2, b_ada_2, g_pre_2, w_in_2, b_fgate_2, sinks_2, w_out_2,
        g_post_2,
    )


_drawn_inputs = setup_inputs


def setup_inputs(seed=0):
    import zlib

    import numpy as np

    out = dict(_drawn_inputs(seed))
    spreads = {}
    factors = {'norm_mix_g': 8.0,
     'q_norm_g': 8.0,
     'k_norm_g': 8.0,
     'conv_b': 200.0,
     'mlstm_norm_g': 33.208,
     'norm_ffn_g': 3.961,
     'final_norm_g': 8.108,
     'sinks_2': 64.0,
     'b_ada_2': 5.733,
     'g_pre_2': 3.399,
     'g_post_2': 13.622}
    for name, (base, spread) in spreads.items():
        noise = np.random.default_rng([zlib.crc32(name.encode()), seed]).standard_normal(out[name].shape)
        drawn = base * np.exp(spread * noise) if base else spread * noise
        out[name] = jnp.asarray(drawn.astype(out[name].dtype))
    for name, factor in factors.items():
        out[name] = (out[name] * factor).astype(out[name].dtype)
    return out
```

```python
from contextlib import ExitStack, contextmanager

import numpy as np

import concourse.bass as bass
from concourse import mybir

ALU = mybir.AluOpType
ACT = mybir.ActivationFunctionType
AX_X = mybir.AxisListType.X
F32 = mybir.dt.float32
F32R = mybir.dt.float32r
BF16 = mybir.dt.bfloat16
I32 = mybir.dt.int32

P = 128
D = 1024
T = 1024
HT = 512
KT = D // P
FFN = 2816
FT = FFN // P
EPS = 1e-6
SC = 64 ** -0.5
KSC = 128 ** -0.5
NEG = -1e30
RING = 2
CW = 256

QM, QA, KA, VA, VM, OM, GA = 0, 8, 12, 13, 14, 18, 22
N_IN1 = 23
FQ, FK, FV, FZ, SQ, SK, SV, SZ, FG = 0, 4, 8, 12, 16, 20, 21, 22, 26
N_IN2 = 27



class Count:

    def __init__(self, handle):
        self.handle, self.now = handle, 0


class Point:

    def __init__(self):
        self.count = None

    def set(self, count, by, loops):
        count.now += by
        self.count, self.first, self.loops = count, count.now, list(loops)
        return self

    def value(self, lag):
        v, inner = self.first, [x for x in self.loops if x.i is not None]
        for x in self.loops:
            step = x.step.get(self.count, 0)
            if x.i is None:
                v = v + (x.n - 1) * step
            elif step:
                v = x.i * step + v
        if lag:
            v = v - lag * inner[-1].step.get(self.count, 0)
        return v


class Loop:
    def __init__(self, n):
        self.n, self.i, self.step = n, None, {}


class Queue:

    def __init__(self, prog, count):
        self.prog, self.done, self.levels = prog, count, [[]]

    def __call__(self, fn, *waits, mark=True, sem=None, by=1, point=None):
        p = (point or Point()) if mark else None
        if p:
            p.set(sem or self.done, by, self.prog.loops)

        def emit(e):
            for w in waits:
                w, lag = w if isinstance(w, tuple) else (w, 0)
                e.wait_ge(w.count.handle, w.value(lag))
            ins = fn(e)
            if p:
                ins.then_inc(p.count.handle, by)

        self.levels[-1].append(emit)
        return p

    def wait(self, *waits):
        def emit(e):
            for w in waits:
                w, lag = w if isinstance(w, tuple) else (w, 0)
                e.wait_ge(w.count.handle, w.value(lag))

        self.levels[-1].append(emit)

    def run(self, e, items=None):
        for x in self.levels[0] if items is None else items:
            if isinstance(x, tuple):
                loop, body = x
                with e.Fori(0, loop.n) as i:
                    loop.i = i
                    self.run(e, body)
                loop.i = None
            else:
                x(e)


class Program:

    def __init__(self, nc, ctx):
        self.nc, self.ctx, self.loops, self.counts = nc, ctx, [], []
        self.pe, self.act, self.dve, self.pool, self.sp = (
            Queue(self, self.count(n)) for n in ("pe_done", "act_done", "dve_done", "pool_done", "sp_done"))
        self.queues = [self.pe, self.act, self.dve, self.pool, self.sp]

    def count(self, name):
        c = Count(self.ctx.enter_context(self.nc.semaphore(name)))
        self.counts.append(c)
        return c

    def start_high(self, by=256):
        for q in self.queues[:4]:
            h = q.done.handle
            q.levels[-1].append(lambda e, h=h: e.sem_inc(h, by))
            q.done.now += by

    @contextmanager
    def loop(self, n):
        x, before = Loop(n), {c: c.now for c in self.counts}
        for q in self.queues:
            q.levels.append([])
        self.loops.append(x)
        yield x
        self.loops.pop()
        for q in self.queues:
            body = q.levels.pop()
            if body:
                q.levels[-1].append((x, body))
        for c in self.counts:
            x.step[c] = c.now - before.get(c, 0)
            c.now += (n - 1) * x.step[c]

    def last(self, q):
        p = Point()
        p.count, p.first, p.loops = q.done, q.done.now, []
        return p

    def meet(self, *queues):
        ends = [(q, self.last(q)) for q in (self.pe, self.act, self.dve, self.pool)]
        for q in queues or self.queues:
            q.wait(*[p for o, p in ends])


def at(x, i):
    return x[:, i]


class Weights:

    def __init__(self, g, dram, place):
        self.g, self.dram = g, dram
        self.raw = [place(f"w_raw{s}", [P, KT * P], F32) for s in range(RING)]
        self.hi = [place(f"w_hi{s}", [P, KT * P], F32R) for s in range(RING)]
        self.lo = [place(f"w_lo{s}", [P, KT * P], F32R) for s in range(RING)]
        self.landed = [g.count(f"w_landed{s}") for s in range(RING)]
        self.n = 0
        self.phase = 0
        self.used = [None]
        self.split = []

    def fetch(self, slot, index, raw_free, used, split_point=None):
        g, raw, hi, lo = self.g, self.raw[slot], self.hi[slot], self.lo[slot]
        landed = g.sp(lambda e: e.dma_start(raw[:, :], self.dram[index()]), *raw_free,
                      sem=self.landed[slot], by=16)
        rounded = g.act(lambda e: e.activation(hi[:, :], raw[:, :], ACT.Copy), landed, *used)
        return g.dve(lambda e: e.tensor_tensor(lo[:, :], raw[:, :], hi[:, :].bitcast(F32), ALU.subtract),
                     rounded, point=split_point)

    def first(self):
        self.split = [None, self.fetch(0, lambda: 0, (), ())]

    def run(self, nb, loop, work, then=None):
        base, g = self.n, self.g
        used, split = [Point() for _ in range(nb)], [Point() for _ in range(nb)]
        if loop:
            assert nb % RING == 0
        for j in range(nb):
            slot = (self.phase + j) % RING
            if loop:
                at_step = (lambda jj: lambda: loop.i * nb + (base + jj + 1))(j)
                free = [split[j - 2] if j > 1 else (split[j - 2], 1)]
                was_used = [used[j - 1] if j else (used[nb - 1], 1)]
                ready = split[j - 1] if j else (split[nb - 1], 1)
            else:
                index = base + j + 1 if j < nb - 1 or then is None else then
                at_step = (lambda index: lambda: index)(index)
                back = lambda pts, old, k: pts[k] if k >= 0 else old[k]
                free = [x for x in [back(split, self.split, j - 2)] if x]
                was_used = [x for x in [back(used, self.used, j - 1)] if x]
                ready = back(split, self.split, j - 1)
            if loop or index >= 0:
                self.fetch((slot + 1) % RING, at_step, free, was_used, split[j])
            work(j, slot, ready, used[j])
        if not loop:
            self.used, self.split, self.n = (self.used + used)[-2:], (self.split + split)[-2:], base + nb
            self.n = self.n if then is None else then
            self.phase += nb
        else:
            self.used, self.split, self.n = used[-2:], split[-2:], base + nb * loop.n

    def enter(self):
        g = self.g
        last_used = [x for x in self.used[-1:] if x]
        g.sp.wait(self.split[-1])
        g.act.wait(*last_used)
        g.dve.wait(*last_used)
        g.pe.wait(self.split[-1])


def product(g, w, slot, out, moving, k0, nk, first, last, waits, point, made=None):
    hi, lo = w.hi[slot], w.lo[slot]
    for k in range(nk):
        for n, (mh, ml) in enumerate(moving):
            for a, b, which in ((hi, mh, 0), (hi, ml, 1), (lo, mh, 2)):
                wt = list(waits) if (k == 0 and n == 0 and which == 0) else []
                if made and n == 0 and which == 0:
                    wt.append(made[k])
                end = k == nk - 1 and n == len(moving) - 1 and which == 2
                g.pe(lambda e, a=a, b=b, k=k, n=n, which=which: e.matmul(
                    out[n], a[:, k * P:(k + 1) * P], b(k0 + k),
                    start=(first and k == 0 and which == 0),
                    stop=(last and k == nk - 1 and which == 2)),
                    *wt, mark=end, point=point if end else None)



BASE = 16512
K1 = 1024

SMALL = {}
_at = 0
for _name, _n in (("c", 8), ("c_2", 8), ("b_ada", 48), ("b_ada_2", 24), ("norm_mix_g", 8), ("norm_ffn_g", 8),
                  ("final_norm_g", 8), ("g_pre_2", 8), ("g_post_2", 8), ("qk_g", 5), ("conv_w", 40),
                  ("conv_b", 8), ("gate_b", 1), ("mlstm_norm_g", 4), ("b_fgate", 1), ("sinks", 8),
                  ("eps", 1), ("tiny", 1), ("one", 1), ("half_pi", 1), ("inv_freq", 1), ("rope_sign", 1)):
    SMALL[_name] = (_at, _n)
    _at += _n
N_SMALL = _at


def build(nc, a, out):
    with ExitStack() as ctx:
        g = Program(nc, ctx)
        ps = ctx.enter_context(nc.psum_tensor("ps", [P, 8, HT], F32))

        class Area:

            def __init__(self, start_kb, end_kb):
                self.at, self.end = int(start_kb * K1), int(end_kb * K1)

            def __call__(self, name, shape, dt):
                size = int(np.prod(shape[1:])) * (2 if dt == BF16 else 4)
                t = nc.alloc_sbuf_tensor_at(name, shape, dt, offset=BASE + self.at)
                self.at += (size + 31) // 32 * 32
                assert self.at <= self.end, name
                return t

        fixed = Area(198, 207.5)
        w = Weights(g, a["weights"], Area(174, 198))
        small = fixed("small", [P, N_SMALL], F32)
        ident = fixed("ident", [P, P], F32)
        ones = fixed("ones", [P, P], F32)
        pair_ones = fixed("pair_ones", [P, P], F32)
        ident_b = fixed("ident_b", [P, P], BF16)
        low_keep = fixed("low_keep", [P, P], BF16)
        up_keep = fixed("up_keep", [P, P], BF16)
        band_keep = fixed("band_keep", [P, P], BF16)
        band_keep_t = fixed("band_keep_t", [P, P], BF16)
        mod1 = fixed("mod1", [P, 48], F32)
        mod2 = fixed("mod2", [P, 24], F32)
        cs = fixed("cs", [P, 16], F32)
        s_mix = fixed("s_mix", [P, KT], F32)
        s_ffn = fixed("s_ffn", [P, KT], F32)
        s_pre = fixed("s_pre", [P, KT], F32)
        s_post = fixed("s_post", [P, KT], F32)

        def col(name, i=0):
            o, n = SMALL[name]
            return small[:, bass.ds(o + i, 1)] if not isinstance(i, int) else small[:, o + i:o + i + 1]

        pe, act, dve, pool, sp = g.pe, g.act, g.dve, g.pool, g.sp
        g.start_high()

        c_small = g.count("c_small")
        c_const = g.count("c_const")
        got_small = sp(lambda e: e.dma_start(small[:, :], a["small"]), sem=c_small, by=16)
        for n, t in enumerate((ident, ones, pair_ones)):
            got_const = sp(lambda e, n=n, t=t: e.dma_start(t[:, :], a["consts"][n]), sem=c_const, by=16)
        cmask = Area(0, 64)("cmask", [P, 5, P], F32)
        got_const = sp(lambda e: e.dma_start(cmask[:, :, :], a["consts"][3:8].rearrange("n p c -> p n c")),
                       sem=c_const, by=16)

        xt = Area(64, 96)("xt", [P, KT, T], F32)
        ada = Area(156, 174)
        wa = [ada(f"wa{s}", [P, KT, CW], F32) for s in range(2)]
        acc_a = [ada(f"acc_a{s}", [P, CW], F32) for s in range(2)]
        wa_landed = [g.count(f"wa_landed{s}") for s in range(2)]
        c_x = g.count("c_x")

        cs_done = act(lambda e: e.activation(cs[:, :], small[:, 0:16], ACT.Silu), got_small)
        for n, t in enumerate((ident_b, low_keep, up_keep, band_keep, band_keep_t)):
            masks_done = pool(lambda e, n=n, t=t: e.tensor_copy(t[:, :], cmask[:, n, :]), got_const)

        class Ada:
            def __init__(self):
                self.acc_used = [None, None]
                self.acc_done = [None, None]
                self.ps_used = None

            def block(self, slot, index, vec, out_cols, bias_cols, lag=None):
                mk = lag or {}
                free = mk.get("acc_done") or self.acc_done[slot]
                landed = sp(lambda e: e.dma_start(wa[slot][:, :, :], a["ada"][index()]),
                            *([free] if free else []), sem=wa_landed[slot], by=16)
                used = mk.get("acc_used") or self.acc_used[slot]
                p = None
                for k in range(KT):
                    wk = [landed, cs_done] if k == 0 else [p]
                    if k == 0 and used:
                        wk.append(used)
                    if k == 0:
                        p = dve(lambda e, k=k: e.tensor_scalar(acc_a[slot][:, :], wa[slot][:, k, :],
                                cs[:, vec + k:vec + k + 1], None, ALU.mult), *wk)
                    else:
                        p = dve(lambda e, k=k: e.scalar_tensor_tensor(
                            acc_a[slot][:, :], wa[slot][:, k, :], cs[:, vec + k:vec + k + 1], acc_a[slot][:, :],
                            ALU.mult, ALU.add), *wk, point=mk.get("new_acc_done") if k == KT - 1 else None)
                self.acc_done[slot] = p
                ps_used = mk.get("ps_used") or self.ps_used
                for h in range(2):
                    u = pe(lambda e, h=h: e.matmul(ps[:, 7, h:h + 1], acc_a[slot][:, h * P:(h + 1) * P], ones[:, 0:1],
                                                   start=(h == 0), stop=True, skip_group_check=True),
                           *(([p, got_const] + ([ps_used] if ps_used else [])) if h == 0 else []), mark=(h == 1),
                           point=mk.get("new_acc_used") if h == 1 else None)
                self.acc_used[slot] = u
                self.ps_used = dve(lambda e: e.tensor_tensor(out_cols(), ps[:, 7, 0:2], bias_cols(), ALU.add),
                                   u, point=mk.get("new_ps_used"))

        ada_m = Ada()

        def ada_static(i):
            if i < 24:
                o = SMALL["b_ada"][0]
                ada_m.block(i % 2, lambda: i, 0, lambda: mod1[:, 2 * i:2 * i + 2], lambda: small[:, o + 2 * i:o + 2 * i + 2])
            else:
                j, o = i - 24, SMALL["b_ada_2"][0]
                ada_m.block(i % 2, lambda: i, 8, lambda: mod2[:, 2 * j:2 * j + 2], lambda: small[:, o + 2 * j:o + 2 * j + 2])

        x_in = [sp(lambda e, n=n: e.dma_start(xt[:, 4 * n:4 * n + 4, :], a["x"][4 * n:4 * n + 4].rearrange("k p t -> p k t")),
                   sem=g.count(f"c_x{n}"), by=16) for n in range(2)]
        w.first()
        for i in range(8):
            ada_static(i)

        hA = Area(0, 64)
        h_hi = hA("h_hi", [P, KT, T], F32R)
        h_lo = hA("h_lo", [P, KT, T], F32R)
        nrm = Area(96, 130)
        sq = [nrm(f"sq{s}", [P, HT], F32) for s in range(2)]
        tt = [nrm(f"tt{s}", [P, HT], F32) for s in range(2)]
        acc = [nrm(f"acc{s}", [P, HT], F32) for s in range(2)]
        rstd = [nrm(f"rstd{s}", [P, HT], F32) for s in range(2)]

        def scale_col(dst, gain, sc_at, mod, *waits):
            o, n = SMALL[gain]
            return dve(lambda e: e.scalar_tensor_tensor(dst[:, :], mod[:, sc_at:sc_at + KT], 1.0, small[:, o:o + n],
                                                        ALU.add, ALU.mult), *waits)

        def square_sum(src, sq, acc, *waits):
            p = dve(lambda e: e.memset(acc[:, :], 0.0))
            read = [None, None]
            for k in range(KT):
                s = k % 2
                q = act(lambda e, k=k, s=s: e.activation(sq[s][:, :], src(k), ACT.Square),
                        *(list(waits) if k == 0 else []), *([read[s]] if read[s] else []))
                p = dve(lambda e, s=s: e.tensor_tensor(acc[:, :], acc[:, :], sq[s][:, :], ALU.add), q, p)
                read[s] = p
            return p

        def inverse_norm(acc, bank, dst, *waits):
            m = pe(lambda e: e.matmul(ps[:, bank, :], ones[:, :], acc[:, :], start=True, stop=True), *waits)
            l = act(lambda e: e.activation(dst[:, :], ps[:, bank, :], ACT.Ln, bias=col("eps"), scale=1.0 / D), m)
            return act(lambda e: e.activation(dst[:, :], dst[:, :], ACT.Exp, scale=-0.5), l)

        def modulate(src, rs, scale, shift, hi, lo, tt, *waits):
            free = [None, None]
            for k in range(KT):
                s = k % 2
                t1 = dve(lambda e, k=k, s=s: e.tensor_tensor(tt[s][:, :], src(k), rs[:, :], ALU.mult),
                         *(waits if k == 0 else ()), *([free[s]] if free[s] else []))
                t2 = act(lambda e, k=k, s=s: e.activation(tt[s][:, :], tt[s][:, :], ACT.Identity,
                                                          bias=shift(k), scale=scale(k)), t1)
                t3 = act(lambda e, k=k, s=s: e.activation(hi(k), tt[s][:, :], ACT.Copy), t2)
                free[s] = dve(lambda e, k=k, s=s: e.tensor_tensor(lo(k), tt[s][:, :], hi(k).bitcast(F32), ALU.subtract), t3)
            return free[(KT - 1) % 2]

        sm_done = scale_col(s_mix, "norm_mix_g", 8, mod1, ada_m.ps_used)
        def mix_norm(n):
            ts = slice(n * HT, (n + 1) * HT)
            p = square_sum(lambda k: xt[:, k, ts], sq, acc[n], *x_in, masks_done)
            r = inverse_norm(acc[n], 4 + n, rstd[n], p, got_const)
            return modulate(lambda k: xt[:, k, ts], rstd[n], lambda k: s_mix[:, k:k + 1], lambda k: mod1[:, k:k + 1],
                            lambda k: h_hi[:, k, ts], lambda k: h_lo[:, k, ts], tt, r, sm_done)

        for n in range(2):
            h_done = mix_norm(n)

        y = Area(64, 156)("y", [P, N_IN1, T], F32)

        def project(n_tiles, dst, extra=None, func=ACT.Copy):
            state, parts = {}, (h_hi_cur, h_lo_cur)

            def work(j, slot, ready, used, lp=None, nb=1, first_evac=(None, None)):
                bank = 2 * (j % 2)
                waits = [ready] + ([state["evac"][j]] if lp is None and j in state.get("evac", {}) else [])
                if lp is not None:
                    waits.append((evac_pt[j], 1))
                elif prev_evac[j % 2]:
                    waits.append(prev_evac[j % 2])
                mov = [(lambda k, n=n: parts[0](k, n), lambda k, n=n: parts[1](k, n)) for n in range(2)]
                product(g, w, slot, [ps[:, bank + n, :] for n in range(2)], mov, 0, KT, True, True, waits, used)
                prev_evac[j % 2] = act(lambda e, j=j: e.activation(dst(lp.i * 2 + j if lp else j), ps[:, bank:bank + 2, :]
                                                                    .rearrange("p a b -> p (a b)"), func),
                                       used, point=evac_pt[j] if lp is not None else None)
                if extra:
                    extra(j, lp)

            evac_pt = [Point(), Point()]
            if n_tiles > 1:
                w.enter()
                pe.wait(*[x for x in prev_evac if x])
                with g.loop(n_tiles // 2) as lp:
                    w.run(2, lp, lambda j, slot, ready, used: work(j, slot, ready, used, lp))
            else:
                w.run(1, None, lambda j, slot, ready, used: work(j, slot, ready, used))

        prev_evac = [None, None]
        h_hi_cur = lambda k, n: h_hi[:, k, n * HT:(n + 1) * HT]
        h_lo_cur = lambda k, n: h_lo[:, k, n * HT:(n + 1) * HT]
        pe.wait(h_done)
        act.wait(h_done)

        class Lagged:

            def __init__(self, uses):
                self.uses = uses
                self.done, self.used, self.psu = [Point(), Point()], [Point(), Point()], Point()

            def keys(self, u, first_of_slot, last_of_slot):
                s = self.uses[u]
                d = {}
                if first_of_slot:
                    d["acc_done"], d["acc_used"] = (self.done[s], 1), (self.used[s], 1)
                if last_of_slot:
                    d["new_acc_done"], d["new_acc_used"] = self.done[s], self.used[s]
                if u == 0:
                    d["ps_used"] = (self.psu, 1)
                if u == len(self.uses) - 1:
                    d["new_ps_used"] = self.psu
                return d

        def ada_loop_block(lg, u, first, per, lp, second=False):
            s = lg.uses[u]
            keys = lg.keys(u, u == lg.uses.index(s), u == len(lg.uses) - 1 - lg.uses[::-1].index(s))
            b0 = SMALL["b_ada_2"][0] if second else SMALL["b_ada"][0]
            m = mod2 if second else mod1
            o = first + u - (24 if second else 0)
            ada_m.block(s, lambda: lp.i * per + (first + u), 8 if second else 0,
                        lambda: m[:, bass.ds(lp.i * (2 * per) + 2 * o, 2)],
                        lambda: small[:, bass.ds(lp.i * (2 * per) + (b0 + 2 * o), 2)], keys)

        def ada_enter():
            sp.wait(*[x for x in ada_m.acc_done if x])
            dve.wait(*[x for x in ada_m.acc_used if x])
            pe.wait(ada_m.ps_used)

        xp_at = BASE + fixed.at
        xp = fixed("xp", [P, T + 4], F32)
        pads = dve(lambda e: e.memset(xp[:, :], 0.0))
        cw = SMALL["conv_w"][0]
        conv = {"taps": None}

        def conv_tile(t, lagged=None):
            free = [(lagged, 1)] if lagged else [x for x in [conv["taps"]] if x]
            p = act(lambda e: e.activation(xp[:, 2:2 + T], y[:, t(), :], ACT.Copy), pads, *free)
            p = dve(lambda e: e.tensor_scalar(y[:, t(), :], xp[:, 0:T], small[:, bass.ds(t() * 5 + cw, 1)], None, ALU.mult), p)
            for j in range(1, 5):
                p = dve(lambda e, j=j: e.scalar_tensor_tensor(
                    y[:, t(), :], xp[:, j:j + T], small[:, bass.ds(t() * 5 + (cw + j), 1)], y[:, t(), :], ALU.mult, ALU.add),
                    p, point=lagged if j == 4 else None)
            conv["taps"] = p
            conv["done"] = act(lambda e: e.activation(y[:, t(), :], y[:, t(), :], ACT.Silu,
                                                      bias=small[:, bass.ds(t() + SMALL["conv_b"][0], 1)]), p)

        ada_enter()
        lg = Lagged([0, 1, 0])
        project(8, lambda m: y[:, m, :],
                extra=lambda j, lp: [ada_loop_block(lg, u, 8, 3, lp) for u in ((0, 1), (2,))[j]])
        act.wait(prev_evac[0], prev_evac[1])
        ada_enter()
        lg2, taps2 = Lagged([0, 1]), Point()
        project(4, lambda m: y[:, 8 + m, :],
                extra=lambda j, lp: (ada_loop_block(lg2, j, 20, 2, lp),
                                     conv_tile(lambda: lp.i, taps2) if j == 0 else None))
        ada_enter()
        lg3, taps3 = Lagged([0, 1, 0]), Point()
        act.wait(taps2)
        project(8, lambda m: y[:, 12 + m, :],
                extra=lambda j, lp: ([ada_loop_block(lg3, u, 24, 3, lp, True) for u in ((0, 1), (2,))[j]],
                                     conv_tile(lambda: lp.i + 2, taps3) if j == 0 else None))
        project(2, lambda m: y[:, 20 + m, :],
                extra=lambda j, lp: conv_tile(lambda: 6) if j == 0 else None)
        project(1, lambda m: y[:, 22, :], extra=lambda j, lp: conv_tile(lambda: 7))
        def pieces(q0, q1):
            return [(n, max(q0, n * HT), min(q1, (n + 1) * HT)) for n in range(2) if max(q0, n * HT) < min(q1, (n + 1) * HT)]

        def flat(b0):
            return ps[:, b0:b0 + 2, :].rearrange("p a b -> p (a b)")

        class Attention:

            def __init__(self, kind, area, area2, area3, rinv):
                self.kind = kind
                n = kind
                self.kk = [area(f"{n}_kk{s}", [P, T], F32R) for s in range(2)]
                self.ka = [area(f"{n}_ka{s}", [P, T], F32R) for s in range(2)]
                self.qq = [area(f"{n}_qq{s}", [P, T], F32R) for s in range(2)]
                self.qa = [area(f"{n}_qa{s}", [P, T], F32R) for s in range(2)]
                self.vh = [area(f"{n}_vh{s}", [P, KT, P], F32R) for s in range(2)]
                self.vl = [area(f"{n}_vl{s}", [P, KT, P], F32R) for s in range(2)]
                self.rinv = rinv
                self.pf = [area2(f"{n}_pf{s}", [P, T], F32) for s in range(2)]
                self.ph = [area(f"{n}_ph{s}", [P, T], F32R) for s in range(2)]
                self.pl = [area2(f"{n}_pl{s}", [P, T], F32R) for s in range(2)]
                self.mx = [area3(f"{n}_mx{s}", [P, KT], F32) for s in range(2)]
                self.end = {}
                p = None
                for s in range(2):
                    for t, value in ((self.ka[s][64:65, :], 1.0), (self.vh[s][:, :, 64:P], 1.0), (self.vl[s][:, :, 64:P], 0.0)):
                        p = pool(lambda e, t=t, value=value: e.memset(t.bitcast(F32), value), *([p] if p else []))
                self.ones_set = p

            def free(self, *names):
                return [self.end[n] for n in names if self.end.get(n)]

            def rows(self, a):
                return slice(64 * a, 64 * a + 64)

            def key_range(self, qt):
                return {"full": (0, T), "causal": (0, (qt + 1) * P), "band": (max(qt - 1, 0) * P, (qt + 1) * P)}[self.kind]

            def query_range(self, kt):
                return {"full": (0, T), "causal": (kt * P, T), "band": (kt * P, min(kt + 2, KT) * P)}[self.kind]

            def prep_k(self, b, a, src, *waits):
                r, o = self.rows(a), self.rows(1 - a)
                h = act(lambda e: e.activation(self.kk[b][r, :], src(), ACT.Copy), *waits, *self.free(f"kk{b}"))
                k2 = act(lambda e: e.activation(self.ka[b][0:64, :], src(), ACT.Copy))
                self.end[f"kk_made{b}"] = k2
                self.end[f"kk_low{b}"] = dve(lambda e: e.tensor_tensor(self.kk[b][o, :], src(), self.kk[b][r, :].bitcast(F32),
                                                                      ALU.subtract), h, *self.free(f"kk{b}"))

            def prep_q(self, b, a, src, *waits):
                r, o = self.rows(a), self.rows(1 - a)
                h = act(lambda e: e.activation(self.qq[b][r, :], src(), ACT.Copy), *waits, *self.free(f"qq{b}"))
                h2 = act(lambda e: e.activation(self.qq[b][o, :], src(), ACT.Copy))
                self.end[f"q_made{b}"] = h2
                self.end[f"q_low{b}"] = dve(lambda e: e.tensor_tensor(self.qa[b][0:64, :], src(), self.qq[b][r, :].bitcast(F32),
                                                                     ALU.subtract), h, *self.free(f"qq{b}"))

            def prep_v(self, s, a, src, *waits):
                r = self.rows(a)
                for k in range(KT):
                    t = pe(lambda e, k=k: e.transpose(ps[:, 4, k * 64:(k + 1) * 64], src()[:, k * P:(k + 1) * P],
                                                      ident[r, 64 * a:64 * a + 64]),
                           *((*waits, *self.free("bank4")) if k == 0 else ()), mark=(k == KT - 1))
                v = lambda: ps[:, 4, :].rearrange("p (k f) -> p k f", k=KT)
                h = act(lambda e: e.activation(self.vh[s][:, :, 0:64], v(), ACT.Copy), t, self.ones_set, *self.free(f"v{s}"))
                self.end["bank4"] = self.end[f"v_made{s}"] = dve(
                    lambda e: e.tensor_tensor(self.vl[s][:, :, 0:64], v(), self.vh[s][:, :, 0:64].bitcast(F32), ALU.subtract), h)

            def max_pass(self, b, kb, ka_row, qt, head):
                k0, k1 = self.key_range(qt)
                q = slice(qt * P, (qt + 1) * P)
                r = self.rows(ka_row)
                waits = [*self.free("bank4", "bank5", f"q_made{b}", f"kk_made{kb}")] if qt == 0 else [*self.free("bank4")]
                pcs = pieces(k0, k1)
                for i, (n, c0, c1) in enumerate(pcs):
                    more = []
                    if self.kind == "causal":
                        more.append((lambda e, n=n, c0=c0, c1=c1: e.matmul(
                            ps[:, 4 + n, c0 - n * HT:c1 - n * HT], self.sel(head), self.cum_split[:, c0:c1],
                            start=False, stop=False, skip_group_check=True)))
                    if self.kind != "full":
                        for t0, m in ((qt, low_keep), (qt - 1, band_keep if self.kind == "band" else None)):
                            if m is not None and c0 <= t0 * P < c1:
                                o = t0 * P - n * HT
                                more.append((lambda e, n=n, o=o, m=m: e.matmul(
                                    ps[:, 4 + n, o:o + P], ident_b[:, :], m[:, :], start=False, stop=False,
                                    skip_group_check=True)))
                    p = pe(lambda e, n=n, c0=c0, c1=c1, m=more: e.matmul(
                        ps[:, 4 + n, c0 - n * HT:c1 - n * HT], self.qq[b][r, q], self.kk[kb][r, c0:c1],
                        start=True, stop=not m, skip_group_check=True), *(waits if i == 0 else ()),
                        mark=(i == len(pcs) - 1 and not more))
                    for j, fn in enumerate(more):
                        p = pe(fn, mark=(i == len(pcs) - 1 and j == len(more) - 1))
                self.end["bank4"] = dve(lambda e: e.tensor_reduce(self.mx[b][:, qt:qt + 1], flat(4)[:, k0:k1], AX_X, ALU.max),
                                        p, *self.free(f"mx{b}"))

            def max_rows(self, b, head):
                p = self.end["bank4"]
                if self.kind == "band":
                    p = dve(lambda e: e.tensor_scalar(self.mx[b][:, :], self.mx[b][:, :], self.sink_raw(head), None, ALU.max), p)
                for qt in range(KT):
                    t = pe(lambda e, qt=qt: e.transpose(ps[0:1, 4 + qt // 4, (qt % 4) * P:(qt % 4 + 1) * P],
                                                      self.mx[b][:, qt:qt + 1], ident[:, :]),
                           *([p] if qt == 0 else []), mark=(qt == KT - 1))
                self.end[f"mx{b}"] = t
                m = act(lambda e: e.activation(self.qa[b][64:65, :], ps[0:1, 4:6, :].rearrange("p a b -> p (a b)"),
                                               ACT.Copy, scale=-1.0), t, *self.free(f"qq{b}"))
                self.end["bank4"] = self.end["bank5"] = self.end[f"row{b}"] = m
                if self.kind == "band":
                    m = act(lambda e: e.activation(self.sf[64:65, :], self.qa[b][64:65, :].bitcast(F32), ACT.Exp,
                                                   bias=self.sink(head), scale=SC), m, *self.free("sf"))
                    m = act(lambda e: e.activation(self.sh[64:65, :], self.sf[64:65, :], ACT.Copy), m, *self.free("sink"))
                    self.end["sf"] = self.end["sink_made"] = dve(lambda e: e.tensor_tensor(
                        self.sl[64:65, :], self.sf[64:65, :], self.sh[64:65, :].bitcast(F32), ALU.subtract), m)

            def scores(self, b, kb, kt, head):
                q0, q1 = self.query_range(kt)
                s, bank = kt % 2, 2 * (kt % 2)
                keys = slice(kt * P, (kt + 1) * P)
                waits = [*self.free(f"s_read{s}")]
                if kt == 0:
                    waits += self.free(f"row{b}", f"q_low{b}", f"kk_low{kb}")
                pcs = pieces(q0, q1)
                for i, (n, c0, c1) in enumerate(pcs):
                    o = ps[:, bank + n, c0 - n * HT:c1 - n * HT]
                    pe(lambda e, o=o, c0=c0, c1=c1: e.matmul(o, self.kk[kb][:, keys], self.qq[b][:, c0:c1], start=True,
                                                             stop=False, skip_group_check=True),
                       *(waits if i == 0 else ()), mark=False)
                    masks = []
                    if self.kind != "full":
                        for t0, m in ((kt, up_keep), (kt + 1, band_keep_t if self.kind == "band" else None)):
                            if m is not None and c0 <= t0 * P < c1:
                                masks.append((t0 * P - n * HT, m))
                    p = pe(lambda e, o=o, c0=c0, c1=c1, last=not masks: e.matmul(o, self.ka[kb][0:65, keys],
                                                                               self.qa[b][0:65, c0:c1], start=False,
                                                                               stop=last, skip_group_check=True),
                           mark=(i == len(pcs) - 1 and not masks))
                    for j, (c, m) in enumerate(masks):
                        p = pe(lambda e, n=n, c=c, m=m, last=(j == len(masks) - 1): e.matmul(
                            ps[:, bank + n, c:c + P], ident_b[:, :], m[:, :], start=False, stop=last, skip_group_check=True),
                            mark=(i == len(pcs) - 1 and j == len(masks) - 1))
                if kt == KT - 1:
                    self.end[f"qq{b}"] = p
                bias = {} if self.kind != "causal" else {"bias": self.cum_col(kt, head)}
                x = act(lambda e: e.activation(self.pf[s][:, q0:q1], flat(bank)[:, q0:q1], ACT.Exp, scale=SC, **bias),
                        p, *self.free(f"pf{s}"))
                self.end[f"s_read{s}"] = x
                h = act(lambda e: e.activation(self.ph[s][:, q0:q1], self.pf[s][:, q0:q1], ACT.Copy), x, *self.free(f"ph{s}"))
                self.end[f"pf{s}"] = self.end[f"p_made{s}"] = dve(
                    lambda e: e.tensor_tensor(self.pl[s][:, q0:q1], self.pf[s][:, q0:q1], self.ph[s][:, q0:q1].bitcast(F32),
                                              ALU.subtract), h)

            def values(self, vb, kt):
                q0, q1 = self.query_range(kt)
                s = kt % 2
                waits = [*self.free(f"p_made{s}")]
                if kt == 0:
                    waits += self.free("out_read", f"v_made{vb}")
                pcs = pieces(q0, q1)
                if kt == 0 and self.kind == "band":
                    for n in range(2):
                        for i, row in enumerate((self.sh, self.sl)):
                            p = pe(lambda e, n=n, row=row, i=i: e.matmul(ps[:, 6 + n, :], self.one_row[64:65, :],
                                                                     row[64:65, n * HT:(n + 1) * HT], start=(i == 0),
                                                                     stop=False, skip_group_check=True),
                                   *((waits + self.free("sink_made")) if (n, i) == (0, 0) else ()), mark=(n == 1 and i == 1))
                    self.end["sink"] = p
                for i, (n, c0, c1) in enumerate(pcs):
                    first = kt == 0 and self.kind != "band"
                    last = kt == KT - 1 or (self.kind != "full" and n == 0 and kt == 3)
                    for j, (v, x) in enumerate(((self.vh, self.ph), (self.vl, self.ph), (self.vh, self.pl))):
                        p = pe(lambda e, n=n, c0=c0, c1=c1, v=v, x=x, j=j, first=first, last=last: e.matmul(
                            ps[:, 6 + n, c0 - n * HT:c1 - n * HT], v[vb][:, kt, :], x[s][:, c0:c1],
                            start=(first and j == 0), stop=(last and j == 2), skip_group_check=True),
                            *(waits if (i, j) == (0, 0) else ()), mark=(i == len(pcs) - 1 and j == 2))
                self.end[f"ph{s}"] = p
                self.end[f"v{vb}"] = self.end["out"] = p

            def write(self, a, dst):
                l = act(lambda e: e.activation(self.rinv[:, :], flat(6)[64:P, :], ACT.Ln), self.end["out"], *self.free("rinv"))
                r = act(lambda e: e.activation(self.rinv[:, :], self.rinv[:, :], ACT.Exp, scale=-1.0), l)
                self.end["rinv"] = self.end["out_read"] = dve(
                    lambda e: e.tensor_tensor(dst(), flat(6)[0:64, :], self.rinv[:, :], ALU.mult), r)

            def maxima(self, b, kb, ka_row, head):
                for qt in range(KT):
                    self.max_pass(b, kb, ka_row, qt, head)
                self.max_rows(b, head)

            def head(self, b, kb, vb, head, a, dst, nxt=None):
                self.scores(b, kb, 0, head)
                for kt in range(KT):
                    if kt + 1 < KT:
                        self.scores(b, kb, kt + 1, head)
                    else:
                        self.end[f"kk{kb}"] = self.end[f"qq{b}"]
                    if nxt:
                        nxt(kt)
                    self.values(vb, kt)
                self.write(a, dst)

        g.meet()
        prep = Area(0, 64)
        cos1 = prep("cos1", [P, T], F32)
        sin1 = prep("sin1", [P, T], F32)
        qsq = prep("qsq", [P, T], F32)
        qr = prep("qr", [P, T], F32)
        qu = prep("qu", [P, T], F32)
        qw = prep("qw", [P, T], F32)
        c_rope = g.count("c_rope")
        sp(lambda e: e.dma_start(cos1[:, :], a["rope"][0]), sem=c_rope, by=16)
        rope_in = sp(lambda e: e.dma_start(sin1[:, :], a["rope"][1]), sem=c_rope, by=16)
        swap16 = [(i + 16) % 32 for i in range(32)]
        gq = SMALL["qk_g"][0]
        free = {}

        def norm_rotate(t):
            src = lambda: y[:, QA + t, :]
            had = lambda n: [free[n]] if n in free else []
            p = act(lambda e: e.activation(qsq[:, :], src(), ACT.Square), *had("sq"))
            for n in range(2):
                p = pe(lambda e, n=n: e.matmul(ps[:, 4 + n, :], pair_ones[:, :], qsq[:, n * HT:(n + 1) * HT], start=True, stop=True),
                       *([p, *had("ps")] if n == 0 else []), mark=(n == 1))
            free["sq"] = p
            p = act(lambda e: e.activation(qr[:, :], flat(4), ACT.Ln, bias=col("eps"), scale=1.0 / 64), p, *had("r"))
            free["ps"] = p
            p = act(lambda e: e.activation(qr[:, :], qr[:, :], ACT.Exp, scale=-0.5), p)
            u = dve(lambda e: e.scalar_tensor_tensor(qu[:, :], src(), small[:, gq + t:gq + t + 1], qr[:, :], ALU.mult, ALU.mult), p, *had("u"))
            free["r"] = u
            v = dve(lambda e: e.stream_shuffle(qw[:, :], qu[:, :], swap16), u)
            v = dve(lambda e: e.tensor_tensor(qw[:, :], qw[:, :], sin1[:, :], ALU.mult), v, rope_in)
            v = dve(lambda e: e.tensor_tensor(qu[:, :], qu[:, :], cos1[:, :], ALU.mult), v)
            free["u"] = dve(lambda e: e.tensor_tensor(src(), qu[:, :], qw[:, :], ALU.add), v)
            return free["u"]

        for t in range(5):
            rotated = norm_rotate(t)

        g.meet(act, dve, pool, pe)
        low_area, high_area = Area(0, 64), Area(156, 174)
        full = Attention("full", low_area, high_area, high_area, low_area("rinv1", [64, T], F32))

        def qrow(h):
            return lambda: y[64 * (h % 2):64 * (h % 2) + 64, QA + h // 2, :]

        for kv in range(2):
            full.prep_v(kv, kv, lambda kv=kv: y[64 * kv:64 * kv + 64, VA, :])
            full.prep_k(kv, kv, lambda kv=kv: y[64 * kv:64 * kv + 64, KA, :], rotated)
        full.prep_q(0, 0, qrow(0))
        full.maxima(0, 0, 0, 0)
        for h in range(8):
            kv, nkv = h // 4, (h + 1) // 4
            if h < 7:
                full.prep_q((h + 1) % 2, (h + 1) % 2, qrow(h + 1))

                def nxt(kt, h=h, nkv=nkv):
                    full.max_pass((h + 1) % 2, nkv, nkv, kt, h + 1)
                    if kt == KT - 1:
                        full.max_rows((h + 1) % 2, h + 1)
            else:
                nxt = None
            full.head(h % 2, kv, kv, h, h % 2, qrow(h), nxt)
        g.meet()
        low, high = Area(0, 64), Area(156, 174)
        e_buf = [low(f"m_e{s}", [P, T], F32) for s in range(2)]
        wh = [low(f"m_wh{s}", [P, T], F32R) for s in range(2)]
        wl = [low(f"m_wl{s}", [P, T], F32R) for s in range(2)]
        qh = [low(f"m_qh{s}", [P, T], F32R) for s in range(2)]
        kh = [low(f"m_kh{s}", [P, T], F32R) for s in range(2)]
        vh = [low(f"m_vh{s}", [P, KT, P], F32R) for s in range(2)]
        m_stack = low("m_stack", [P, T], F32R)
        nm_stack = low("nm_stack", [P, T], F32R)
        sel = low("sel", [P, 8, P], F32R)
        nb = low("m_nb", [P, T], F32)
        mb = [high(f"m_mb{s}", [P, T], F32) for s in range(2)]
        hs = high("m_hs", [P, T], F32)
        a_cols = high("a_cols", [P, KT, 64], F32)
        ones_r = high("ones_r", [P, P], F32R)
        den = high("m_den", [P, HT], F32)
        yr = Area(64, 156)("y_r", [P, N_IN1, T], F32R)
        gt = Area(0, 64)
        f_pre, f_log, b_cum, a_gate, m_max, i_pre, zeros, n_max, sel_raw = (
            gt(f"g_{n}", [64, T] if n != "sel_raw" else [P, T], F32)
            for n in ("f_pre", "f_log", "b_cum", "a_gate", "m_max", "i_pre", "zeros", "n_max", "sel_raw"))

        c_sel = g.count("c_sel")
        sel_in = sp(lambda e: e.dma_start(sel_raw[:, :], a["sel"].rearrange("p k c -> p (k c)")), sem=c_sel, by=16)
        gb = col("gate_b")
        p = act(lambda e: e.activation(f_pre[:, :], y[64:P, GA, :], ACT.Identity, bias=gb[64:P, :]))
        q = act(lambda e: e.activation(i_pre[:, :], y[0:64, GA, :], ACT.Identity, bias=gb[0:64, :]))
        z = dve(lambda e: e.memset(zeros[:, :], 0.0))
        p1 = act(lambda e: e.activation(f_log[:, :], f_pre[:, :], ACT.Abs), p)
        p1 = act(lambda e: e.activation(f_log[:, :], f_log[:, :], ACT.Exp, scale=-1.0), p1)
        p1 = act(lambda e: e.activation(f_log[:, :], f_log[:, :], ACT.Ln, bias=col("one")[0:64, :]), p1)
        p = dve(lambda e: e.scalar_tensor_tensor(f_log[:, :], f_pre[:, :], 0.0, f_log[:, :], ALU.min, ALU.subtract), p1, z)
        both = ((slice(0, 32), slice(None, None, 1)), (slice(32, 64), slice(None, None, -1)))

        def scan(out, d0, d1, op0, op1, *waits):
            for r, o in both:
                x = dve(lambda e, r=r, o=o: e.tensor_tensor_scan(out[r, o], d0[r, o], d1[r, o], 0.0, op0, op1), *waits)
            return x

        p = scan(b_cum, f_log, zeros, ALU.add, ALU.add, p)
        p = dve(lambda e: e.tensor_tensor(a_gate[:, :], i_pre[:, :], b_cum[:, :], ALU.subtract), p, q)
        a_done = p
        p = scan(m_max, a_gate, a_gate, ALU.max, ALU.max, p)
        m_done = p
        p = dve(lambda e: e.scalar_tensor_tensor(n_max[:, :], b_cum[:, :], -1.0, m_max[:, :], ALU.mult, ALU.subtract), p)
        stacked = []
        for src, dst, ready in ((m_max, m_stack, m_done), (n_max, nm_stack, p)):
            x = act(lambda e, src=src, dst=dst: e.activation(dst[0:64, :], src[:, :], ACT.Copy), ready)
            stacked.append(dve(lambda e, src=src, dst=dst: e.tensor_tensor(dst[64:P, :], src[:, :], dst[0:64, :].bitcast(F32),
                                                                         ALU.subtract), x))
        for kt in range(KT):
            p = pe(lambda e, kt=kt: e.transpose(ps[:, 4, kt * 64:(kt + 1) * 64], a_gate[:, kt * P:(kt + 1) * P],
                                              ident[0:64, 0:64]), *([a_done] if kt == 0 else []), mark=(kt == KT - 1))
        p = act(lambda e: e.activation(a_cols[:, :, :].rearrange("p a b -> p (a b)"), ps[:, 4, :], ACT.Copy), p)
        p = act(lambda e: e.activation(sel[:, :, :].rearrange("p a b -> p (a b)"), sel_raw[:, :], ACT.Copy), sel_in)
        p = act(lambda e: e.activation(ones_r[:, :], ones[:, :], ACT.Copy))
        p = act(lambda e: e.activation(y[:, OM:OM + 4, :], y[:, OM:OM + 4, :], ACT.Sigmoid))
        g.meet()

        ring = {"n": 0, "read": [None, None]}
        m_end = {}

        def m_free(*names):
            return [m_end[n] for n in names if m_end.get(n)]

        def next_banks():
            s = ring["n"] % 2
            ring["n"] += 1
            return s, 2 * s, [x for x in [ring["read"][s]] if x]

        def m_prep(h):
            b = h % 2
            for src, hi in ((QM + h, qh), (QM + 4 + h, kh)):
                x = act(lambda e, src=src, hi=hi: e.activation(hi[b][:, :], y[:, src, :], ACT.Copy), *m_free(f"heads{b}"))
                m_end[f"prep{b}"] = dve(lambda e, src=src, hi=hi: e.tensor_tensor(yr[:, src, :], y[:, src, :],
                                                                                hi[b][:, :].bitcast(F32), ALU.subtract), x)
            s, bank, waits = next_banks()
            for k in range(KT):
                t = pe(lambda e, k=k: e.transpose(ps[:, bank + k // 4, (k % 4) * P:(k % 4 + 1) * P],
                                                y[:, VM + h, k * P:(k + 1) * P], ident[:, :]), *(waits if k == 0 else []), mark=(k == 7))
            x = act(lambda e: e.activation(vh[b][:, :, :].rearrange("p a b -> p (a b)"), flat(bank), ACT.Copy), t, *m_free(f"heads{b}"))
            x = dve(lambda e: e.tensor_tensor(yr[:, VM + h, :], flat(bank), vh[b][:, :, :].rearrange("p a b -> p (a b)").bitcast(F32),
                                              ALU.subtract), x)
            m_end[f"v_prep{b}"] = ring["read"][s] = x

        def m_rows(h, d, which):
            k, u = d * 4 + h, (2 * h + d) % 2
            for stack, dst, name in (((m_stack, mb[u], f"mb{u}"), (nm_stack, nb, "nb"))[which],):
                s, bank, waits = next_banks()
                for n in range(2):
                    t = pe(lambda e, n=n, bank=bank, stack=stack: e.matmul(ps[:, bank + n, :], sel[:, k, :],
                                                                          stack[:, n * HT:(n + 1) * HT], start=True, stop=True),
                           *(waits if n == 0 else []), mark=(n == 1))
                x = act(lambda e, bank=bank, dst=dst: e.activation(dst[:, :], flat(bank), ACT.Copy), t, *m_free(name))
                ring["read"][s] = m_end[name + "_made"] = x

        def m_weights(h, d, kt, i):
            b, s2, u = h % 2, i % 2, (2 * h + d) % 2
            q0, q1 = (kt * P, T) if d == 0 else (0, (kt + 1) * P)
            s, bank, waits = next_banks()
            keys = slice(kt * P, (kt + 1) * P)
            waits = waits + m_free(f"prep{b}")
            pcs = pieces(q0, q1)
            for j, (n, c0, c1) in enumerate(pcs):
                for m, (x, z) in enumerate(((kh[b][:, keys], lambda c0, c1: qh[b][:, c0:c1]),
                                            (yr[:, QM + 4 + h, keys], lambda c0, c1: qh[b][:, c0:c1]),
                                            (kh[b][:, keys], lambda c0, c1: yr[:, QM + h, c0:c1]))):
                    p = pe(lambda e, n=n, c0=c0, c1=c1, x=x, z=z, m=m: e.matmul(
                        ps[:, bank + n, c0 - n * HT:c1 - n * HT], x, z(c0, c1), start=(m == 0), stop=(m == 2),
                        skip_group_check=True), *(waits if (j, m) == (0, 0) else ()), mark=(j == len(pcs) - 1 and m == 2))
            sign = 1 if d == 0 else -1
            masked = pool(lambda e: e.affine_select(out=e_buf[s2][:, keys], in_=mb[u][:, keys], pattern=[[sign, P]],
                                                    compare_op=ALU.is_ge, fill=-NEG, base=0, channel_multiplier=-sign),
                          *m_free(f"mb{u}_made", f"e{s2}"))
            r0, r1 = (q0 + P, q1) if d == 0 else (q0, q1 - P)
            bias = a_cols[:, kt, 32 * d + h:32 * d + h + 1]
            if r1 > r0:
                act(lambda e: e.activation(e_buf[s2][:, r0:r1], mb[u][:, r0:r1], ACT.Exp, scale=-1.0, bias=bias),
                    *m_free(f"mb{u}_made", f"e{s2}"))
            x = act(lambda e: e.activation(e_buf[s2][:, keys], e_buf[s2][:, keys], ACT.Exp, scale=-1.0, bias=bias), masked)
            m_end[f"mb{u}"] = x
            x = dve(lambda e: e.scalar_tensor_tensor(e_buf[s2][:, q0:q1], flat(bank)[:, q0:q1], KSC, e_buf[s2][:, q0:q1],
                                                     ALU.mult, ALU.mult), x, p)
            ring["read"][s] = x
            x = act(lambda e: e.activation(wh[s2][:, q0:q1], e_buf[s2][:, q0:q1], ACT.Copy), x, *m_free(f"w{s2}"))
            m_end[f"e{s2}"] = m_end[f"w_made{s2}"] = dve(lambda e: e.tensor_tensor(
                wl[s2][:, q0:q1], e_buf[s2][:, q0:q1], wh[s2][:, q0:q1].bitcast(F32), ALU.subtract), x)

        def m_sums(h, d, kt, i):
            b, s2 = h % 2, i % 2
            q0, q1 = (kt * P, T) if d == 0 else (0, (kt + 1) * P)
            first = kt == (0 if d == 0 else KT - 1)
            pcs = pieces(q0, q1)
            if d == 0:
                pcs = pcs[::-1]
            waits = m_free(f"w_made{s2}", f"v_prep{b}")
            for n, c0, c1 in pcs:
                last = (kt == (3 if n == 0 else 7)) if d == 0 else (kt == (4 if n == 1 else 0))
                o = slice(c0 - n * HT, c1 - n * HT)
                wt = waits + (m_free(f"out_read{n}") if first else [])
                keys = slice(kt * P, (kt + 1) * P)
                for j, (base, v, x) in enumerate(((6, vh[b][:, kt, :], wh), (6, yr[:, VM + h, keys], wh), (6, vh[b][:, kt, :], wl),
                                                  (4, ones_r[:, :], wh), (4, ones_r[:, :], wl))):
                    p = pe(lambda e, j=j, base=base, v=v, x=x, n=n, o=o, c0=c0, c1=c1, last=last: e.matmul(
                        ps[:, base + n, o], v, x[s2][:, c0:c1], start=(first and j in (0, 3)), stop=(last and j in (2, 4)),
                        skip_group_check=True), *(wt if j == 0 else ()), mark=(j == 4))
                waits = []
                if last:
                    m_finish(h, d, n, p)
            m_end[f"w{s2}"] = p
            if kt == (7 if d == 0 else 0) and d == 1:
                m_end[f"heads{b}"] = p

        def m_finish(h, d, n, done):
            ts = slice(n * HT, (n + 1) * HT)
            x = act(lambda e: e.activation(den[:, :], ps[:, 4 + n, :], ACT.Abs), done, *m_free("den"))
            x = act(lambda e: e.activation(den[:, :], den[:, :], ACT.Ln, bias=col("tiny")), x)
            x = dve(lambda e: e.tensor_tensor(den[:, :], den[:, :], nb[:, ts], ALU.max), x, *m_free("nb_made"))
            m_end["nb"] = x
            x = act(lambda e: e.activation(den[:, :], den[:, :], ACT.Exp, scale=-1.0), x)
            if d == 0:
                x = dve(lambda e: e.tensor_tensor(hs[:, ts], ps[:, 6 + n, :], den[:, :], ALU.mult), x, *m_free("hs"))
            else:
                x = dve(lambda e: e.tensor_tensor(den[:, :], ps[:, 6 + n, :], den[:, :], ALU.mult), x)
            m_end["den"] = m_end[f"out_read{n}"] = x
            if d == 1:
                x = dve(lambda e: e.tensor_tensor(hs[:, ts], hs[:, ts], den[:, :], ALU.add), x)
                m_end["den"] = m_end[f"sum{n}"] = x

        def m_output(h):
            s2 = 0
            x = act(lambda e: e.activation(y[:, QM + h, :], hs[:, :], ACT.Square), *m_free("sum0", "sum1", f"heads{h % 2}"))
            s, bank, waits = next_banks()
            for n in range(2):
                t = pe(lambda e, n=n: e.matmul(ps[:, bank + n, :], ones[:, :], y[:, QM + h, n * HT:(n + 1) * HT], start=True, stop=True),
                       *((waits + [x]) if n == 0 else []), mark=(n == 1))
            x = act(lambda e: e.activation(y[:, QM + h, :], flat(bank), ACT.Ln, bias=col("eps"), scale=1.0 / P), t)
            ring["read"][s] = x
            x = act(lambda e: e.activation(y[:, QM + h, :], y[:, QM + h, :], ACT.Exp, scale=-0.5), x)
            x = dve(lambda e: e.scalar_tensor_tensor(y[:, QM + h, :], y[:, QM + h, :], col("mlstm_norm_g", h), hs[:, :],
                                                     ALU.mult, ALU.mult), x)
            m_end["hs"] = x
            dve(lambda e: e.tensor_tensor(y[:, QM + h, :], y[:, QM + h, :], y[:, OM + h, :], ALU.mult), x)

        steps = [(h, d, kt) for h in range(4) for d in range(2) for kt in (range(KT) if d == 0 else range(KT)[::-1])]
        m_prep(0)
        m_rows(0, 0, 0)
        m_rows(0, 0, 1)
        m_weights(*steps[0], 0)
        for i, (h, d, kt) in enumerate(steps):
            if i + 1 < len(steps):
                h2, d2, kt2 = steps[i + 1]
                if d2 != d:
                    m_rows(h2, d2, 0)
                m_weights(h2, d2, kt2, i + 1)
            if d == 1 and kt == 5 and h < 3:
                m_prep(h + 1)
            m_sums(h, d, kt, i)
            if i + 1 < len(steps) and steps[i + 1][1] != d:
                m_rows(steps[i + 1][0], steps[i + 1][1], 1)
            if d == 0 and kt == 1 and h:
                m_output(h - 1)
        m_output(3)
        g.meet()
        x1_dram = nc.dram_tensor("x1_scratch", (2, KT, P, HT), F32, kind="Internal").ap()
        xb_dram = nc.dram_tensor("xb_scratch", (2, P, KT, HT), F32, kind="Internal").ap()
        x1 = Area(120, 152)("x1", [P, 2, KT, HT], F32)
        mix = Area(0, 64)
        mix_hi = mix("mix_hi", [P, KT, T], F32R)
        mix_lo = mix("mix_lo", [P, KT, T], F32R)
        again = Area(156, 174)
        x_again = [again(f"x_again{s}", [P, T], F32) for s in range(2)]
        sq1 = [again(f"sq1_{s}", [P, HT], F32) for s in range(2)]
        acc1 = [nc.alloc_sbuf_tensor_at(f"acc1_{s}", [P, HT], F32, offset=xp_at + s * 2048) for s in range(2)]
        rs = [nc.alloc_sbuf_tensor_at(f"rs_{s}", [P, HT], F32, offset=BASE + 152 * K1 + s * 2048) for s in range(2)]

        mix_made = {}
        for k in range(KT):
            src = (QA + k) if k < 4 else (QM + k - 4)
            x = act(lambda e, k=k, src=src: e.activation(mix_hi[:, k, :], y[:, src, :], ACT.Copy))
            mix_made[k] = dve(lambda e, k=k, src=src: e.tensor_tensor(mix_lo[:, k, :], y[:, src, :], mix_hi[:, k, :].bitcast(F32),
                                                                      ALU.subtract), x)
        zero = dve(lambda e: e.memset(acc1[0][:, :], 0.0))
        acc_at = [zero, dve(lambda e: e.memset(acc1[1][:, :], 0.0))]
        x_landed = [g.count(f"x_again_landed{s}") for s in range(2)]
        x_used, banks_read, sq_read = [None, None], [None, None], [None, None]
        for pair in range(4):
            def w_out_tile(j, slot, ready, used, pair=pair):
                m, s, bank = 2 * pair + j, j, 2 * j
                lx = sp(lambda e: e.dma_start(x_again[s][:, :], a["x"][m]), *([x_used[s]] if x_used[s] else []),
                        sem=x_landed[s], by=16)
                mov = [(lambda k, n=n: mix_hi[:, k, n * HT:(n + 1) * HT], lambda k, n=n: mix_lo[:, k, n * HT:(n + 1) * HT])
                       for n in range(2)]
                product(g, w, slot, [ps[:, bank + n, :] for n in range(2)], mov, 0, KT, True, True,
                        [ready] + ([banks_read[s]] if banks_read[s] else []), used, mix_made if m == 0 else None)
                for n in range(2):
                    x = dve(lambda e, n=n: e.scalar_tensor_tensor(x1[:, n, m, :], ps[:, bank + n, :], mod1[:, 16 + m:17 + m],
                                                                 x_again[s][:, n * HT:(n + 1) * HT], ALU.mult, ALU.add), used, lx)
                    q = act(lambda e, n=n: e.activation(sq1[n][:, :], x1[:, n, m, :], ACT.Square), x,
                            *([sq_read[n]] if sq_read[n] else []))
                    acc_at[n] = sq_read[n] = dve(lambda e, n=n: e.tensor_tensor(acc1[n][:, :], acc1[n][:, :], sq1[n][:, :], ALU.add),
                                                 q, acc_at[n])
                x_used[s] = banks_read[s] = x
            w.run(2, None, w_out_tile)
        c_x1 = g.count("c_x1_kept")
        for n in range(2):
            x1_kept = sp(lambda e, n=n: e.dma_start(x1_dram[n].rearrange("k p t -> p k t"), x1[:, n, :, :]), x_used[1], sem=c_x1, by=16)

        norm_hl = [Area(32 * n, 32 * n + 32) for n in range(2)]
        h2_hi = [norm_hl[n](f"h2_hi{n}", [P, KT, HT], F32R) for n in range(2)]
        h2_lo = [norm_hl[n](f"h2_lo{n}", [P, KT, HT], F32R) for n in range(2)]
        hid = Area(64, 152)
        hid_hi = hid("hid_hi", [P, FT, HT], F32R)
        hid_lo = hid("hid_lo", [P, FT, HT], F32R)
        x2 = Area(152, 168)("x2", [P, KT, HT], F32)
        tail = Area(168, 174)
        gated = tail("gated", [P, HT], F32)
        x1c = [tail(f"x1c{s}", [P, HT], F32) for s in range(2)]
        sf_done = scale_col(s_ffn, "norm_ffn_g", 32, mod1)

        def normed(src, bank, acc, r, acc_ready, scale, shift, hi, lo, tt, made):
            state = {"free": [None, None]}

            def start():
                state["r"] = inverse_norm(acc, bank, r, acc_ready())

            def tile(k):
                s = k % 2
                f = state["free"]
                t1 = dve(lambda e: e.tensor_tensor(tt[s][:, :], src(k), r[:, :], ALU.mult), state["r"], *([f[s]] if f[s] else []))
                t2 = act(lambda e: e.activation(tt[s][:, :], tt[s][:, :], ACT.Identity, bias=shift(k), scale=scale(k)), t1)
                t3 = act(lambda e: e.activation(hi(k), tt[s][:, :], ACT.Copy), t2)
                f[s] = made[k] = dve(lambda e: e.tensor_tensor(lo(k), tt[s][:, :], hi(k).bitcast(F32), ALU.subtract), t3)

            return [start] + [lambda k=k: tile(k) for k in range(KT)]

        h2_made = [{}, {}]
        both_acc = list(acc_at)

        def ffn_norm(n):
            tt2 = [x1c[0], x1c[1]]
            return normed(lambda k: x1[:, n, k, :], 6, acc1[n], rs[n], lambda: both_acc[n], lambda k: s_ffn[:, k:k + 1],
                          lambda k: mod1[:, 24 + k:25 + k], lambda k: h2_hi[n][:, k, :], lambda k: h2_lo[n][:, k, :], tt2, h2_made[n])

        g.meet(act, dve)
        for step in ffn_norm(0):
            step()
        gated_read = {"p": None}
        bank_pts = {}

        def gate_up(n, turns, extras, loop):
            def tile(j, slot, ready, used, lp, turn):
                bank = j
                first = turn == 0 and j == 0
                mov = [(lambda k: h2_hi[n][:, k, :], lambda k: h2_lo[n][:, k, :])]
                waits = [ready]
                if lp is not None:
                    waits.append((evac[j // 2], 1))
                elif bank_pts.get(j // 2):
                    waits.append(bank_pts[j // 2])
                product(g, w, slot, [ps[:, bank, :]], mov, 0, KT, True, True, waits, used,
                        h2_made[n] if first else None)
                for _ in range(2):
                    if lp is None and extras:
                        extras.pop(0)()
                if j % 2 == 0:
                    silu_waits[0] = used
                    return
                m = (lambda: lp.i * 2 + (2 * turn0 + j // 2)) if lp is not None else (lambda: 2 * turn + j // 2)
                half = j // 2
                x = act(lambda e: e.activation(gated[:, :], ps[:, bank - 1, :], ACT.Silu), silu_waits[0],
                        *([gated_read["p"]] if gated_read["p"] else []))
                x = dve(lambda e: e.tensor_tensor(gated[:, :], gated[:, :], ps[:, bank, :], ALU.mult), x, used,
                        point=evac[half] if lp is not None else None)
                bank_pts[half] = x
                x = act(lambda e: e.activation(hid_hi[:, m(), :], gated[:, :], ACT.Copy), x)
                gated_read["p"] = dve(lambda e: e.tensor_tensor(hid_lo[:, m(), :], gated[:, :], hid_hi[:, m(), :].bitcast(F32),
                                                                ALU.subtract), x, point=made if (lp is not None and half == 1) else None)

            evac, made = [Point(), Point()], Point()
            silu_waits = [None]
            for turn in range(turns):
                w.run(4, None, lambda j, slot, ready, used, turn=turn: tile(j, slot, ready, used, None, turn))
            while extras:
                extras.pop(0)()
            turn0 = turns
            w.enter()
            act.wait(x1_kept)
            dve.wait(x1_kept)
            pe.wait(bank_pts[1])
            act.wait(gated_read["p"])
            gated_read["p"] = None
            with g.loop(FT // 2 - turns) as lp:
                gated_read["p"] = (made, 1)
                w.run(4, lp, lambda j, slot, ready, used: tile(j, slot, ready, used, lp, turns))
            gated_read["p"] = made
            before = Point()
            before.count, before.loops = made.count, []
            before.first = made.first + (lp.n - 2) * lp.step[made.count]
            gated_read["before"] = before

        def down(n, then):
            lhs = {"evac": [None, None], "x1": [Point(), Point()], "sq": None}
            landed = [c_x1c[0], c_x1c[1]]
            acc_z = dve(lambda e: e.memset(acc1[n][:, :], 0.0), h2_made[n][KT - 1], *([h3_made[0][KT - 1]] if n else []))
            start_waits = gated_read["p"]

            def tile(j, slot, ready, used, lp, turn):
                s, part = j // 3, j % 3
                nk = 8 if part < 2 else FT - 16
                waits = [ready]
                if part == 0:
                    if lp is not None:
                        waits.append((evac[s], 1))
                    elif lhs["evac"][s]:
                        waits.append(lhs["evac"][s])
                if part == 2 and s == 0:
                    waits.append(start_waits)
                mov = [(lambda k: hid_hi[:, k, :], lambda k: hid_lo[:, k, :])]
                product(g, w, slot, [ps[:, 4 + s, :]], mov, 8 * part, nk, part == 0, part == 2, waits, used)
                if part != 1 and part != 2:
                    x_wait = [(evac[s], 1)] if lp is not None else [x for x in [lhs["evac"][s]] if x]
                    m_ = m_of(lp, s)
                    lhs["lx"] = sp(lambda e: e.dma_start(x1c[s][:, :], x1_dram[n, m_()]), *x_wait, sem=landed[s], by=16)
                if part == 2:
                    m_ = m_of(lp, s)
                    lx = lhs["lx"]
                    x = dve(lambda e: e.scalar_tensor_tensor(x2[:, m_(), :], ps[:, 4 + s, :], mod1[:, bass.ds(m_() + 40, 1)],
                                                             x1c[s][:, :], ALU.mult, ALU.add), used, lx,
                            point=evac[s] if lp is not None else None)
                    lhs["evac"][s] = x
                    q = act(lambda e: e.activation(gated[:, :], x2[:, m_(), :], ACT.Square), x,
                            *([(sq_done, 1) if (s == 0) else lhs["sq"]] if lp is not None else [y_ for y_ in [lhs["sq"]] if y_]))
                    lhs["sq"] = dve(lambda e: e.tensor_tensor(acc1[n][:, :], acc1[n][:, :], gated[:, :], ALU.add), q, *dq,
                                    point=sq_done if (lp is not None and s == 1) else None)

            evac, sq_done = [Point(), Point()], Point()
            dq = [acc_z]
            m_of = lambda lp, s: (lambda: lp.i * 2 + s) if lp is not None else (lambda: 6 + s)
            w.enter()
            sp.wait(x1_kept, g.last(act), acc_z)
            act.wait(acc_z)
            pe.wait(gated_read["before"])
            with g.loop(3) as lp:
                w.run(6, lp, lambda j, slot, ready, used: tile(j, slot, ready, used, lp, 0))
            lhs["evac"] = [evac[0], evac[1]]
            lhs["sq"] = sq_done
            w.run(6, None, lambda j, slot, ready, used: tile(j, slot, ready, used, None, 3), then=then)
            return lhs["sq"]

        h3_made = [{}, {}]
        c_x1c = [g.count(f"x1c_landed{s}") for s in range(2)]
        c_xb = g.count("c_xb")
        spp_done = scale_col(s_pre, "g_pre_2", 8, mod2)
        kept = {}

        def between(n, x2_done):
            st, rs2 = {}, acc1[1 - n]
            fg = SMALL["final_norm_g"][0]

            def a0():
                st["r"] = inverse_norm(acc1[n], 6, rs2, x2_done)
                st["z"] = dve(lambda e: e.memset(acc1[n][:, :], 0.0), st["r"])
                st["sq"] = [None, None]

            def a1(k):
                s = k % 2
                x = dve(lambda e: e.scalar_tensor_tensor(x2[:, k, :], x2[:, k, :], small[:, fg + k:fg + k + 1], rs2[:, :],
                                                         ALU.mult, ALU.mult), st["r"])
                q = act(lambda e: e.activation(x1c[s][:, :], x2[:, k, :], ACT.Square), x, *([st["sq"][s]] if st["sq"][s] else []))
                st["sq"][s] = st["acc"] = dve(lambda e: e.tensor_tensor(acc1[n][:, :], acc1[n][:, :], x1c[s][:, :], ALU.add), q, st["z"],
                                              *([st["acc"]] if "acc" in st else []))
                if k == KT - 1:
                    kept[n] = sp(lambda e: e.dma_start(xb_dram[n], x2[:, :, :]), x, sem=c_xb, by=16)

            def lazy():
                return st["acc"]

            return ([a0] + [lambda k=k: a1(k) for k in range(KT)] +
                    normed(lambda k: x2[:, k, :], 6, acc1[n], rs2, lazy, lambda k: s_pre[:, k:k + 1],
                           lambda k: mod2[:, k:k + 1], lambda k: h2_hi[n][:, k, :], lambda k: h2_lo[n][:, k, :], x1c, h3_made[n]))

        gate_up(0, 3, ffn_norm(1), True)
        x2_done = down(0, 31)
        gate_up(1, 5, between(0, x2_done), True)
        dve.wait(kept[0])
        x2_done = down(1, None)
        for step in between(1, x2_done):
            step()
        g.meet()
        y2 = Area(64, 172)("y2", [P, N_IN2, T], F32)
        h_hi_cur = lambda k, n: h2_hi[n][:, k, :]
        h_lo_cur = lambda k, n: h2_lo[n][:, k, :]
        z_dram = nc.dram_tensor("z_scratch", (P, 4, T), F32, kind="Internal").ap()
        act.wait(*kept.values())
        project(12, lambda m: y2[:, m, :])
        act.wait(*prev_evac)
        project(4, lambda m: y2[:, FZ + m, :], func=ACT.Silu)
        act.wait(*prev_evac)
        project(6, lambda m: y2[:, SQ + m, :])
        act.wait(*prev_evac)
        project(4, lambda m: y2[:, SZ + m, :], func=ACT.Silu)
        c_z, c_pos, c_swap, c_back = (g.count(n) for n in ("c_z", "c_pos", "c_swap", "c_back"))
        z_kept = sp(lambda e: e.dma_start(z_dram, y2[:, SZ:SZ + 4, :]), prev_evac[1], sem=c_z, by=16)
        project(1, lambda m: y2[:, FG, :])
        g.meet()

        lo2, hi2, ti2 = Area(0, 64), Area(152, 168), Area(172, 174)
        rinv2 = nc.alloc_sbuf_tensor_at("rinv2", [64, T], F32, offset=xp_at)
        fox = Attention("causal", lo2, hi2, ti2, rinv2)
        sel_f = lo2("sel_f", [P, 8, P], F32R)
        fox.cum_split = lo2("cum_split", [P, T], F32R)
        cum_cols = ti2("cum_cols", [P, KT, 8], F32)
        sink8 = ti2("sink8", [P, 8], F32)
        gt2 = Area(0, 20)
        f_pre2, f_log2, cum2, zero2, sel_raw2 = (gt2(f"f2_{n}", [P if n == "sel_raw" else 8, T], F32)
                                                for n in ("pre", "log", "cum", "zero", "sel_raw"))
        fox.sel = lambda head: sel_f[:, head, :]
        fox.cum_col = lambda kt, head: cum_cols[:, kt, head:head + 1]
        g.meet()
        ki = sp(lambda e: e.dma_start(sel_raw2[:, :], a["sel_f"].rearrange("p k c -> p (k c)")), sem=c_pos, by=16)
        act(lambda e: e.activation(sel_f[:, :, :].rearrange("p k c -> p (k c)"), sel_raw2[:, :], ACT.Copy), ki)
        fb = col("b_fgate")
        p = act(lambda e: e.activation(f_pre2[:, :], y2[0:8, FG, :], ACT.Identity, bias=fb[0:8, :]))
        p = act(lambda e: e.activation(f_log2[:, :], f_pre2[:, :], ACT.Abs), p)
        p = act(lambda e: e.activation(f_log2[:, :], f_log2[:, :], ACT.Exp, scale=-1.0), p)
        p = act(lambda e: e.activation(f_log2[:, :], f_log2[:, :], ACT.Ln, bias=col("one")[0:8, :]), p)
        z = dve(lambda e: e.memset(zero2[:, :], 0.0))
        z = dve(lambda e: e.memset(fox.cum_split[:, :].bitcast(F32), 0.0))
        dve(lambda e: e.tensor_scalar(sink8[:, :], small[:, SMALL["sinks"][0]:SMALL["sinks"][0] + 8], 1 / SC, None, ALU.mult))
        p = dve(lambda e: e.scalar_tensor_tensor(f_log2[:, :], f_pre2[:, :], 0.0, f_log2[:, :], ALU.min, ALU.subtract), p)
        p = dve(lambda e: e.tensor_tensor_scan(cum2[:, :], f_log2[:, :], zero2[:, :], 0.0, ALU.add, ALU.add), p, z)
        p = dve(lambda e: e.tensor_scalar(cum2[:, :], cum2[:, :], -1.0, None, ALU.mult), p)
        q = dve(lambda e: e.tensor_scalar(f_log2[:, :], cum2[:, :], 1 / SC, None, ALU.mult), p)
        h = act(lambda e: e.activation(fox.cum_split[0:8, :], f_log2[:, :], ACT.Copy), q)
        dve(lambda e: e.tensor_tensor(fox.cum_split[32:40, :], f_log2[:, :], fox.cum_split[0:8, :].bitcast(F32), ALU.subtract), h)
        for kt in range(KT):
            t = pe(lambda e, kt=kt: e.transpose(ps[:, 4, kt * 8:(kt + 1) * 8], cum2[:, kt * P:(kt + 1) * P], ident[0:8, 0:8]),
                   *([p] if kt == 0 else []), mark=(kt == KT - 1))
        act(lambda e: e.activation(cum_cols[:, :, :].rearrange("p a b -> p (a b)"), ps[:, 4, 0:64], ACT.Copy), t)
        for q in g.queues:
            q.wait(z_kept)
        g.meet()

        def row2(tile, h):
            return lambda: y2[64 * (h % 2):64 * (h % 2) + 64, tile + h // 2, :]

        def fox_prep(h):
            b, r = h % 2, h % 2
            fox.prep_q(b, r, row2(FQ, h))
            fox.prep_k(b, r, row2(FK, h))
            fox.prep_v(b, r, row2(FV, h))

        fox_prep(0)
        fox.maxima(0, 0, 0, 0)
        for h in range(8):
            if h < 7:
                fox_prep(h + 1)

                def nxt(kt, h=h):
                    fox.max_pass((h + 1) % 2, (h + 1) % 2, (h + 1) % 2, kt, h + 1)
                    if kt == KT - 1:
                        fox.max_rows((h + 1) % 2, h + 1)
            else:
                nxt = None
            fox.head(h % 2, h % 2, h % 2, h, h % 2, row2(FQ, h), nxt)
        g.meet()

        ro = Area(80, 112)
        cos2 = ro("cos2", [P, T], F32)
        sin2 = ro("sin2", [P, T], F32)
        swapped = ro("swapped", [P, 5, T], F32)
        turn2 = ro("turn2", [P, T], F32)
        pos_i = nc.alloc_sbuf_tensor_at("pos_i", [P, T], I32, offset=BASE + 168 * K1)
        for j in range(4):
            s0, d0 = 32 * j, 32 * (j ^ 1)
            swap_in = sp(lambda e, s0=s0, d0=d0: e.dma_start(swapped[d0:d0 + 32, :, :], y2[s0:s0 + 32, SQ:SQ + 5, :]),
                         sem=c_swap, by=16)
        ang = cos2
        pos_in = sp(lambda e: e.dma_start(pos_i[:, :], a["positions"].to_broadcast([P, T])), sem=c_pos, by=16)
        p = dve(lambda e: e.tensor_copy(ang[:, :], pos_i[:, :]), pos_in)
        p = dve(lambda e: e.tensor_scalar(ang[:, :], ang[:, :], col("inv_freq"), None, ALU.mult), p)
        magic = 1.5 * 2 ** 23
        p = dve(lambda e: e.tensor_scalar(turn2[:, :], ang[:, :], 1 / (2 * np.pi), magic, ALU.mult, ALU.add), p)
        p = dve(lambda e: e.tensor_scalar(turn2[:, :], turn2[:, :], magic, None, ALU.subtract), p)
        rest = 2 * np.pi
        for part in range(3):
            c = float(np.round(rest * 2 ** (5, 21, 40)[part]) / 2 ** (5, 21, 40)[part])
            rest -= c
            p = dve(lambda e, c=c: e.scalar_tensor_tensor(ang[:, :], turn2[:, :], -c, ang[:, :], ALU.mult, ALU.add), p)
        p = dve(lambda e: e.tensor_scalar(ang[:, :], ang[:, :], float(np.float32(3.1415925)), -float(np.float32(3.1415925)),
                                          ALU.min, ALU.max), p)
        q = act(lambda e: e.activation(sin2[:, :], ang[:, :], ACT.Sin), p)
        x = act(lambda e: e.activation(cos2[:, :], ang[:, :], ACT.Abs), q)
        x = act(lambda e: e.activation(cos2[:, :], cos2[:, :], ACT.Sin, bias=col("half_pi"), scale=-1.0), x)
        p = dve(lambda e: e.tensor_scalar(sin2[:, :], sin2[:, :], col("rope_sign"), None, ALU.mult), x)
        for t in range(5):
            p = dve(lambda e, t=t: e.tensor_tensor(swapped[:, t, :], swapped[:, t, :], sin2[:, :], ALU.mult), p, swap_in)
            p = dve(lambda e, t=t: e.tensor_tensor(y2[:, SQ + t, :], y2[:, SQ + t, :], cos2[:, :], ALU.mult), p)
            p = dve(lambda e, t=t: e.tensor_tensor(y2[:, SQ + t, :], y2[:, SQ + t, :], swapped[:, t, :], ALU.add), p)
        g.meet()

        band = fox
        band.kind = "band"
        bd = Area(80, 96)
        band.sf = bd("sink_f", [65, T], F32)
        band.sh = bd("sink_h", [65, T], F32R)
        band.sl = bd("sink_l", [65, T], F32R)
        band.one_row = bd("sink_to", [65, P], F32R)
        p = pool(lambda e: e.memset(band.one_row[64:65, 0:64].bitcast(F32), 0.0))
        p = pool(lambda e: e.memset(band.one_row[64:65, 64:P].bitcast(F32), 1.0), p)
        pe.wait(p)
        z2 = Area(96, 112)("z2", [P, 4, T], F32)
        z_back = sp(lambda e: e.dma_start(z2[:, :, :], z_dram), z_kept, sem=c_back, by=16)
        band.sink_raw = lambda head: sink8[:, head:head + 1]
        band.sink = lambda head: col("sinks", head)[64:65, :]
        for kv in range(2):
            band.prep_k(kv, kv, lambda kv=kv: y2[64 * kv:64 * kv + 64, SK, :])
            band.prep_v(kv, kv, lambda kv=kv: y2[64 * kv:64 * kv + 64, SV, :])
        band.prep_q(0, 0, row2(SQ, 0))
        band.maxima(0, 0, 0, 0)
        for h in range(8):
            kv, nkv = h // 4, (h + 1) // 4
            if h < 7:
                band.prep_q((h + 1) % 2, (h + 1) % 2, row2(SQ, h + 1))

                def nxt(kt, h=h, nkv=nkv):
                    band.max_pass((h + 1) % 2, nkv, nkv, kt, h + 1)
                    if kt == KT - 1:
                        band.max_rows((h + 1) % 2, h + 1)
            else:
                nxt = None
            band.head(h % 2, kv, kv, h, h % 2, row2(SQ, h), nxt)
        g.meet()

        m2 = Area(0, 64)
        mix2_hi = m2("mix2_hi", [P, KT, T], F32R)
        mix2_lo = m2("mix2_lo", [P, KT, T], F32R)
        made2 = {}
        for k in range(KT):
            src = (FQ + k) if k < 4 else (SQ + k - 4)
            x = dve(lambda e, k=k, src=src: e.tensor_tensor(y2[:, src, :], y2[:, src, :],
                                                            y2[:, FZ + k, :] if k < 4 else z2[:, k - 4, :], ALU.mult), z_back)
            x = act(lambda e, k=k, src=src: e.activation(mix2_hi[:, k, :], y2[:, src, :], ACT.Copy), x)
            made2[k] = dve(lambda e, k=k, src=src: e.tensor_tensor(mix2_lo[:, k, :], y2[:, src, :], mix2_hi[:, k, :].bitcast(F32),
                                                                   ALU.subtract), x)
        yo = Area(64, 96)("y_out", [P, 2, KT, HT], F32)
        xb = Area(112, 144)("xb", [P, 2, KT, HT], F32)
        end2 = Area(144, 164)
        sq3 = [end2(f"sq3_{s}", [P, HT], F32) for s in range(2)]
        acc3 = [end2(f"acc3_{s}", [P, HT], F32) for s in range(2)]
        rs3 = [end2(f"rs3_{s}", [P, HT], F32) for s in range(2)]
        c_xback, c_out = g.count("c_xback"), [g.count("c_out0"), g.count("c_out1")]
        for n in range(2):
            xb_in = sp(lambda e, n=n: e.dma_start(xb[:, n, :, :], xb_dram[n]), made2[KT - 1], *kept.values(), sem=c_xback, by=16)
        sp_done = dve(lambda e: e.tensor_tensor(s_post[:, :], mod2[:, 16:24], small[:, SMALL["g_post_2"][0]:SMALL["g_post_2"][0] + 8],
                                                ALU.mult), made2[KT - 1])
        act.wait(sp_done)
        read4 = [None, None]
        sqr = [None, None]
        for n in range(2):
            accp = {"p": dve(lambda e, n=n: e.memset(acc3[n][:, :], 0.0))}

            def out_tile(j, slot, ready, used, n=n, accp=accp):
                s = j % 2
                mov = [(lambda k: mix2_hi[:, k, n * HT:(n + 1) * HT], lambda k: mix2_lo[:, k, n * HT:(n + 1) * HT])]
                product(g, w, slot, [ps[:, s, :]], mov, 0, KT, True, True, [ready] + ([read4[s]] if read4[s] else []), used,
                        made2 if (n == 0 and j == 0) else None)
                q = act(lambda e: e.activation(sq3[s][:, :], ps[:, s, :], ACT.Square), used, *([sqr[s]] if sqr[s] else []))
                read4[s] = act(lambda e: e.activation(yo[:, n, j, :], ps[:, s, :], ACT.Copy, scale=s_post[:, j:j + 1]), used)
                sqr[s] = accp["p"] = dve(lambda e: e.tensor_tensor(acc3[n][:, :], acc3[n][:, :], sq3[s][:, :], ALU.add), q, accp["p"])

            w.run(8, None, out_tile, then=126 if n == 0 else -1)
            r = inverse_norm(acc3[n], 2 + n, rs3[n], accp["p"])
            for k in range(KT):
                x = dve(lambda e, k=k, n=n: e.tensor_tensor(yo[:, n, k, :], yo[:, n, k, :], rs3[n][:, :], ALU.mult), r)
                x = dve(lambda e, k=k, n=n: e.tensor_tensor(yo[:, n, k, :], yo[:, n, k, :], xb[:, n, k, :], ALU.add), x, xb_in)
                if k % 4 == 3:
                    written = sp(lambda e, k=k, n=n: e.dma_start(out[k - 3:k + 1, :, n * HT:(n + 1) * HT].rearrange("k p t -> p k t"),
                                                                 yo[:, n, k - 3:k + 1, :]), x, sem=c_out[n], by=16)
            outs_done = [written] + ([outs_done[0]] if n else [])
        sp.wait(*outs_done)
        emit(nc, g, ctx)





def emit(nc, g, ctx):
    block = ctx.enter_context(nc.Block())
    block.sync(lambda e: g.sp.run(e))
    block.gpsimd(lambda e: g.pool.run(e))
    block.scalar(lambda e: g.act.run(e))
    block.vector(lambda e: g.dve.run(e))
    block.tensor(lambda e: g.pe.run(e))



def blocks(w, cols=None):
    k, m = w.shape
    nk, nm = -(-k // P), -(-m // P)
    out = np.zeros((nk * P, nm * P), w.dtype)
    out[:k, :m] = w
    return out.reshape(nk, P, nm, P).transpose(2, 1, 0, 3).reshape(nm, P, nk * P)


def columns(v):
    return np.ascontiguousarray(v.reshape(-1, P).T)


def lay_out(i):
    f = np.float32
    w_in = i["w_in"][0]
    o = [0, 512, 640, 768, 1792, 2304, 2816]
    gates = np.zeros((D, P), f)
    gate_b = np.zeros((P,), f)
    for n, at_row in enumerate((0, 64, 32, 96)):
        gates[:, at_row:at_row + 4] = w_in[:, o[6] + 4 * n:o[6] + 4 * n + 4]
        gate_b[at_row:at_row + 4] = i["gate_b"][0, 4 * n:4 * n + 4]
    w1 = [w_in[:, o[3]:o[4]], w_in[:, :o[3]], w_in[:, o[4]:o[6]], gates]
    w_in2 = i["w_in_2"][0]
    p = [0, 1536, 1544, 2056, 2824, 3336]
    w2 = [w_in2[:, :p[1]], w_in2[:, p[2]:], w_in2[:, p[1]:p[2]]]
    gu = np.stack([blocks(i["w_gate"][0]), blocks(i["w_up"][0])], 1).reshape(2 * FT, P, D)
    down = np.zeros((KT, P, 24 * P), f)
    down[:, :, :FFN] = blocks(i["w_down"][0])
    down = down.reshape(KT, P, 3, D).transpose(0, 2, 1, 3).reshape(3 * KT, P, D)
    weights = np.concatenate([blocks(x) for x in w1] + [blocks(i["w_out"][0]), gu, down]
                             + [blocks(x) for x in w2] + [blocks(i["w_out_2"][0])])
    ada = np.concatenate([i["w_ada"][0], i["w_ada_2"][0]], 1)
    ada = np.ascontiguousarray(ada.reshape(KT, P, 36, CW).transpose(2, 1, 0, 3))
    x = np.ascontiguousarray(i["x"][0].T).reshape(KT, P, T)

    small = np.zeros((P, N_SMALL), f)

    def put(name, v):
        c, n = SMALL[name]
        small[:, c:c + n] = v

    for name in ("c", "c_2", "b_ada", "b_ada_2", "norm_mix_g", "norm_ffn_g", "final_norm_g", "g_pre_2", "g_post_2",
                 "conv_b", "mlstm_norm_g"):
        put(name, columns(i[name].reshape(-1)))
    put("qk_g", np.tile(np.stack([i["q_norm_g"][0]] * 4 + [i["k_norm_g"][0]], 1), (2, 1)))
    put("conv_w", i["conv_w"][0].reshape(5, KT, P).transpose(2, 1, 0).reshape(P, 40))
    put("gate_b", gate_b[:, None])
    fg = np.zeros((P, 1), f)
    fg[:8, 0] = i["b_fgate_2"][0]
    put("b_fgate", fg)
    put("sinks", np.broadcast_to(i["sinks_2"][0][None, :], (P, 8)))
    put("eps", EPS)
    put("tiny", 1e-37)
    put("one", 1.0)
    put("half_pi", np.pi / 2)
    half = 32
    freq = (f(10000.0) ** (-np.arange(half, dtype=f) / f(half))).astype(f)
    put("inv_freq", np.tile(freq, 4)[:, None])
    put("rope_sign", np.tile(np.repeat(np.array([-1.0, 1.0], f), 32), 2)[:, None])

    r = np.arange(P)
    row, c = r[:, None], r[None, :]
    consts = np.stack([row == c, np.ones((P, P)), row // 64 == c // 64, row == c,
                       np.where(c > row, NEG, 0), np.where(c < row, NEG, 0),
                       np.where(c <= row, NEG, 0), np.where(c >= row, NEG, 0)]).astype(f)

    inv = (f(10000.0) ** (-np.arange(0, 32, 2, dtype=f) / f(32))).astype(f)
    t = np.arange(T)
    ang = np.stack([(t // 64).astype(f)[None] * inv[:, None], (t % 64).astype(f)[None] * inv[:, None]])
    cos = np.repeat(np.cos(ang)[:, None], 2, 1).reshape(64, T)
    sin = np.stack([-np.sin(ang), np.sin(ang)], 1).reshape(64, T)
    rope = np.stack([np.tile(cos, (2, 1)), np.tile(sin, (2, 1))]).astype(f)

    sel = np.zeros((P, 8, P), f)
    for k in range(8):
        at_row = (k // 4) * 32 + k % 4
        sel[[at_row, 64 + at_row], k, :] = 1.0
    sel_f = np.zeros((P, 8, P), f)
    for k in range(8):
        sel_f[[k, 32 + k], k, :] = 1.0
    return {"weights": weights, "ada": ada, "x": x, "small": small, "consts": consts, "rope": rope,
            "sel": sel, "sel_f": sel_f, "positions": np.ascontiguousarray(i["positions_2"])}


def kernel(**inputs):
    import concourse.bacc as bacc
    from concourse.bass_utils import run_bass_kernel_spmd

    nc = bacc.Bacc("TRN2", target_bir_lowering=False, num_devices=1)
    arrays = {f"in_{n}": v for n, v in lay_out({n: np.asarray(v) for n, v in inputs.items()}).items()}
    ins = {n[3:]: nc.dram_tensor(n, v.shape, mybir.dt.from_np(v.dtype), kind="ExternalInput").ap() for n, v in arrays.items()}
    out = nc.dram_tensor("out_dram", (KT, P, T), F32, kind="ExternalOutput").ap()
    build(nc, ins, out)
    r = run_bass_kernel_spmd(nc, [arrays], core_ids=[0])
    return np.ascontiguousarray(r.results[0]["out_dram"].reshape(D, T).T)[None]
```

```python
from contextlib import ExitStack, contextmanager

import numpy as np

import concourse.bass as bass
from concourse import mybir

ALU = mybir.AluOpType
ACT = mybir.ActivationFunctionType
AX_X = mybir.AxisListType.X
F32 = mybir.dt.float32
F32R = mybir.dt.float32r
BF16 = mybir.dt.bfloat16
I32 = mybir.dt.int32

P = 128
D = 1024
T = 1024
HT = 512
KT = D // P
FFN = 2816
FT = FFN // P
EPS = 1e-6
SC = 64 ** -0.5
KSC = 128 ** -0.5
NEG = -1e30
RING = 2
CW = 256

QM, QA, KA, VA, VM, OM, GA = 0, 8, 12, 13, 14, 18, 22
N_IN1 = 23
FQ, FK, FV, FZ, SQ, SK, SV, SZ, FG = 0, 4, 8, 12, 16, 20, 21, 22, 26
N_IN2 = 27



class Count:

    def __init__(self, handle):
        self.handle, self.now = handle, 0


class Point:

    def __init__(self):
        self.count = None

    def set(self, count, by, loops):
        count.now += by
        self.count, self.first, self.loops = count, count.now, list(loops)
        return self

    def value(self, lag):
        v, inner = self.first, [x for x in self.loops if x.i is not None]
        for x in self.loops:
            step = x.step.get(self.count, 0)
            if x.i is None:
                v = v + (x.n - 1) * step
            elif step:
                v = x.i * step + v
        if lag:
            v = v - lag * inner[-1].step.get(self.count, 0)
        return v


class Loop:
    def __init__(self, n):
        self.n, self.i, self.step = n, None, {}


class Queue:

    def __init__(self, prog, count):
        self.prog, self.done, self.levels = prog, count, [[]]

    def __call__(self, fn, *waits, mark=True, sem=None, by=1, point=None):
        p = (point or Point()) if mark else None
        if p:
            p.set(sem or self.done, by, self.prog.loops)

        def emit(e):
            for w in waits:
                w, lag = w if isinstance(w, tuple) else (w, 0)
                e.wait_ge(w.count.handle, w.value(lag))
            ins = fn(e)
            if p:
                ins.then_inc(p.count.handle, by)

        self.levels[-1].append(emit)
        return p

    def wait(self, *waits):
        def emit(e):
            for w in waits:
                w, lag = w if isinstance(w, tuple) else (w, 0)
                e.wait_ge(w.count.handle, w.value(lag))

        self.levels[-1].append(emit)

    def run(self, e, items=None):
        for x in self.levels[0] if items is None else items:
            if isinstance(x, tuple):
                loop, body = x
                with e.Fori(0, loop.n) as i:
                    loop.i = i
                    self.run(e, body)
                loop.i = None
            else:
                x(e)


class Program:

    def __init__(self, nc, ctx):
        self.nc, self.ctx, self.loops, self.counts = nc, ctx, [], []
        self.pe, self.act, self.dve, self.pool, self.sp = (
            Queue(self, self.count(n)) for n in ("pe_done", "act_done", "dve_done", "pool_done", "sp_done"))
        self.queues = [self.pe, self.act, self.dve, self.pool, self.sp]

    def count(self, name):
        c = Count(self.ctx.enter_context(self.nc.semaphore(name)))
        self.counts.append(c)
        return c

    def start_high(self, by=256):
        for q in self.queues[:4]:
            h = q.done.handle
            q.levels[-1].append(lambda e, h=h: e.sem_inc(h, by))
            q.done.now += by

    @contextmanager
    def loop(self, n):
        x, before = Loop(n), {c: c.now for c in self.counts}
        for q in self.queues:
            q.levels.append([])
        self.loops.append(x)
        yield x
        self.loops.pop()
        for q in self.queues:
            body = q.levels.pop()
            if body:
                q.levels[-1].append((x, body))
        for c in self.counts:
            x.step[c] = c.now - before.get(c, 0)
            c.now += (n - 1) * x.step[c]

    def last(self, q):
        p = Point()
        p.count, p.first, p.loops = q.done, q.done.now, []
        return p

    def meet(self, *queues):
        ends = [(q, self.last(q)) for q in (self.pe, self.act, self.dve, self.pool)]
        for q in queues or self.queues:
            q.wait(*[p for o, p in ends])


class Weights:

    def __init__(self, g, dram, place):
        self.g, self.dram = g, dram
        self.raw = [place(f"w_raw{s}", [P, KT * P], F32) for s in range(RING)]
        self.hi = [place(f"w_hi{s}", [P, KT * P], F32R) for s in range(RING)]
        self.lo = [place(f"w_lo{s}", [P, KT * P], F32R) for s in range(RING)]
        self.landed = [g.count(f"w_landed{s}") for s in range(RING)]
        self.n = 0
        self.phase = 0
        self.used = [None]
        self.split = []

    def fetch(self, slot, index, raw_free, used, split_point=None):
        g, raw, hi, lo = self.g, self.raw[slot], self.hi[slot], self.lo[slot]
        landed = g.sp(lambda e: e.dma_start(raw[:, :], self.dram[index()]), *raw_free,
                      sem=self.landed[slot], by=16)
        rounded = g.act(lambda e: e.activation(hi[:, :], raw[:, :], ACT.Copy), landed, *used)
        return g.dve(lambda e: e.tensor_tensor(lo[:, :], raw[:, :], hi[:, :].bitcast(F32), ALU.subtract),
                     rounded, point=split_point)

    def first(self):
        self.split = [None, self.fetch(0, lambda: 0, (), ())]

    def run(self, nb, loop, work, then=None):
        base, g = self.n, self.g
        used, split = [Point() for _ in range(nb)], [Point() for _ in range(nb)]
        if loop:
            assert nb % RING == 0
        for j in range(nb):
            slot = (self.phase + j) % RING
            if loop:
                at_step = (lambda jj: lambda: loop.i * nb + (base + jj + 1))(j)
                free = [split[j - 2] if j > 1 else (split[j - 2], 1)]
                was_used = [used[j - 1] if j else (used[nb - 1], 1)]
                ready = split[j - 1] if j else (split[nb - 1], 1)
            else:
                index = base + j + 1 if j < nb - 1 or then is None else then
                at_step = (lambda index: lambda: index)(index)
                back = lambda pts, old, k: pts[k] if k >= 0 else old[k]
                free = [x for x in [back(split, self.split, j - 2)] if x]
                was_used = [x for x in [back(used, self.used, j - 1)] if x]
                ready = back(split, self.split, j - 1)
            if loop or index >= 0:
                self.fetch((slot + 1) % RING, at_step, free, was_used, split[j])
            work(j, slot, ready, used[j])
        if not loop:
            self.used, self.split, self.n = (self.used + used)[-2:], (self.split + split)[-2:], base + nb
            self.n = self.n if then is None else then
            self.phase += nb
        else:
            self.used, self.split, self.n = used[-2:], split[-2:], base + nb * loop.n

    def enter(self):
        g = self.g
        last_used = [x for x in self.used[-1:] if x]
        g.sp.wait(self.split[-1])
        g.act.wait(*last_used)
        g.dve.wait(*last_used)
        g.pe.wait(self.split[-1])


def product(g, w, slot, out, moving, k0, nk, first, last, waits, point, made=None):
    hi, lo = w.hi[slot], w.lo[slot]
    for k in range(nk):
        for n, (mh, ml) in enumerate(moving):
            for a, b, which in ((hi, mh, 0), (hi, ml, 1), (lo, mh, 2)):
                wt = list(waits) if (k == 0 and n == 0 and which == 0) else []
                if made and n == 0 and which == 0:
                    wt.append(made[k])
                end = k == nk - 1 and n == len(moving) - 1 and which == 2
                g.pe(lambda e, a=a, b=b, k=k, n=n, which=which: e.matmul(
                    out[n], a[:, k * P:(k + 1) * P], b(k0 + k),
                    start=(first and k == 0 and which == 0),
                    stop=(last and k == nk - 1 and which == 2)),
                    *wt, mark=end, point=point if end else None)



BASE = 16512
K1 = 1024

SMALL = {}
_at = 0
for _name, _n in (("c", 8), ("c_2", 8), ("b_ada", 48), ("b_ada_2", 24), ("norm_mix_g", 8), ("norm_ffn_g", 8),
                  ("final_norm_g", 8), ("g_pre_2", 8), ("g_post_2", 8), ("qk_g", 5), ("conv_w", 40),
                  ("conv_b", 8), ("gate_b", 1), ("mlstm_norm_g", 4), ("b_fgate", 1), ("sinks", 8),
                  ("eps", 1), ("tiny", 1), ("one", 1), ("half_pi", 1), ("inv_freq", 1), ("rope_sign", 1)):
    SMALL[_name] = (_at, _n)
    _at += _n
N_SMALL = _at


def build(nc, a, out):
    with ExitStack() as ctx:
        g = Program(nc, ctx)
        ps = ctx.enter_context(nc.psum_tensor("ps", [P, 8, HT], F32))

        class Area:

            def __init__(self, start_kb, end_kb):
                self.at, self.end = int(start_kb * K1), int(end_kb * K1)

            def __call__(self, name, shape, dt):
                size = int(np.prod(shape[1:])) * (2 if dt == BF16 else 4)
                t = nc.alloc_sbuf_tensor_at(name, shape, dt, offset=BASE + self.at)
                self.at += (size + 31) // 32 * 32
                assert self.at <= self.end, name
                return t

        fixed = Area(198, 207.5)
        w = Weights(g, a["weights"], Area(174, 198))
        small = fixed("small", [P, N_SMALL], F32)
        ident = fixed("ident", [P, P], F32)
        ones = fixed("ones", [P, P], F32)
        pair_ones = fixed("pair_ones", [P, P], F32)
        ident_b = fixed("ident_b", [P, P], BF16)
        low_keep = fixed("low_keep", [P, P], BF16)
        up_keep = fixed("up_keep", [P, P], BF16)
        band_keep = fixed("band_keep", [P, P], BF16)
        band_keep_t = fixed("band_keep_t", [P, P], BF16)
        mod1 = fixed("mod1", [P, 48], F32)
        mod2 = fixed("mod2", [P, 24], F32)
        cs = fixed("cs", [P, 16], F32)
        s_mix = fixed("s_mix", [P, KT], F32)
        s_ffn = fixed("s_ffn", [P, KT], F32)
        s_pre = fixed("s_pre", [P, KT], F32)
        s_post = fixed("s_post", [P, KT], F32)

        def col(name, i=0):
            o, n = SMALL[name]
            return small[:, bass.ds(o + i, 1)] if not isinstance(i, int) else small[:, o + i:o + i + 1]

        pe, act, dve, pool, sp = g.pe, g.act, g.dve, g.pool, g.sp
        g.start_high()

        c_small = g.count("c_small")
        c_const = g.count("c_const")
        got_small = sp(lambda e: e.dma_start(small[:, :], a["small"]), sem=c_small, by=16)
        for n, t in enumerate((ident, ones, pair_ones)):
            got_const = sp(lambda e, n=n, t=t: e.dma_start(t[:, :], a["consts"][n]), sem=c_const, by=16)
        cmask = Area(0, 64)("cmask", [P, 5, P], F32)
        got_const = sp(lambda e: e.dma_start(cmask[:, :, :], a["consts"][3:8].rearrange("n p c -> p n c")),
                       sem=c_const, by=16)

        xt = Area(64, 96)("xt", [P, KT, T], F32)
        ada = Area(156, 174)
        wa = [ada(f"wa{s}", [P, KT, CW], F32) for s in range(2)]
        acc_a = [ada(f"acc_a{s}", [P, CW], F32) for s in range(2)]
        wa_landed = [g.count(f"wa_landed{s}") for s in range(2)]
        c_x = g.count("c_x")

        cs_done = act(lambda e: e.activation(cs[:, :], small[:, 0:16], ACT.Silu), got_small)
        for n, t in enumerate((ident_b, low_keep, up_keep, band_keep, band_keep_t)):
            masks_done = pool(lambda e, n=n, t=t: e.tensor_copy(t[:, :], cmask[:, n, :]), got_const)

        class Ada:
            def __init__(self):
                self.acc_used = [None, None]
                self.acc_done = [None, None]
                self.ps_used = None

            def rows_on_pool(self, rows, acc, vec, waits, point=None):
                p = pool(lambda e: e.tensor_tensor(rows[:, :, :], rows[:, :, :],
                                                   cs[:, vec:vec + KT].unsqueeze(2).to_broadcast([P, KT, CW]), ALU.mult), *waits)
                for n in (4, 2):
                    p = pool(lambda e, n=n: e.tensor_tensor(rows[:, 0:n, :], rows[:, 0:n, :], rows[:, n:2 * n, :], ALU.add), p)
                return pool(lambda e: e.tensor_tensor(acc[:, :], rows[:, 0, :], rows[:, 1, :], ALU.add), p, point=point)

            def block(self, slot, index, vec, out_cols, bias_cols, lag=None, on_pool=False):
                mk = lag or {}
                free = mk.get("acc_done") or self.acc_done[slot]
                landed = sp(lambda e: e.dma_start(wa[slot][:, :, :], a["ada"][index()]),
                            *([free] if free else []), sem=wa_landed[slot], by=16)
                used = mk.get("acc_used") or self.acc_used[slot]
                p = None
                if on_pool:
                    p = self.rows_on_pool(wa[slot], acc_a[slot], vec, [landed, cs_done] + ([used] if used else []),
                                          mk.get("new_acc_done"))
                for k in range(0 if on_pool else KT):
                    wk = [landed, cs_done] if k == 0 else [p]
                    if k == 0 and used:
                        wk.append(used)
                    if k == 0:
                        p = dve(lambda e, k=k: e.tensor_scalar(acc_a[slot][:, :], wa[slot][:, k, :],
                                cs[:, vec + k:vec + k + 1], None, ALU.mult), *wk)
                    else:
                        p = dve(lambda e, k=k: e.scalar_tensor_tensor(
                            acc_a[slot][:, :], wa[slot][:, k, :], cs[:, vec + k:vec + k + 1], acc_a[slot][:, :],
                            ALU.mult, ALU.add), *wk, point=mk.get("new_acc_done") if k == KT - 1 else None)
                self.acc_done[slot] = p
                ps_used = mk.get("ps_used") or self.ps_used
                for h in range(2):
                    u = pe(lambda e, h=h: e.matmul(ps[:, 7, h:h + 1], acc_a[slot][:, h * P:(h + 1) * P], ones[:, 0:1],
                                                   start=(h == 0), stop=True, skip_group_check=True),
                           *(([p, got_const] + ([ps_used] if ps_used else [])) if h == 0 else []), mark=(h == 1),
                           point=mk.get("new_acc_used") if h == 1 else None)
                self.acc_used[slot] = u
                self.ps_used = dve(lambda e: e.tensor_tensor(out_cols(), ps[:, 7, 0:2], bias_cols(), ALU.add),
                                   u, point=mk.get("new_ps_used"))

        ada_m = Ada()

        early = Area(130, 156)
        early_wa = [early(f"early_wa{s}", [P, KT, CW], F32) for s in range(3)]
        early_acc = [early(f"early_acc{s}", [P, CW], F32) for s in range(2)]
        buffers = [wa[0], wa[1], *early_wa]
        early_landed = [g.count(f"early_landed{s}") for s in range(5)]
        free_wa = [None] * 5

        def ada_load(i):
            s = i % 5
            return sp(lambda e: e.dma_start(buffers[s][:, :, :], a["ada"][i]), *([free_wa[s]] if free_wa[s] else []),
                      sem=early_landed[s], by=16)

        def ada_early(i, how, landed, n_acc):
            s, o = i % 5, SMALL["b_ada"][0] + 2 * i
            rows, acc = buffers[s], (acc_a + early_acc)[n_acc]
            if how == "pe":
                for h in range(2):
                    for k in range(KT):
                        u = pe(lambda e, h=h, k=k: e.matmul(ps[:, 7, 2 * i + h:2 * i + h + 1], rows[:, k, h * P:(h + 1) * P], cs[:, k:k + 1],
                                                            start=(k == 0), stop=(k == KT - 1), skip_group_check=True),
                               *([landed, cs_done] if (h, k) == (0, 0) else []),
                               mark=((h, k) == (1, KT - 1)))
                free_wa[s] = u
            else:
                if how == "pool":
                    p = ada_m.rows_on_pool(rows, acc, 0, [landed, cs_done])
                else:
                    p = dve(lambda e: e.tensor_scalar(acc[:, :], rows[:, 0, :], cs[:, 0:1], None, ALU.mult), landed, cs_done)
                    for k in range(1, KT):
                        p = dve(lambda e, k=k: e.scalar_tensor_tensor(acc[:, :], rows[:, k, :], cs[:, k:k + 1], acc[:, :],
                                                                      ALU.mult, ALU.add), p)
                free_wa[s] = p
                for h in range(2):
                    u = pe(lambda e, h=h: e.matmul(ps[:, 7, 2 * i + h:2 * i + h + 1], acc[:, h * P:(h + 1) * P], ones[:, 0:1],
                                                   start=True, stop=True, skip_group_check=True),
                           *([p, got_const] if h == 0 else []), mark=(h == 1))
            ada_m.acc_done = [free_wa[0], free_wa[1]]
            ada_m.acc_used = [u, u]

        x_in = [sp(lambda e, n=n: e.dma_start(xt[:, 4 * n:4 * n + 4, :], a["x"][4 * n:4 * n + 4].rearrange("k p t -> p k t")),
                   sem=g.count(f"c_x{n}"), by=16) for n in range(2)]
        w.first()
        hA = Area(0, 64)
        h_hi = hA("h_hi", [P, KT, T], F32R)
        h_lo = hA("h_lo", [P, KT, T], F32R)
        nrm = Area(96, 130)
        sq = [nrm(f"sq{s}", [P, HT], F32) for s in range(2)]
        wide = [nrm(f"wide{s}", [P, T], F32) for s in range(2)]
        acc = [nrm(f"acc{s}", [P, HT], F32) for s in range(2)]
        rstd = [nrm(f"rstd{s}", [P, HT], F32) for s in range(2)]

        def scale_col(dst, gain, sc_at, mod, *waits):
            o, n = SMALL[gain]
            return dve(lambda e: e.scalar_tensor_tensor(dst[:, :], mod[:, sc_at:sc_at + KT], 1.0, small[:, o:o + n],
                                                        ALU.add, ALU.mult), *waits)

        def square_sum(src, sq, acc, *waits):
            p = dve(lambda e: e.memset(acc[:, :], 0.0))
            read = [None, None]
            for k in range(KT):
                s = k % 2
                q = act(lambda e, k=k, s=s: e.activation(sq[s][:, :], src(k), ACT.Square),
                        *(list(waits) if k == 0 else []), *([read[s]] if read[s] else []))
                p = dve(lambda e, s=s: e.tensor_tensor(acc[:, :], acc[:, :], sq[s][:, :], ALU.add), q, p)
                read[s] = p
            return p

        def exp_tables():
            act(lambda e: e.preload_act_table_set("natural_log_exp_and_others"), mark=False)

        def inverse_norm(acc, bank, dst, *waits, tables=True):
            if tables:
                exp_tables()
            m = pe(lambda e: e.matmul(ps[:, bank, :], ones[:, :], acc[:, :], start=True, stop=True), *waits)
            l = act(lambda e: e.activation(dst[:, :], ps[:, bank, :], ACT.Ln, bias=col("eps"), scale=1.0 / D), m)
            return act(lambda e: e.activation(dst[:, :], dst[:, :], ACT.Exp, scale=-0.5), l)

        plan = (("pe", 0), ("pe", 0), ("pe", 0), ("pool", 0), ("pe", 0), ("dve", 1), ("pool", 2), ("dve", 3))
        loaded = [ada_load(i) for i in range(5)]
        ada_early(0, *plan[0][:1], loaded[0], 0)
        halves_of = [slice(n * HT, (n + 1) * HT) for n in range(2)]
        for n, ts in enumerate(halves_of):
            p = square_sum(lambda k, ts=ts: xt[:, k, ts], sq, acc[n], *x_in, masks_done)
            r = inverse_norm(acc[n], 4 + n, rstd[n], p, got_const)
            if n == 0:
                ada_early(1, "pe", loaded[1], 0)
            for k in range(KT):
                scaled = dve(lambda e, k=k, n=n, ts=ts: e.tensor_tensor(xt[:, k, ts], xt[:, k, ts], rstd[n][:, :], ALU.mult), r)
        for i in (2, 3, 4):
            ada_early(i, plan[i][0], loaded[i], plan[i][1])
        loaded += [ada_load(i) for i in range(5, 8)]
        for i in (5, 6, 7):
            ada_early(i, plan[i][0], loaded[i], plan[i][1])
        o = SMALL["b_ada"][0]
        ada_m.ps_used = dve(lambda e: e.tensor_tensor(mod1[:, 0:16], ps[:, 7, 0:16], small[:, o:o + 16], ALU.add), g.last(pe))
        sm_done = scale_col(s_mix, "norm_mix_g", 8, mod1, ada_m.ps_used)
        p, free_tt, h_made = None, [None, None], {}
        for k in range(KT):
            s = k % 2
            x = dve(lambda e, k=k, s=s: e.tensor_scalar(wide[s][:, :], xt[:, k, :], s_mix[:, k:k + 1], mod1[:, k:k + 1],
                                                        ALU.mult, ALU.add), scaled, sm_done, *([free_tt[s]] if free_tt[s] else []))
            x = act(lambda e, k=k, s=s: e.activation(h_hi[:, k, :], wide[s][:, :], ACT.Copy), x)
            if p:
                p()

            def p(k=k, s=s, x=x):
                h_made[k] = free_tt[s] = dve(lambda e: e.tensor_tensor(h_lo[:, k, :], wide[s][:, :], h_hi[:, k, :].bitcast(F32),
                                                                       ALU.subtract), x)
        p()
        h_done = h_made[KT - 1]

        y = Area(64, 156)("y", [P, N_IN1, T], F32)

        def project(n_tiles, dst, extra=None, func=ACT.Copy, rolled=True, made=None):
            parts = (h_hi_cur, h_lo_cur)

            def work(j, slot, ready, used, lp=None):
                bank = 2 * (j % 2)
                waits = [ready]
                if lp is not None:
                    waits.append((evac_pt[j], 1))
                elif prev_evac[j % 2]:
                    waits.append(prev_evac[j % 2])
                mov = [(lambda k, n=n: parts[0](k, n), lambda k, n=n: parts[1](k, n)) for n in range(2)]
                product(g, w, slot, [ps[:, bank + n, :] for n in range(2)], mov, 0, KT, True, True, waits, used, made if j == 0 else None)
                prev_evac[j % 2] = act(lambda e, j=j: e.activation(dst(lp.i * 2 + j if lp else j), ps[:, bank:bank + 2, :]
                                                                    .rearrange("p a b -> p (a b)"), func),
                                       used, point=evac_pt[j] if lp is not None else None)
                if extra:
                    extra(j, lp)

            evac_pt = [Point(), Point()]
            if n_tiles > 1 and rolled:
                w.enter()
                pe.wait(*[x for x in prev_evac if x])
                with g.loop(n_tiles // 2) as lp:
                    w.run(2, lp, lambda j, slot, ready, used: work(j, slot, ready, used, lp))
            else:
                w.run(n_tiles, None, lambda j, slot, ready, used: work(j, slot, ready, used))

        prev_evac = [None, None]
        h_hi_cur = lambda k, n: h_hi[:, k, n * HT:(n + 1) * HT]
        h_lo_cur = lambda k, n: h_lo[:, k, n * HT:(n + 1) * HT]
        act.wait(h_done)

        class Lagged:

            def __init__(self, uses):
                self.uses = uses
                self.done, self.used, self.psu = [Point(), Point()], [Point(), Point()], Point()

            def keys(self, u, first_of_slot, last_of_slot):
                s = self.uses[u]
                d = {}
                if first_of_slot:
                    d["acc_done"], d["acc_used"] = (self.done[s], 1), (self.used[s], 1)
                if last_of_slot:
                    d["new_acc_done"], d["new_acc_used"] = self.done[s], self.used[s]
                if u == 0:
                    d["ps_used"] = (self.psu, 1)
                if u == len(self.uses) - 1:
                    d["new_ps_used"] = self.psu
                return d

        def ada_loop_block(lg, u, first, per, lp, second=False):
            s = lg.uses[u]
            keys = lg.keys(u, u == lg.uses.index(s), u == len(lg.uses) - 1 - lg.uses[::-1].index(s))
            b0 = SMALL["b_ada_2"][0] if second else SMALL["b_ada"][0]
            m = mod2 if second else mod1
            o = first + u - (24 if second else 0)
            ada_m.block(s, lambda: lp.i * per + (first + u), 8 if second else 0,
                        lambda: m[:, bass.ds(lp.i * (2 * per) + 2 * o, 2)],
                        lambda: small[:, bass.ds(lp.i * (2 * per) + (b0 + 2 * o), 2)], keys, on_pool=(s == 1))

        def ada_enter():
            sp.wait(*[x for x in ada_m.acc_done if x])
            dve.wait(*[x for x in ada_m.acc_used if x])
            pool.wait(*[x for x in ada_m.acc_used if x])
            pe.wait(ada_m.ps_used)

        xp_at = BASE + fixed.at
        xp = fixed("xp", [P, T + 4], F32)
        pads = dve(lambda e: e.memset(xp[:, :], 0.0))
        cw = SMALL["conv_w"][0]
        conv = {"taps": None}

        def conv_tile(t, lagged=None, meanwhile=None):
            free = [(lagged, 1)] if lagged else [x for x in [conv["taps"]] if x]
            p = act(lambda e: e.activation(xp[:, 2:2 + T], y[:, t(), :], ACT.Copy), pads, *free)
            p = dve(lambda e: e.tensor_scalar(y[:, t(), :], xp[:, 0:T], small[:, bass.ds(t() * 5 + cw, 1)], None, ALU.mult), p)
            for j in range(1, 5):
                p = dve(lambda e, j=j: e.scalar_tensor_tensor(
                    y[:, t(), :], xp[:, j:j + T], small[:, bass.ds(t() * 5 + (cw + j), 1)], y[:, t(), :], ALU.mult, ALU.add),
                    p, point=lagged if j == 4 else None)
            conv["taps"] = p
            if meanwhile:
                meanwhile()
            conv["done"] = act(lambda e: e.activation(y[:, t(), :], y[:, t(), :], ACT.Silu,
                                                      bias=small[:, bass.ds(t() + SMALL["conv_b"][0], 1)]), p)

        ada_enter()
        lg = Lagged([0, 1, 0])
        project(8, lambda m: y[:, m, :], made=h_made,
                extra=lambda j, lp: [ada_loop_block(lg, u, 8, 3, lp) for u in ((0, 1), (2,))[j]])
        act.wait(prev_evac[0], prev_evac[1])
        ada_enter()
        lg2, taps2 = Lagged([0, 1]), Point()
        project(4, lambda m: y[:, 8 + m, :],
                extra=lambda j, lp: (ada_loop_block(lg2, j, 20, 2, lp),
                                     conv_tile(lambda: lp.i, taps2) if j == 0 else None))
        ada_enter()
        lg3, taps3 = Lagged([0, 1, 0]), Point()
        act.wait(taps2)
        project(8, lambda m: y[:, 12 + m, :],
                extra=lambda j, lp: ([ada_loop_block(lg3, u, 24, 3, lp, True) for u in ((0, 1), (2,))[j]],
                                     conv_tile(lambda: lp.i + 2, taps3) if j == 0 else None))
        project(2, lambda m: y[:, 20 + m, :],
                extra=lambda j, lp: conv_tile(lambda: 6) if j == 0 else None)
        def output_gates():
            act(lambda e: e.activation(y[:, OM:OM + 4, :], y[:, OM:OM + 4, :], ACT.Sigmoid), *prev_evac)

        project(1, lambda m: y[:, 22, :], extra=lambda j, lp: conv_tile(lambda: 7, meanwhile=output_gates))
        def pieces(q0, q1):
            return [(n, max(q0, n * HT), min(q1, (n + 1) * HT)) for n in range(2) if max(q0, n * HT) < min(q1, (n + 1) * HT)]

        def flat(b0):
            return ps[:, b0:b0 + 2, :].rearrange("p a b -> p (a b)")

        class Attention:

            def __init__(self, kind, area, area2, maxima, rinv):
                self.kind = kind
                n = kind
                self.kk = [area(f"{n}_kk{s}", [P, T], F32R) for s in range(2)]
                self.ka = [area(f"{n}_ka{s}", [P, T], F32R) for s in range(2)]
                self.qq = [area(f"{n}_qq{s}", [P, T], F32R) for s in range(2)]
                self.qa = [area(f"{n}_qa{s}", [P, T], F32R) for s in range(2)]
                self.vh = [area(f"{n}_vh{s}", [P, KT, P], F32R) for s in range(2)]
                self.vl = [area(f"{n}_vl{s}", [P, KT, P], F32R) for s in range(2)]
                self.rinv = rinv
                self.ph = [area(f"{n}_ph{s}", [P, T], F32R) for s in range(3)]
                at = area2.at
                self.pf = [area2(f"{n}_pf{s}", [P, T], F32) for s in range(3)]
                again = Area(at / K1, area2.at / K1)
                self.pl = [again(f"{n}_pl{s}", [P, T], F32R) for s in range(3)]
                self.mx, self.mh = maxima
                self.end = {}
                self.unit = 0
                p = None
                for s in range(2):
                    for t, value in ((self.ka[s][64:65, :], 1.0), (self.vh[s][:, :, 64:P], 1.0), (self.vl[s][:, :, 64:P], 0.0),
                                     (self.mh[s][:, :, :], NEG)):
                        p = pool(lambda e, t=t, value=value: e.memset(t.bitcast(F32) if t.dtype == F32R else t, value),
                                 *([p] if p else []))
                self.ones_set = p

            def free(self, *names):
                return [self.end[n] for n in names if self.end.get(n)]

            def rows(self, a):
                return slice(64 * a, 64 * a + 64)

            def query_range(self, kt):
                return {"full": (0, T), "causal": (kt * P, T), "band": (kt * P, min(kt + 2, KT) * P)}[self.kind]

            def prep_k(self, b, a, src, part=None, waits=()):
                r, o = self.rows(a), self.rows(1 - a)
                if part in (None, 0):
                    self.end[f"kk_made{b}"] = act(lambda e: e.activation(self.kk[b][r, :], src(), ACT.Copy), *waits, *self.free(f"kk{b}"))
                if part in (None, 2):
                    self.end[f"kk_copy{b}"] = dve(lambda e: e.tensor_copy(self.ka[b][0:64, :], src()), *waits, *self.free(f"kk{b}"))
                    self.end[f"kk_low{b}"] = dve(lambda e: e.tensor_tensor(self.kk[b][o, :], src(), self.kk[b][r, :].bitcast(F32),
                                                                          ALU.subtract), *self.free(f"kk{b}", f"kk_made{b}"))

            def prep_q(self, b, a, src, part=None, waits=()):
                r, o = self.rows(a), self.rows(1 - a)
                if part in (None, 0):
                    self.end[f"q_made{b}"] = act(lambda e: e.activation(self.qq[b][r, :], src(), ACT.Copy), *waits, *self.free(f"qq{b}"))
                    self.end[f"q_copy{b}"] = dve(lambda e: e.tensor_copy(self.qq[b][o, :], src()), *waits, *self.free(f"qq{b}"))
                if part in (None, 1):
                    self.end[f"q_low{b}"] = dve(lambda e: e.tensor_tensor(self.qa[b][0:64, :], src(), self.qq[b][r, :].bitcast(F32),
                                                                         ALU.subtract), *self.free(f"qq{b}", f"q_made{b}"))

            def max_bank(self):
                self.unit += 1
                bank = 4 + self.unit % 2
                return bank, self.free(f"bank{bank}")

            def prep_v(self, s, a, src, *waits):
                r = self.rows(a)
                bank, was = self.max_bank()
                for k in range(KT):
                    t = pe(lambda e, k=k: e.transpose(ps[:, bank, k * 64:(k + 1) * 64], src()[:, k * P:(k + 1) * P],
                                                      ident[r, 64 * a:64 * a + 64]),
                           *((*waits, *was) if k == 0 else ()), mark=(k == KT - 1))
                v = lambda: ps[:, bank, :].rearrange("p (k f) -> p k f", k=KT)
                h = act(lambda e: e.activation(self.vh[s][:, :, 0:64], v(), ACT.Copy), t, self.ones_set, *self.free(f"v{s}"))
                self.end[f"bank{bank}"] = self.end[f"v_made{s}"] = dve(
                    lambda e: e.tensor_tensor(self.vl[s][:, :, 0:64], v(), self.vh[s][:, :, 0:64].bitcast(F32), ALU.subtract), h)

            def units(self):
                if self.kind == "band":
                    return [(qt, None) for qt in range(0, KT, 2)]
                return [(qt, n) for qt in range(KT) for n in range(2) if self.kind == "full" or n * HT < (qt + 1) * P]

            def max_unit(self, b, kb, ka_row, unit, head, first):
                qt, half = unit
                r = self.rows(ka_row)
                bank, waits = self.max_bank()
                if first:
                    waits = waits + self.free(f"q_made{b}", f"q_copy{b}", f"kk_made{kb}", f"mx{b}")
                todo = []
                if half is not None:
                    k0, k1 = half * HT, min((half + 1) * HT, T if self.kind == "full" else (qt + 1) * P)
                    todo.append((0, k1 - k0, self.qq[b][r, qt * P:(qt + 1) * P], self.kk[kb][r, k0:k1], True))
                    if self.kind == "causal":
                        todo.append((0, k1 - k0, self.sel(head), self.cum_split[:, k0:k1], False))
                        if k1 == (qt + 1) * P:
                            todo.append((k1 - P - k0, k1 - k0, ident_b[:, :], low_keep[:, :], False))
                else:
                    for i in range(2):
                        q = qt + i
                        for j, key in enumerate((max(q - 1, 0), q)):
                            c = (2 * i + j) * P
                            todo.append((c, c + P, self.qq[b][r, q * P:(q + 1) * P], self.kk[kb][r, key * P:(key + 1) * P], True))
                            todo.append((c, c + P, ident_b[:, :], (low_keep if key == q else band_keep)[:, :], False))
                for j, (c0, c1, x, z, start) in enumerate(todo):
                    end = j == len(todo) - 1
                    p = pe(lambda e, c0=c0, c1=c1, x=x, z=z, start=start, end=end: e.matmul(
                        ps[:, bank, c0:c1], x, z, start=start, stop=end, skip_group_check=True),
                        *(waits if j == 0 else ()), mark=end)
                if half is None:
                    red = lambda e: e.tensor_reduce(self.mx[b][:, qt:qt + 2], ps[:, bank, :].rearrange("p (a k) -> p a k", a=2),
                                                    AX_X, ALU.max)
                else:
                    red = lambda e: e.tensor_reduce(self.mh[b][:, half, qt:qt + 1], ps[:, bank, 0:k1 - k0], AX_X, ALU.max)
                self.end[f"bank{bank}"] = self.end["reduced"] = dve(red, p, *([self.ones_set, *self.free(f"mx{b}")] if first else []))

            def max_columns(self, b, head):
                p = self.end["reduced"]
                if self.kind == "band":
                    p = dve(lambda e: e.tensor_scalar(self.mx[b][:, :], self.mx[b][:, :], self.sink_raw(head), None, ALU.max), p)
                else:
                    p = dve(lambda e: e.tensor_tensor(self.mx[b][:, :], self.mh[b][:, 0, :], self.mh[b][:, 1, :], ALU.max), p)
                self.end["columns"] = p

            def max_rows(self, b, head):
                p = self.end["columns"]
                for qt in range(KT):
                    t = pe(lambda e, qt=qt: e.transpose(ps[0:1, 4 + qt // 4, (qt % 4) * P:(qt % 4 + 1) * P],
                                                      self.mx[b][:, qt:qt + 1], ident[:, :]),
                           *([p, *self.free("bank4", "bank5")] if qt == 0 else []), mark=(qt == KT - 1))
                self.end[f"mx{b}"] = t
                m = act(lambda e: e.activation(self.qa[b][64:65, :], ps[0:1, 4:6, :].rearrange("p a b -> p (a b)"),
                                               ACT.Copy, scale=-1.0), t, *self.free(f"qq{b}"))
                self.end["bank4"] = self.end["bank5"] = self.end[f"row{b}"] = m
                if self.kind == "band":
                    m = act(lambda e: e.activation(self.sf[64:65, :], self.qa[b][64:65, :].bitcast(F32), ACT.Exp,
                                                   bias=self.sink(head), scale=SC), m, *self.free(f"sf"))
                    m = act(lambda e: e.activation(self.sh[b][64:65, :], self.sf[64:65, :], ACT.Copy), m, *self.free(f"sink{b}"))
                    self.end["sf"] = self.end[f"sink_made{b}"] = dve(lambda e: e.tensor_tensor(
                        self.sl[b][64:65, :], self.sf[64:65, :], self.sh[b][64:65, :].bitcast(F32), ALU.subtract), m)

            def group(self, i):
                return range(4 * i, 4 * i + 4) if self.kind == "band" else [i]

            def scores(self, i, b, kb, gr, head):
                s, bank = i % 3, 2 * (i % 2)
                waits = self.free(f"s_read{i % 2}")
                if gr == 0:
                    waits += self.free(f"row{b}", f"q_low{b}", f"kk_low{kb}", f"kk_copy{kb}")
                todo = []
                for kt in self.group(gr):
                    keys = slice(kt * P, (kt + 1) * P)
                    if self.kind == "band":
                        n, c = bank + kt % 4 // 2, (kt % 2) * 256
                        for j in range(2):
                            q = min(kt + j, KT - 1)
                            qs, o = slice(q * P, (q + 1) * P), (n, c + j * P, c + (j + 1) * P)
                            todo.append((*o, self.kk[kb][:, keys], self.qq[b][:, qs], True))
                            todo.append((*o, self.ka[kb][0:65, keys], self.qa[b][0:65, qs], False))
                            todo.append((*o, ident_b[:, :], (band_keep_t if j else up_keep)[:, :], False))
                        cols = (0, T)
                    else:
                        cols = q0, q1 = self.query_range(kt)
                        for n, c0, c1 in pieces(q0, q1):
                            o = (bank + n, c0 - n * HT, c1 - n * HT)
                            todo.append((*o, self.kk[kb][:, keys], self.qq[b][:, c0:c1], True))
                            todo.append((*o, self.ka[kb][0:65, keys], self.qa[b][0:65, c0:c1], False))
                            if self.kind == "causal" and c0 <= kt * P < c1:
                                todo.append((bank + n, kt * P - n * HT, kt * P - n * HT + P, ident_b[:, :], up_keep[:, :], False))
                for j, (n, c0, c1, x, z, start) in enumerate(todo):
                    end = j == len(todo) - 1
                    p = pe(lambda e, n=n, c0=c0, c1=c1, x=x, z=z, start=start, end=end: e.matmul(
                        ps[:, n, c0:c1], x, z, start=start, stop=end, skip_group_check=True),
                        *(waits if j == 0 else ()), mark=end)
                if kt == KT - 1:
                    self.end[f"qq{b}"] = self.end[f"kk{kb}"] = p
                c0, c1 = cols
                bias = {} if self.kind != "causal" else {"bias": self.cum_col(kt, head)}
                x = act(lambda e: e.activation(self.pf[s][:, c0:c1], flat(bank)[:, c0:c1], ACT.Exp, scale=SC, **bias),
                        p, *self.free(f"p{s}"))
                self.end[f"s_read{i % 2}"] = x
                h = act(lambda e: e.activation(self.ph[s][:, c0:c1], self.pf[s][:, c0:c1], ACT.Copy), x)
                self.end[f"split{s}"] = (h, c0, c1)

            def split(self, i):
                s = i % 3
                h, c0, c1 = self.end[f"split{s}"]
                self.end[f"p_made{s}"] = dve(lambda e: e.tensor_tensor(
                    self.pl[s][:, c0:c1], self.pf[s][:, c0:c1], self.ph[s][:, c0:c1].bitcast(F32), ALU.subtract), h)

            def values(self, i, b, vb, gr):
                s = i % 3
                waits = self.free(f"p_made{s}")
                if gr == 0:
                    waits += self.free("out_read", "sums_read", f"v_made{vb}")
                    if self.kind == "band":
                        for n in range(2):
                            for j, row in enumerate((self.sh[b], self.sl[b])):
                                p = pe(lambda e, n=n, row=row, j=j: e.matmul(ps[:, 6 + n, :], self.one_row[64:65, :],
                                                                             row[64:65, n * HT:(n + 1) * HT], start=(j == 0),
                                                                             stop=False, skip_group_check=True),
                                       *((waits + self.free(f"sink_made{b}")) if (n, j) == (0, 0) else ()), mark=(n == 1 and j == 1))
                        self.end[f"sink{b}"] = p
                todo = []
                for kt in self.group(gr):
                    q0, q1 = self.query_range(kt)
                    shift = (kt % 4) * 256 - kt * P if self.kind == "band" else 0
                    for n, c0, c1 in pieces(q0, q1):
                        first = kt == 0 and self.kind != "band"
                        for v, x, j in ((self.vh, self.ph, 0), (self.vl, self.ph, 1), (self.vh, self.pl, 2)):
                            todo.append((n, c0, c1, v[vb][:, kt, :], x[s][:, c0 + shift:c1 + shift], first and j == 0))
                for j, (n, c0, c1, v, x, start) in enumerate(todo):
                    end = j == len(todo) - 1
                    p = pe(lambda e, n=n, c0=c0, c1=c1, v=v, x=x, start=start, end=end: e.matmul(
                        ps[:, 6 + n, c0 - n * HT:c1 - n * HT], v, x, start=start, stop=end, skip_group_check=True),
                        *(waits if j == 0 else ()), mark=end)
                self.end[f"p{s}"] = p
                self.end[f"v{vb}"] = self.end["out"] = p

            def take(self, dst):
                l = act(lambda e: e.activation(self.rinv[:, :], flat(6)[64:P, :], ACT.Ln), self.end["out"], *self.free("rinv"))
                c = dve(lambda e: e.tensor_copy(dst(), flat(6)[0:64, :]), self.end["out"])
                self.end["sums_read"], self.end["out_read"] = l, c

            def divide(self, dst):
                l, c = self.free("sums_read", "out_read")
                r = act(lambda e: e.activation(self.rinv[:, :], self.rinv[:, :], ACT.Exp, scale=-1.0), l)
                self.end["rinv"] = dve(lambda e: e.tensor_tensor(dst(), dst(), self.rinv[:, :], ALU.mult), r, c)

            def run(self, prep_qk, prep_v, kv_of, dst):
                groups = len(range(0, KT, len(self.group(0))))
                steps = [(h, gr) for h in range(8) for gr in range(groups)]
                for part in range(3):
                    prep_qk(0, part)
                prep_v(0)
                units = self.units()
                for j, u in enumerate(units):
                    self.max_unit(0, kv_of(0)[0], kv_of(0)[1], u, 0, j == 0)
                self.max_columns(0, 0)
                self.max_rows(0, 0)
                self.scores(0, 0, kv_of(0)[0], 0, 0)
                self.split(0)
                ahead, pending = [], []

                def after(i):
                    h, gr = steps[i]
                    self.values(i, h % 2, kv_of(h)[0], gr)
                    if gr == groups - 1:
                        self.take(dst(h))
                        pending.append(dst(h))

                for part in range(3):
                    prep_qk(1, part)
                for i, (h, gr) in enumerate(steps):
                    last = gr == groups - 1
                    if gr == 0:
                        ahead = [(u, j == 0) for j, u in enumerate(units)]
                    if i and (last or gr == 0):
                        after(i - 1)
                    if i + 1 < len(steps):
                        h2, g2 = steps[i + 1]
                        self.scores(i + 1, h2 % 2, kv_of(h2)[0], g2, h2)
                    if h < 7 and not last and (gr or groups == 2):
                        for _ in range(-(-len(ahead) // (groups - 1 - gr))):
                            u, first = ahead.pop(0)
                            self.max_unit((h + 1) % 2, kv_of(h + 1)[0], kv_of(h + 1)[1], u, h + 1, first)
                        if not ahead:
                            self.max_columns((h + 1) % 2, h + 1)
                    if i + 1 < len(steps):
                        self.split(i + 1)
                    if pending:
                        self.divide(pending.pop(0))
                    if i and not (last or gr == 0):
                        after(i - 1)
                    if h < 7 and gr == groups - 2:
                        self.max_rows((h + 1) % 2, h + 1)
                    if last and h < 6:
                        prep_qk(h + 2, 0)
                    for part, at_step in ((1, 2), (2, 3)) if groups > 2 else ((1, 0), (2, 0)):
                        if 1 <= h < 7 and gr == at_step:
                            prep_qk(h + 1, part)
                    if gr == 0 and h < 7:
                        prep_v(h + 1)
                after(len(steps) - 1)
                self.divide(pending.pop(0))

        tables = Area(156, 164)
        cos1 = tables("cos1", [P, T], F32)
        sin1 = tables("sin1", [P, T], F32)
        c_rope = g.count("c_rope")
        sp(lambda e: e.dma_start(cos1[:, :], a["rope"][0]), *ada_m.acc_done, *ada_m.acc_used, sem=c_rope, by=16)
        rope_in = sp(lambda e: e.dma_start(sin1[:, :], a["rope"][1]), sem=c_rope, by=16)
        for q in (act, dve, pool):
            q.wait(g.last(pe))
        dve.wait(*prev_evac)
        prep = Area(0, 64)
        q_sq = prep("q_sq", [P, 5, T], F32)
        q_rstd = prep("q_rstd", [P, 5, T], F32)
        q_normed = [prep(f"q_normed{s}", [P, T], F32) for s in range(2)]
        q_swap = [prep(f"q_swap{s}", [P, T], F32) for s in range(2)]
        swap16 = [(i + 16) % 32 for i in range(32)]
        gq = SMALL["qk_g"][0]
        exp_tables()
        bank_free, rstd_made, squares = [None, None], [], []
        for t in range(5):
            squares.append(act(lambda e, t=t: e.activation(q_sq[:, t, :], y[:, QA + t, :], ACT.Square)))
        for t in range(5):
            bank = 4 + 2 * (t % 2)
            for n in range(2):
                p = pe(lambda e, n=n, t=t, bank=bank: e.matmul(ps[:, bank + n, :], pair_ones[:, :],
                                                               q_sq[:, t, n * HT:(n + 1) * HT], start=True, stop=True),
                       *([squares[t]] + ([bank_free[t % 2]] if bank_free[t % 2] else []) if n == 0 else []), mark=(n == 1))
            p = bank_free[t % 2] = act(lambda e, t=t, bank=bank: e.activation(q_rstd[:, t, :], flat(bank), ACT.Ln, bias=col("eps"),
                                                                            scale=1.0 / 64), p)
            rstd_made.append(act(lambda e, t=t: e.activation(q_rstd[:, t, :], q_rstd[:, t, :], ACT.Exp, scale=-0.5), p))
        last_use = [None, None]
        for t in range(5):
            s = t % 2
            had = [last_use[s]] if last_use[s] else []
            u = dve(lambda e, t=t, s=s: e.scalar_tensor_tensor(q_normed[s][:, :], y[:, QA + t, :], small[:, gq + t:gq + t + 1],
                                                               q_rstd[:, t, :], ALU.mult, ALU.mult), rstd_made[t], *had)
            v = dve(lambda e, s=s: e.stream_shuffle(q_swap[s][:, :], q_normed[s][:, :], swap16), u)
            c = pool(lambda e, s=s: e.tensor_tensor(q_normed[s][:, :], q_normed[s][:, :], cos1[:, :], ALU.mult), v, rope_in)
            v = dve(lambda e, s=s: e.tensor_tensor(q_swap[s][:, :], q_swap[s][:, :], sin1[:, :], ALU.mult), v, rope_in)
            if t:
                last_use[1 - s] = rotated = dve(add_last, *add_waits)

            def add_last(e, t=t, s=s):
                return e.tensor_tensor(y[:, QA + t, :], q_normed[s][:, :], q_swap[s][:, :], ALU.add)
            add_waits = (v, c)
        rotated = dve(add_last, *add_waits)

        g.meet(act, dve, pool, pe)
        low_area, high_area = Area(0, 64), Area(156, 174)
        high_area.at += 12 * K1
        maxima1 = ([high_area(f"mx1_{s}", [P, KT], F32) for s in range(2)], [high_area(f"mh1_{s}", [P, 2, KT], F32) for s in range(2)])
        high_area.at -= high_area.at - 156 * K1
        full = Attention("full", low_area, high_area, maxima1, low_area("rinv1", [64, T], F32))

        def qrow(h):
            return lambda: y[64 * (h % 2):64 * (h % 2) + 64, QA + h // 2, :]

        for kv in range(2):
            full.prep_v(kv, kv, lambda kv=kv: y[64 * kv:64 * kv + 64, VA, :])
            full.prep_k(kv, kv, lambda kv=kv: y[64 * kv:64 * kv + 64, KA, :], waits=[rotated])
        full.run(lambda h, part: full.prep_q(h % 2, h % 2, qrow(h), part), lambda h: None, lambda h: (h // 4, h // 4), qrow)
        g.meet()
        low, high = Area(0, 64), Area(156, 174)
        e_buf = [low(f"m_e{s}", [P, T], F32) for s in range(3)]
        wl = [Area(4 * s, 4 * s + 4)(f"m_wl{s}", [P, T], F32R) for s in range(3)]
        wh = [low(f"m_wh{s}", [P, T], F32R) for s in range(3)]
        qh = [low(f"m_qh{s}", [P, T], F32R) for s in range(2)]
        kh = [low(f"m_kh{s}", [P, T], F32R) for s in range(2)]
        vh = [low(f"m_vh{s}", [P, KT, P], F32R) for s in range(2)]
        m_stack = low("m_stack", [P, T], F32R)
        nm_stack = low("nm_stack", [P, T], F32R)
        sel = low("sel", [P, 8, P], F32R)
        nb = low("m_nb", [P, T], F32)
        mb = [high(f"m_mb{s}", [P, T], F32) for s in range(2)]
        hs = [high(f"m_hs{s}", [P, T], F32) for s in range(2)]
        a_cols = high("a_cols", [P, KT, 64], F32)
        ones_r = fixed("ones_r", [P, P], F32R)
        den = nc.alloc_sbuf_tensor_at("m_den", [P, HT], F32, offset=xp_at)
        num = nc.alloc_sbuf_tensor_at("m_num", [P, HT], F32, offset=xp_at + 2048)
        yr = Area(64, 156)("y_r", [P, N_IN1, T], F32R)
        gt = Area(0, 64)
        f_pre, f_log, b_cum, a_gate, m_max, i_pre, zeros, n_max, sel_raw = (
            gt(f"g_{n}", [64, T] if n != "sel_raw" else [P, T], F32)
            for n in ("f_pre", "f_log", "b_cum", "a_gate", "m_max", "i_pre", "zeros", "n_max", "sel_raw"))

        c_sel = g.count("c_sel")
        sel_in = sp(lambda e: e.dma_start(sel_raw[:, :], a["sel"].rearrange("p k c -> p (k c)")), sem=c_sel, by=16)
        gb = col("gate_b")
        p = act(lambda e: e.activation(f_pre[:, :], y[64:P, GA, :], ACT.Identity, bias=gb[64:P, :]))
        q = act(lambda e: e.activation(i_pre[:, :], y[0:64, GA, :], ACT.Identity, bias=gb[0:64, :]))
        z = dve(lambda e: e.memset(zeros[:, :], 0.0))
        p1 = act(lambda e: e.activation(f_log[:, :], f_pre[:, :], ACT.Abs), p)
        p1 = act(lambda e: e.activation(f_log[:, :], f_log[:, :], ACT.Exp, scale=-1.0), p1)
        p1 = act(lambda e: e.activation(f_log[:, :], f_log[:, :], ACT.Ln, bias=col("one")[0:64, :]), p1)
        p = dve(lambda e: e.scalar_tensor_tensor(f_log[:, :], f_pre[:, :], 0.0, f_log[:, :], ALU.min, ALU.subtract), p1, z)
        both = ((slice(0, 32), slice(None, None, 1)), (slice(32, 64), slice(None, None, -1)))

        def scan(out, d0, d1, op0, op1, *waits):
            for r, o in both:
                x = dve(lambda e, r=r, o=o: e.tensor_tensor_scan(out[r, o], d0[r, o], d1[r, o], 0.0, op0, op1), *waits)
            return x

        p = scan(b_cum, f_log, zeros, ALU.add, ALU.add, p)
        p = dve(lambda e: e.tensor_tensor(a_gate[:, :], i_pre[:, :], b_cum[:, :], ALU.subtract), p, q)
        a_done = p
        p = scan(m_max, a_gate, a_gate, ALU.max, ALU.max, p)
        m_done = p
        p = dve(lambda e: e.scalar_tensor_tensor(n_max[:, :], b_cum[:, :], -1.0, m_max[:, :], ALU.mult, ALU.subtract), p)
        stacked = []
        for src, dst, ready in ((m_max, m_stack, m_done), (n_max, nm_stack, p)):
            x = act(lambda e, src=src, dst=dst: e.activation(dst[0:64, :], src[:, :], ACT.Copy), ready)
            stacked.append(dve(lambda e, src=src, dst=dst: e.tensor_tensor(dst[64:P, :], src[:, :], dst[0:64, :].bitcast(F32),
                                                                         ALU.subtract), x))
        for kt in range(KT):
            p = pe(lambda e, kt=kt: e.transpose(ps[:, 4, kt * 64:(kt + 1) * 64], a_gate[:, kt * P:(kt + 1) * P],
                                              ident[0:64, 0:64]), *([a_done] if kt == 0 else []), mark=(kt == KT - 1))
        p = act(lambda e: e.activation(a_cols[:, :, :].rearrange("p a b -> p (a b)"), ps[:, 4, :], ACT.Copy), p)
        p = act(lambda e: e.activation(sel[:, :, :].rearrange("p a b -> p (a b)"), sel_raw[:, :], ACT.Copy), sel_in)
        p = act(lambda e: e.activation(ones_r[:, :], ones[:, :], ACT.Copy))
        g.meet()

        ring = {"n": 0, "read": [None, None]}
        m_end = {}

        def m_free(*names):
            return [m_end[n] for n in names if m_end.get(n)]

        jobs, now = {}, [0]

        def later(k, fn):
            jobs.setdefault(now[0] + k, []).append(fn)

        def next_banks():
            s = ring["n"] % 2
            ring["n"] += 1
            return s, 2 * s, [x for x in [ring["read"][s]] if x]

        def m_prep(h, part):
            b = h % 2
            if part < 2:
                src, hi = ((QM + h, qh), (QM + 4 + h, kh))[part]
                x = act(lambda e: e.activation(hi[b][:, :], y[:, src, :], ACT.Copy), *m_free(f"heads{b}"))

                def low_part():
                    m_end[f"prep{b}"] = dve(lambda e: e.tensor_tensor(yr[:, src, :], y[:, src, :], hi[b][:, :].bitcast(F32),
                                                                      ALU.subtract), x)
                return later(1, low_part)
            s, bank, waits = next_banks()
            for k in range(KT):
                t = pe(lambda e, k=k: e.transpose(ps[:, bank + k // 4, (k % 4) * P:(k % 4 + 1) * P],
                                                y[:, VM + h, k * P:(k + 1) * P], ident[:, :]), *(waits if k == 0 else []), mark=(k == 7))
            x = act(lambda e: e.activation(vh[b][:, :, :].rearrange("p a b -> p (a b)"), flat(bank), ACT.Copy), t, *m_free(f"heads{b}"))
            x = dve(lambda e: e.tensor_tensor(yr[:, VM + h, :], flat(bank), vh[b][:, :, :].rearrange("p a b -> p (a b)").bitcast(F32),
                                              ALU.subtract), x)
            m_end[f"v_prep{b}"] = ring["read"][s] = x

        def m_rows(h, d, which):
            k, u = d * 4 + h, (2 * h + d) % 2
            for stack, dst, name in (((m_stack, mb[u], f"mb{u}"), (nm_stack, nb, "nb"))[which],):
                s, bank, waits = next_banks()
                for n in range(2):
                    t = pe(lambda e, n=n, bank=bank, stack=stack: e.matmul(ps[:, bank + n, :], sel[:, k, :],
                                                                          stack[:, n * HT:(n + 1) * HT], start=True, stop=True),
                           *(waits if n == 0 else []), mark=(n == 1))
                x = act(lambda e, bank=bank, dst=dst: e.activation(dst[:, :], flat(bank), ACT.Copy), t, *m_free(name))
                ring["read"][s] = m_end[name + "_made"] = x

        def span(d, kt):
            return (kt * P, T) if d == 0 else (0, (kt + 1) * P)

        def m_decay(i):
            h, d, kt = steps[i]
            s3, u = i % 3, (2 * h + d) % 2
            q0, q1 = span(d, kt)
            keys = slice(kt * P, (kt + 1) * P)
            waits = m_free(f"mb{u}_made", f"w{s3}")
            sign = 1 if d == 0 else -1
            masked = pool(lambda e: e.affine_select(out=e_buf[s3][:, keys], in_=mb[u][:, keys], pattern=[[sign, P]],
                                                    compare_op=ALU.is_ge, fill=-NEG, base=0, channel_multiplier=-sign), *waits)
            r0, r1 = (q0 + P, q1) if d == 0 else (q0, q1 - P)
            bias = a_cols[:, kt, 32 * d + h:32 * d + h + 1]
            if r1 > r0:
                act(lambda e: e.activation(e_buf[s3][:, r0:r1], mb[u][:, r0:r1], ACT.Exp, scale=-1.0, bias=bias), *waits)
            x = act(lambda e: e.activation(e_buf[s3][:, keys], e_buf[s3][:, keys], ACT.Exp, scale=-1.0, bias=bias), masked)
            m_end[f"mb{u}"] = m_end[f"e{s3}"] = x

        def m_weights(i):
            h, d, kt = steps[i]
            b, s3 = h % 2, i % 3
            q0, q1 = span(d, kt)
            s, bank, waits = next_banks()
            keys = slice(kt * P, (kt + 1) * P)
            waits = waits + m_free(f"prep{b}")
            pcs = pieces(q0, q1)
            for j, (n, c0, c1) in enumerate(pcs):
                for m, (x, z) in enumerate(((kh[b][:, keys], lambda c0, c1: qh[b][:, c0:c1]),
                                            (yr[:, QM + 4 + h, keys], lambda c0, c1: qh[b][:, c0:c1]),
                                            (kh[b][:, keys], lambda c0, c1: yr[:, QM + h, c0:c1]))):
                    p = pe(lambda e, n=n, c0=c0, c1=c1, x=x, z=z, m=m: e.matmul(
                        ps[:, bank + n, c0 - n * HT:c1 - n * HT], x, z(c0, c1), start=(m == 0), stop=(m == 2),
                        skip_group_check=True), *(waits if (j, m) == (0, 0) else ()), mark=(j == len(pcs) - 1 and m == 2))
            x = dve(lambda e: e.scalar_tensor_tensor(e_buf[s3][:, q0:q1], flat(bank)[:, q0:q1], KSC, e_buf[s3][:, q0:q1],
                                                     ALU.mult, ALU.mult), *m_free(f"e{s3}"), p)
            ring["read"][s] = x
            m_end[f"wh{s3}"] = act(lambda e: e.activation(wh[s3][:, q0:q1], e_buf[s3][:, q0:q1], ACT.Copy), x)

        def m_split(i):
            h, d, kt = steps[i]
            s3 = i % 3
            q0, q1 = span(d, kt)
            m_end[f"w_made{s3}"] = dve(lambda e: e.tensor_tensor(
                wl[s3][:, q0:q1], e_buf[s3][:, q0:q1], wh[s3][:, q0:q1].bitcast(F32), ALU.subtract), *m_free(f"wh{s3}"))

        def m_sums(i):
            h, d, kt = steps[i]
            b, s3 = h % 2, i % 3
            q0, q1 = span(d, kt)
            first = kt == (0 if d == 0 else KT - 1)
            pcs = pieces(q0, q1)
            if d == 0:
                pcs = pcs[::-1]
            waits, done = m_free(f"w_made{s3}", f"v_prep{b}"), []
            for n, c0, c1 in pcs:
                last = (kt == (3 if n == 0 else 7)) if d == 0 else (kt == (4 if n == 1 else 0))
                o = slice(c0 - n * HT, c1 - n * HT)
                wt = waits + (m_free(f"num_read{n}", f"den_read{n}") if first else [])
                keys = slice(kt * P, (kt + 1) * P)
                for j, (base, v, x) in enumerate(((6, vh[b][:, kt, :], wh), (6, yr[:, VM + h, keys], wh), (6, vh[b][:, kt, :], wl),
                                                  (4, ones_r[:, :], wh), (4, ones_r[:, :], wl))):
                    p = pe(lambda e, j=j, base=base, v=v, x=x, n=n, o=o, c0=c0, c1=c1, last=last: e.matmul(
                        ps[:, base + n, o], v, x[s3][:, c0:c1], start=(first and j in (0, 3)), stop=(last and j in (2, 4)),
                        skip_group_check=True), *(wt if j == 0 else ()), mark=(j == 4))
                waits = []
                if last:
                    done.append((h, d, n, p))
            m_end[f"w{s3}"] = p
            if kt == 0 and d == 1:
                m_end[f"heads{b}"] = p
            return done

        def m_finish(h, d, n, done):
            ts = slice(n * HT, (n + 1) * HT)
            sums = hs[h % 2]
            to = sums[:, ts] if d == 0 else num[:, :]
            m_end[f"num_read{n}"] = m_end["num"] = dve(lambda e: e.tensor_copy(to, ps[:, 6 + n, :]), done,
                                                       *m_free(f"hs{h % 2}" if d == 0 else "summed"))
            x = m_end[f"den_read{n}"] = act(lambda e: e.activation(den[:, :], ps[:, 4 + n, :], ACT.Abs), done, *m_free("den"))
            m_end["log"] = act(lambda e: e.activation(den[:, :], den[:, :], ACT.Ln, bias=col("tiny")), x)

            def largest():
                m_end["nb"] = dve(lambda e: e.tensor_tensor(den[:, :], den[:, :], nb[:, ts], ALU.max), *m_free("log", "nb_made"))
                if (d, n) in ((0, 1), (1, 0)) and (h, d) != (3, 1):
                    m_rows(h + d, 1 - d, 1)

            def inverse():
                m_end["inverse"] = act(lambda e: e.activation(den[:, :], den[:, :], ACT.Exp, scale=-1.0), *m_free("nb"))

            def multiply():
                x = m_end["den"] = dve(lambda e: e.tensor_tensor(to, to, den[:, :], ALU.mult), *m_free("inverse", "num"))
                if d == 1:
                    m_end["summed"] = m_end[f"sum{n}"] = dve(lambda e: e.tensor_tensor(sums[:, ts], sums[:, ts], num[:, :], ALU.add), x)
                if (d, n) == (1, 0):
                    for part in range(4):
                        later(part + 1, lambda part=part: m_output(h, part))

            later(1, largest)
            later(2, inverse)
            later(3, multiply)

        def m_output(h, part):
            out_h = y[:, QM + h, :]
            if part == 0:
                m_end["sq"] = act(lambda e: e.activation(out_h, hs[h % 2][:, :], ACT.Square), *m_free("sum0", "sum1", f"heads{h % 2}"))
            elif part == 1:
                s, bank, waits = next_banks()
                for n in range(2):
                    t = pe(lambda e, n=n: e.matmul(ps[:, bank + n, :], ones[:, :], y[:, QM + h, n * HT:(n + 1) * HT], start=True, stop=True),
                           *((waits + m_free("sq")) if n == 0 else []), mark=(n == 1))
                x = ring["read"][s] = act(lambda e: e.activation(out_h, flat(bank), ACT.Ln, bias=col("eps"), scale=1.0 / P), t)
                m_end["rstd"] = act(lambda e: e.activation(out_h, out_h, ACT.Exp, scale=-0.5), x)
            elif part == 2:
                m_end[f"hs{h % 2}"] = dve(lambda e: e.scalar_tensor_tensor(out_h, out_h, col("mlstm_norm_g", h), hs[h % 2][:, :],
                                                                           ALU.mult, ALU.mult), *m_free("rstd"))
            else:
                dve(lambda e: e.tensor_tensor(out_h, out_h, y[:, OM + h, :], ALU.mult), *m_free(f"hs{h % 2}"))

        steps = [(h, d, kt) for h in range(4) for d in range(2) for kt in (range(KT) if d == 0 else range(KT)[::-1])]
        def run_jobs():
            for fn in jobs.pop(now[0], []):
                fn()
            now[0] += 1

        for part in range(3):
            m_prep(0, part)
        m_rows(0, 0, 0)
        m_rows(0, 0, 1)
        run_jobs()
        run_jobs()
        m_decay(0)
        m_decay(1)
        m_weights(0)

        for i, (h, d, kt) in enumerate(steps):
            if i + 1 < len(steps):
                m_weights(i + 1)
            m_split(i)
            if i:
                for x in m_sums(i - 1):
                    m_finish(*x)
            if i + 2 < len(steps):
                h2, d2, _ = steps[i + 2]
                if (h2, d2) != steps[i + 1][:2]:
                    m_rows(h2, d2, 0)
                m_decay(i + 2)
            if d == 1 and h < 3 and kt in (6, 5, 4):
                m_prep(h + 1, 6 - kt)
            run_jobs()
        for x in m_sums(len(steps) - 1):
            m_finish(*x)
        while jobs:
            run_jobs()
        g.meet()
        x1_dram = nc.dram_tensor("x1_scratch", (2, KT, P, HT), F32, kind="Internal").ap()
        xb_dram = nc.dram_tensor("xb_scratch", (2, P, KT, HT), F32, kind="Internal").ap()
        x1 = Area(120, 152)("x1", [P, 2, KT, HT], F32)
        mix = Area(0, 64)
        mix_hi = mix("mix_hi", [P, KT, T], F32R)
        mix_lo = mix("mix_lo", [P, KT, T], F32R)
        again = Area(156, 174)
        x_again = [again(f"x_again{s}", [P, T], F32) for s in range(2)]
        sq1 = [again(f"sq1_{s}", [P, HT], F32) for s in range(2)]
        acc1 = [nc.alloc_sbuf_tensor_at(f"acc1_{s}", [P, HT], F32, offset=xp_at + s * 2048) for s in range(2)]
        rs = [nc.alloc_sbuf_tensor_at(f"rs_{s}", [P, HT], F32, offset=BASE + 152 * K1 + s * 2048) for s in range(2)]

        mix_made = {}
        for k in range(KT):
            src = (QA + k) if k < 4 else (QM + k - 4)
            x = act(lambda e, k=k, src=src: e.activation(mix_hi[:, k, :], y[:, src, :], ACT.Copy))
            mix_made[k] = dve(lambda e, k=k, src=src: e.tensor_tensor(mix_lo[:, k, :], y[:, src, :], mix_hi[:, k, :].bitcast(F32),
                                                                      ALU.subtract), x)
        zero = dve(lambda e: e.memset(acc1[0][:, :], 0.0))
        acc_at = [zero, dve(lambda e: e.memset(acc1[1][:, :], 0.0))]
        x_landed = [g.count(f"x_again_landed{s}") for s in range(2)]
        x_used, banks_read, sq_read = [None, None], [None, None], [None, None]
        for pair in range(4):
            def w_out_tile(j, slot, ready, used, pair=pair):
                m, s, bank = 2 * pair + j, j, 2 * j
                lx = sp(lambda e: e.dma_start(x_again[s][:, :], a["x"][m]), *([x_used[s]] if x_used[s] else []),
                        sem=x_landed[s], by=16)
                mov = [(lambda k, n=n: mix_hi[:, k, n * HT:(n + 1) * HT], lambda k, n=n: mix_lo[:, k, n * HT:(n + 1) * HT])
                       for n in range(2)]
                product(g, w, slot, [ps[:, bank + n, :] for n in range(2)], mov, 0, KT, True, True,
                        [ready] + ([banks_read[s]] if banks_read[s] else []), used, mix_made if m == 0 else None)
                for n in range(2):
                    x = dve(lambda e, n=n: e.scalar_tensor_tensor(x1[:, n, m, :], ps[:, bank + n, :], mod1[:, 16 + m:17 + m],
                                                                 x_again[s][:, n * HT:(n + 1) * HT], ALU.mult, ALU.add), used, lx)
                    q = act(lambda e, n=n: e.activation(sq1[n][:, :], x1[:, n, m, :], ACT.Square), x,
                            *([sq_read[n]] if sq_read[n] else []))
                    acc_at[n] = sq_read[n] = dve(lambda e, n=n: e.tensor_tensor(acc1[n][:, :], acc1[n][:, :], sq1[n][:, :], ALU.add),
                                                 q, acc_at[n])
                x_used[s] = banks_read[s] = x
            w.run(2, None, w_out_tile)
        c_x1 = g.count("c_x1_kept")
        for n in range(2):
            x1_kept = sp(lambda e, n=n: e.dma_start(x1_dram[n].rearrange("k p t -> p k t"), x1[:, n, :, :]), x_used[1], sem=c_x1, by=16)

        norm_hl = [Area(32 * n, 32 * n + 32) for n in range(2)]
        h2_hi = [norm_hl[n](f"h2_hi{n}", [P, KT, HT], F32R) for n in range(2)]
        h2_lo = [norm_hl[n](f"h2_lo{n}", [P, KT, HT], F32R) for n in range(2)]
        hid = Area(64, 152)
        hid_hi = hid("hid_hi", [P, FT, HT], F32R)
        hid_lo = hid("hid_lo", [P, FT, HT], F32R)
        x2 = Area(152, 168)("x2", [P, KT, HT], F32)
        tail = Area(168, 174)
        gated = tail("gated", [P, HT], F32)
        x1c = [tail(f"x1c{s}", [P, HT], F32) for s in range(2)]
        sf_done = scale_col(s_ffn, "norm_ffn_g", 32, mod1)

        def normed(src, bank, acc, r, acc_ready, scale, shift, hi, lo, tt, made):
            state = {"free": [None, None]}

            def start():
                state["r"] = inverse_norm(acc, bank, r, acc_ready())

            def tile(k):
                s = k % 2
                f = state["free"]
                t1 = dve(lambda e: e.tensor_tensor(tt[s][:, :], src(k), r[:, :], ALU.mult), state["r"], *([f[s]] if f[s] else []))
                t2 = act(lambda e: e.activation(tt[s][:, :], tt[s][:, :], ACT.Identity, bias=shift(k), scale=scale(k)), t1)
                t3 = act(lambda e: e.activation(hi(k), tt[s][:, :], ACT.Copy), t2)
                f[s] = made[k] = dve(lambda e: e.tensor_tensor(lo(k), tt[s][:, :], hi(k).bitcast(F32), ALU.subtract), t3)

            return [start] + [lambda k=k: tile(k) for k in range(KT)]

        h2_made = [{}, {}]
        both_acc = list(acc_at)

        def ffn_norm(n):
            tt2 = [x1c[0], x1c[1]]
            return normed(lambda k: x1[:, n, k, :], 6, acc1[n], rs[n], lambda: both_acc[n], lambda k: s_ffn[:, k:k + 1],
                          lambda k: mod1[:, 24 + k:25 + k], lambda k: h2_hi[n][:, k, :], lambda k: h2_lo[n][:, k, :], tt2, h2_made[n])

        g.meet(act, dve)
        for step in ffn_norm(0):
            step()
        gated_read = {"p": None}
        bank_pts = {}

        def gate_up(n, turns, extras, loop):
            def tile(j, slot, ready, used, lp, turn):
                bank = j
                first = turn == 0 and j == 0
                mov = [(lambda k: h2_hi[n][:, k, :], lambda k: h2_lo[n][:, k, :])]
                waits = [ready]
                if lp is not None:
                    waits.append((evac[j // 2], 1))
                elif bank_pts.get(j // 2):
                    waits.append(bank_pts[j // 2])
                product(g, w, slot, [ps[:, bank, :]], mov, 0, KT, True, True, waits, used,
                        h2_made[n] if first else None)
                for _ in range(2):
                    if lp is None and extras:
                        extras.pop(0)()
                if j % 2 == 0:
                    silu_waits[0] = used
                    return
                m = (lambda: lp.i * 2 + (2 * turn0 + j // 2)) if lp is not None else (lambda: 2 * turn + j // 2)
                half = j // 2
                x = act(lambda e: e.activation(gated[:, :], ps[:, bank - 1, :], ACT.Silu), silu_waits[0],
                        *([gated_read["p"]] if gated_read["p"] else []))
                x = dve(lambda e: e.tensor_tensor(gated[:, :], gated[:, :], ps[:, bank, :], ALU.mult), x, used,
                        point=evac[half] if lp is not None else None)
                bank_pts[half] = x
                x = act(lambda e: e.activation(hid_hi[:, m(), :], gated[:, :], ACT.Copy), x)
                gated_read["p"] = dve(lambda e: e.tensor_tensor(hid_lo[:, m(), :], gated[:, :], hid_hi[:, m(), :].bitcast(F32),
                                                                ALU.subtract), x, point=made if (lp is not None and half == 1) else None)

            evac, made = [Point(), Point()], Point()
            silu_waits = [None]
            for turn in range(turns):
                w.run(4, None, lambda j, slot, ready, used, turn=turn: tile(j, slot, ready, used, None, turn))
            while extras:
                extras.pop(0)()
            turn0 = turns
            w.enter()
            act.wait(x1_kept)
            dve.wait(x1_kept)
            pe.wait(bank_pts[1])
            act.wait(gated_read["p"])
            gated_read["p"] = None
            with g.loop(FT // 2 - turns) as lp:
                gated_read["p"] = (made, 1)
                w.run(4, lp, lambda j, slot, ready, used: tile(j, slot, ready, used, lp, turns))
            gated_read["p"] = made
            before = Point()
            before.count, before.loops = made.count, []
            before.first = made.first + (lp.n - 2) * lp.step[made.count]
            gated_read["before"] = before

        def down(n, then):
            lhs = {"evac": [None, None], "x1": [Point(), Point()], "sq": None}
            landed = c_x1c
            acc_z = dve(lambda e: e.memset(acc1[n][:, :], 0.0), h2_made[n][KT - 1], *([h3_made[0][KT - 1]] if n else []))
            start_waits = gated_read["p"]

            def tile(j, slot, ready, used, lp, turn):
                s, part = j // 3, j % 3
                nk = 8 if part < 2 else FT - 16
                waits = [ready]
                if part == 0:
                    if lp is not None:
                        waits.append((evac[s], 1))
                    elif lhs["evac"][s]:
                        waits.append(lhs["evac"][s])
                if part == 2 and s == 0:
                    waits.append(start_waits)
                mov = [(lambda k: hid_hi[:, k, :], lambda k: hid_lo[:, k, :])]
                product(g, w, slot, [ps[:, 4 + s, :]], mov, 8 * part, nk, part == 0, part == 2, waits, used)
                if part == 0:
                    x_wait = [(evac[s], 1)] if lp is not None else [x for x in [lhs["evac"][s]] if x]
                    m_ = m_of(lp, s)
                    lhs["lx"] = sp(lambda e: e.dma_start(x1c[s][:, :], x1_dram[n, m_()]), *x_wait, sem=landed[s], by=16)
                if part == 2:
                    m_ = m_of(lp, s)
                    lx = lhs["lx"]
                    x = dve(lambda e: e.scalar_tensor_tensor(x2[:, m_(), :], ps[:, 4 + s, :], mod1[:, bass.ds(m_() + 40, 1)],
                                                             x1c[s][:, :], ALU.mult, ALU.add), used, lx,
                            point=evac[s] if lp is not None else None)
                    lhs["evac"][s] = x
                    q = act(lambda e: e.activation(gated[:, :], x2[:, m_(), :], ACT.Square), x,
                            *([(sq_done, 1) if (s == 0) else lhs["sq"]] if lp is not None else [y_ for y_ in [lhs["sq"]] if y_]))
                    lhs["sq"] = dve(lambda e: e.tensor_tensor(acc1[n][:, :], acc1[n][:, :], gated[:, :], ALU.add), q, *dq,
                                    point=sq_done if (lp is not None and s == 1) else None)

            evac, sq_done = [Point(), Point()], Point()
            dq = [acc_z]
            m_of = lambda lp, s: (lambda: lp.i * 2 + s) if lp is not None else (lambda: 6 + s)
            w.enter()
            sp.wait(x1_kept, g.last(act), acc_z)
            act.wait(acc_z)
            pe.wait(gated_read["before"])
            with g.loop(3) as lp:
                w.run(6, lp, lambda j, slot, ready, used: tile(j, slot, ready, used, lp, 0))
            lhs["evac"] = [evac[0], evac[1]]
            lhs["sq"] = sq_done
            w.run(6, None, lambda j, slot, ready, used: tile(j, slot, ready, used, None, 3), then=then)
            return lhs["sq"]

        h3_made = [{}, {}]
        c_x1c = [g.count(f"x1c_landed{s}") for s in range(2)]
        c_xb = g.count("c_xb")
        spp_done = scale_col(s_pre, "g_pre_2", 8, mod2)
        kept = {}

        def between(n, x2_done):
            st, rs2 = {}, acc1[1 - n]
            fg = SMALL["final_norm_g"][0]

            def a0():
                st["r"] = inverse_norm(acc1[n], 6, rs2, x2_done)
                st["z"] = dve(lambda e: e.memset(acc1[n][:, :], 0.0), st["r"])
                st["sq"] = [None, None]

            def a1(k):
                s = k % 2
                x = dve(lambda e: e.scalar_tensor_tensor(x2[:, k, :], x2[:, k, :], small[:, fg + k:fg + k + 1], rs2[:, :],
                                                         ALU.mult, ALU.mult), st["r"])
                q = act(lambda e: e.activation(x1c[s][:, :], x2[:, k, :], ACT.Square), x, *([st["sq"][s]] if st["sq"][s] else []))
                st["sq"][s] = st["acc"] = dve(lambda e: e.tensor_tensor(acc1[n][:, :], acc1[n][:, :], x1c[s][:, :], ALU.add), q, st["z"],
                                              *([st["acc"]] if "acc" in st else []))
                if k == KT - 1:
                    kept[n] = sp(lambda e: e.dma_start(xb_dram[n], x2[:, :, :]), x, sem=c_xb, by=16)

            def lazy():
                return st["acc"]

            return ([a0] + [lambda k=k: a1(k) for k in range(KT)] +
                    normed(lambda k: x2[:, k, :], 6, acc1[n], rs2, lazy, lambda k: s_pre[:, k:k + 1],
                           lambda k: mod2[:, k:k + 1], lambda k: h2_hi[n][:, k, :], lambda k: h2_lo[n][:, k, :], x1c, h3_made[n]))

        gate_up(0, 3, ffn_norm(1), True)
        x2_done = down(0, 31)
        gate_up(1, 5, between(0, x2_done), True)
        dve.wait(kept[0])
        x2_done = down(1, None)
        norm_steps = between(1, x2_done)
        y2 = Area(64, 172)("y2", [P, N_IN2, T], F32)
        h_hi_cur = lambda k, n: h2_hi[n][:, k, :]
        h_lo_cur = lambda k, n: h2_lo[n][:, k, :]
        z_dram = nc.dram_tensor("z_scratch", (P, 4, T), F32, kind="Internal").ap()
        c_z, c_pos, c_swap, c_back = (g.count(n) for n in ("c_z", "c_pos", "c_swap", "c_back"))
        halves = {"evac": [None, None]}

        def project_half(n, then, extras):
            def work(j, slot, ready, used):
                s = j % 2
                was = halves["evac"][s] or prev_evac[s]
                product(g, w, slot, [ps[:, s, :]], [(lambda k: h2_hi[n][:, k, :], lambda k: h2_lo[n][:, k, :])], 0, KT, True, True,
                        [ready] + ([was] if was else []), used, h3_made[n] if j == 0 else None)
                halves["evac"][s] = act(lambda e: e.activation(y2[:, SQ + j, n * HT:(n + 1) * HT], ps[:, s, :], ACT.Copy), used)
                for fn in extras[3 * j:3 * j + 3]:
                    fn()

            w.run(6, None, work, then=then)

        act.wait(g.last(pe))
        project_half(0, 99, norm_steps)
        project_half(1, None, [])
        pe.wait(*halves["evac"])
        act.wait(*kept.values())
        exp_tables()
        project(1, lambda m: y2[:, FG, :])

        gt2, ti2 = Area(64, 80), Area(172, 174)
        f_pre2, f_log2, cum2, zero2 = (gt2(f"f2_{n}", [8, T], F32) for n in ("pre", "log", "cum", "zero"))
        mx2 = [ti2(f"mx2_{s}", [P, KT], F32) for s in range(2)]
        mh2 = [ti2(f"mh2_{s}", [P, 2, KT], F32) for s in range(2)]
        cum_cols = ti2("cum_cols", [P, KT, 8], F32)
        sink8 = ti2("sink8", [P, 8], F32)
        sink_to = ti2("sink_to", [65, P], F32R)
        sel_raw2 = nc.alloc_sbuf_tensor_at("sel_raw2", [P, T], F32, offset=xp_at)
        cum_split = Area(168, 172)("cum_split", [P, T], F32R)
        sel_in2 = sp(lambda e: e.dma_start(sel_raw2[:, :], a["sel_f"].rearrange("p k c -> p (k c)")), g.last(pe), sem=c_pos, by=16)
        fb = col("b_fgate")
        fg_done = prev_evac[0]
        p = act(lambda e: e.activation(f_pre2[:, :], y2[0:8, FG, :], ACT.Identity, bias=fb[0:8, :]), fg_done)
        p = act(lambda e: e.activation(f_log2[:, :], f_pre2[:, :], ACT.Abs), p)
        p = act(lambda e: e.activation(f_log2[:, :], f_log2[:, :], ACT.Exp, scale=-1.0), p)
        p = act(lambda e: e.activation(f_log2[:, :], f_log2[:, :], ACT.Ln, bias=col("one")[0:8, :]), p)
        z = dve(lambda e: e.memset(zero2[:, :], 0.0))
        dve(lambda e: e.tensor_scalar(sink8[:, :], small[:, SMALL["sinks"][0]:SMALL["sinks"][0] + 8], 1 / SC, None, ALU.mult))
        p = dve(lambda e: e.scalar_tensor_tensor(f_log2[:, :], f_pre2[:, :], 0.0, f_log2[:, :], ALU.min, ALU.subtract), p)
        z2p = dve(lambda e: e.memset(cum_split[:, :].bitcast(F32), 0.0), p)
        p = dve(lambda e: e.tensor_tensor_scan(cum2[:, :], f_log2[:, :], zero2[:, :], 0.0, ALU.add, ALU.add), p, z)
        p = dve(lambda e: e.tensor_scalar(cum2[:, :], cum2[:, :], -1.0, None, ALU.mult), p)
        cum_done = p
        q = dve(lambda e: e.tensor_scalar(f_log2[:, :], cum2[:, :], 1 / SC, None, ALU.mult), p)
        sums_done = [q, z2p]

        act.wait(*[x for x in prev_evac if x])
        ro = Area(80, 112)
        cos2 = ro("cos2", [P, T], F32)
        sin2 = ro("sin2", [P, T], F32)
        swapped = ro("swapped", [P, 5, T], F32)
        at_turn = ro.at / K1
        turn2 = ro("turn2", [P, T], F32)
        pos_i = Area(at_turn, 112)("pos_i", [P, T], I32)
        for j in range(4):
            s0, d0 = 32 * j, 32 * (j ^ 1)
            swap_in = sp(lambda e, s0=s0, d0=d0: e.dma_start(swapped[d0:d0 + 32, :, :], y2[s0:s0 + 32, SQ:SQ + 5, :]),
                         *halves["evac"], sem=c_swap, by=16)
        pos_in = sp(lambda e: e.dma_start(pos_i[:, :], a["positions"].to_broadcast([P, T])), sel_in2, sem=c_pos, by=16)
        rj = {}

        def angle():
            ang, magic, rest = cos2, 1.5 * 2 ** 23, 2 * np.pi
            p = dve(lambda e: e.tensor_copy(ang[:, :], pos_i[:, :]), pos_in)
            p = dve(lambda e: e.tensor_scalar(ang[:, :], ang[:, :], col("inv_freq"), None, ALU.mult), p)
            p = dve(lambda e: e.tensor_scalar(turn2[:, :], ang[:, :], 1 / (2 * np.pi), magic, ALU.mult, ALU.add), p)
            p = dve(lambda e: e.tensor_scalar(turn2[:, :], turn2[:, :], magic, None, ALU.subtract), p)
            for bits in (5, 21, 40):
                c = float(np.round(rest * 2 ** bits) / 2 ** bits)
                rest -= c
                p = dve(lambda e, c=c: e.scalar_tensor_tensor(ang[:, :], turn2[:, :], -c, ang[:, :], ALU.mult, ALU.add), p)
            pi = float(np.float32(3.1415925))
            rj["p"] = dve(lambda e: e.tensor_scalar(ang[:, :], ang[:, :], pi, -pi, ALU.min, ALU.max), p)

        def sines():
            q = act(lambda e: e.activation(sin2[:, :], cos2[:, :], ACT.Sin), rj["p"])
            x = act(lambda e: e.activation(cos2[:, :], cos2[:, :], ACT.Abs), q)
            x = act(lambda e: e.activation(cos2[:, :], cos2[:, :], ACT.Sin, bias=col("half_pi"), scale=-1.0), x)
            rj["p"] = dve(lambda e: e.tensor_scalar(sin2[:, :], sin2[:, :], col("rope_sign"), None, ALU.mult), x)

        def rotate(t):
            p = dve(lambda e: e.tensor_tensor(swapped[:, t, :], swapped[:, t, :], sin2[:, :], ALU.mult), rj["p"], swap_in)
            p = dve(lambda e: e.tensor_tensor(y2[:, SQ + t, :], y2[:, SQ + t, :], cos2[:, :], ALU.mult), p)
            rj["p"] = dve(lambda e: e.tensor_tensor(y2[:, SQ + t, :], y2[:, SQ + t, :], swapped[:, t, :], ALU.add), p)

        z_dst = lambda m: y2[:, SZ + m, :]
        project(4, z_dst, func=ACT.Silu)
        act.wait(*prev_evac)
        z_kept = sp(lambda e: e.dma_start(z_dram, y2[:, SZ:SZ + 4, :]), *prev_evac, sem=c_z, by=16)
        h = act(lambda e: e.activation(cum_split[0:8, :], f_log2[:, :], ACT.Copy), *sums_done)
        split_done = dve(lambda e: e.tensor_tensor(cum_split[32:40, :], f_log2[:, :], cum_split[0:8, :].bitcast(F32), ALU.subtract), h)
        for kt in range(KT):
            t = pe(lambda e, kt=kt: e.transpose(ps[:, 4, kt * 8:(kt + 1) * 8], cum2[:, kt * P:(kt + 1) * P], ident[0:8, 0:8]),
                   *([cum_done] if kt == 0 else []), mark=(kt == KT - 1))
        cols_done = act(lambda e: e.activation(cum_cols[:, :, :].rearrange("p a b -> p (a b)"), ps[:, 4, 0:64], ACT.Copy), t)
        rope_jobs = [angle, sines] + [lambda t=t: rotate(t) for t in range(5)]

        def rope_job(j, lp):
            if rope_jobs:
                rope_jobs.pop(0)()

        project(4, lambda m: y2[:, FZ + m, :], func=ACT.Silu, rolled=False, extra=rope_job)
        act.wait(*prev_evac)
        act.wait(split_done, cols_done)
        project(4, lambda m: y2[:, m, :], rolled=False, extra=rope_job)
        act.wait(rj["p"], *prev_evac)
        project(8, lambda m: y2[:, 4 + m, :])
        exp_tables()
        g.meet()
        lo2, hi2 = Area(0, 64), Area(152, 168)
        rinv2 = nc.alloc_sbuf_tensor_at("rinv2", [64, T], F32, offset=xp_at)
        fox = Attention("causal", lo2, hi2, (mx2, mh2), rinv2)
        sel_f = lo2("sel_f", [P, 8, P], F32R)
        fox.cum_split = cum_split
        fox.sel = lambda head: sel_f[:, head, :]
        fox.cum_col = lambda kt, head: cum_cols[:, kt, head:head + 1]
        act(lambda e: e.activation(sel_f[:, :, :].rearrange("p k c -> p (k c)"), sel_raw2[:, :], ACT.Copy), sel_in2)
        for q in g.queues:
            q.wait(z_kept)
        g.meet()

        def row2(tile, h):
            return lambda: y2[64 * (h % 2):64 * (h % 2) + 64, tile + h // 2, :]

        def fox_prep(h, part):
            fox.prep_q(h % 2, h % 2, row2(FQ, h), part)
            fox.prep_k(h % 2, h % 2, row2(FK, h), part)

        fox.run(fox_prep, lambda h: fox.prep_v(h % 2, h % 2, row2(FV, h)), lambda h: (h % 2, h % 2), lambda h: row2(FQ, h))
        g.meet()

        band = fox
        band.kind = "band"
        bd = Area(80, 96)
        band.sf = bd("sink_f", [65, T], F32)
        band.sh = [bd(f"sink_h{s}", [65, T], F32R) for s in range(2)]
        band.sl = [bd("sink_l0", [65, T], F32R), Area(168, 172)("sink_l1", [65, T], F32R)]
        band.one_row = sink_to
        p = pool(lambda e: e.memset(band.one_row[64:65, 0:64].bitcast(F32), 0.0))
        p = pool(lambda e: e.memset(band.one_row[64:65, 64:P].bitcast(F32), 1.0), p)
        pe.wait(p)
        z2 = Area(96, 112)("z2", [P, 4, T], F32)
        z_back = sp(lambda e: e.dma_start(z2[:, :, :], z_dram), z_kept, sem=c_back, by=16)
        band.sink_raw = lambda head: sink8[:, head:head + 1]
        band.sink = lambda head: col("sinks", head)[64:65, :]
        for kv in range(2):
            band.prep_k(kv, kv, lambda kv=kv: y2[64 * kv:64 * kv + 64, SK, :])
            band.prep_v(kv, kv, lambda kv=kv: y2[64 * kv:64 * kv + 64, SV, :])
        band.run(lambda h, part: band.prep_q(h % 2, h % 2, row2(SQ, h), part), lambda h: None, lambda h: (h // 4, h // 4),
                 lambda h: row2(SQ, h))
        g.meet()

        m2 = Area(0, 64)
        mix2_hi = m2("mix2_hi", [P, KT, T], F32R)
        mix2_lo = m2("mix2_lo", [P, KT, T], F32R)
        made2 = {}
        def gate_tile(k):
            src = (FQ + k) if k < 4 else (SQ + k - 4)
            x = dve(lambda e: e.tensor_tensor(y2[:, src, :], y2[:, src, :], y2[:, FZ + k, :] if k < 4 else z2[:, k - 4, :],
                                              ALU.mult), z_back)
            return src, act(lambda e: e.activation(mix2_hi[:, k, :], y2[:, src, :], ACT.Copy), x)

        gated_tiles = [gate_tile(0)]
        for k in range(KT):
            if k + 1 < KT:
                gated_tiles.append(gate_tile(k + 1))
            src, x = gated_tiles[k]
            made2[k] = dve(lambda e, k=k, src=src: e.tensor_tensor(mix2_lo[:, k, :], y2[:, src, :], mix2_hi[:, k, :].bitcast(F32),
                                                                   ALU.subtract), x)
        yo = Area(64, 96)("y_out", [P, 2, KT, HT], F32)
        xb = Area(112, 144)("xb", [P, 2, KT, HT], F32)
        end2 = Area(144, 164)
        sq3 = [end2(f"sq3_{s}", [P, HT], F32) for s in range(2)]
        acc3 = [end2(f"acc3_{s}", [P, HT], F32) for s in range(2)]
        rs3 = [end2(f"rs3_{s}", [P, HT], F32) for s in range(2)]
        c_xback, c_out = [g.count("c_xback0"), g.count("c_xback1")], [g.count("c_out0"), g.count("c_out1")]
        xb_in = {}

        def load_xb(piece):
            n, k0 = piece // 4, 2 * (piece % 4)
            xb_in["p"] = sp(lambda e: e.dma_start(xb[:, n, k0:k0 + 2, :], xb_dram[n][:, k0:k0 + 2, :]), made2[KT - 1],
                            *kept.values(), sem=c_xback[n], by=16)
            xb_in[n] = xb_in["p"]

        sp_done = dve(lambda e: e.tensor_tensor(s_post[:, :], mod2[:, 16:24], small[:, SMALL["g_post_2"][0]:SMALL["g_post_2"][0] + 8],
                                                ALU.mult), made2[KT - 1])
        act.wait(sp_done)
        read4 = [None, None]
        sqr = [None, None]
        finishing, outs_done = [], [None, None]

        def finish_tile(n, k, r):
            x = dve(lambda e: e.tensor_tensor(yo[:, n, k, :], yo[:, n, k, :], rs3[n][:, :], ALU.mult), r())
            x = dve(lambda e: e.tensor_tensor(yo[:, n, k, :], yo[:, n, k, :], xb[:, n, k, :], ALU.add), x, xb_in[n])
            if k % 2:
                outs_done[n] = sp(lambda e: e.dma_start(out[k - 1:k + 1, :, n * HT:(n + 1) * HT].rearrange("k p t -> p k t"),
                                                        yo[:, n, k - 1:k + 1, :]), x, sem=c_out[n], by=16)

        for n in range(2):
            accp = {"p": dve(lambda e, n=n: e.memset(acc3[n][:, :], 0.0))}

            def out_tile(j, slot, ready, used, n=n, accp=accp):
                s = j % 2
                mov = [(lambda k: mix2_hi[:, k, n * HT:(n + 1) * HT], lambda k: mix2_lo[:, k, n * HT:(n + 1) * HT])]
                product(g, w, slot, [ps[:, s, :]], mov, 0, KT, True, True, [ready] + ([read4[s]] if read4[s] else []), used,
                        made2 if (n == 0 and j == 0) else None)
                q = act(lambda e: e.activation(sq3[s][:, :], ps[:, s, :], ACT.Square), used, *([sqr[s]] if sqr[s] else []))
                read4[s] = act(lambda e: e.activation(yo[:, n, j, :], ps[:, s, :], ACT.Copy, scale=s_post[:, j:j + 1]), used)
                sqr[s] = accp["p"] = dve(lambda e: e.tensor_tensor(acc3[n][:, :], acc3[n][:, :], sq3[s][:, :], ALU.add), q, accp["p"])
                if n == 0:
                    load_xb(j)
                for _ in range(2):
                    if finishing:
                        finishing.pop(0)()

            w.run(8, None, out_tile, then=126 if n == 0 else -1)
            r = {}

            def norm_out(n=n, accp=accp, r=r):
                r["p"] = inverse_norm(acc3[n], 2 + n, rs3[n], accp["p"], tables=False)

            finishing += [norm_out] + [lambda n=n, k=k, r=r: finish_tile(n, k, lambda: r["p"]) for k in range(KT)]
        for fn in finishing:
            fn()
        sp.wait(*outs_done)
        emit(nc, g, ctx)





def emit(nc, g, ctx):
    block = ctx.enter_context(nc.Block())
    block.sync(lambda e: g.sp.run(e))
    block.gpsimd(lambda e: g.pool.run(e))
    block.scalar(lambda e: g.act.run(e))
    block.vector(lambda e: g.dve.run(e))
    block.tensor(lambda e: g.pe.run(e))



def blocks(w, cols=None):
    k, m = w.shape
    nk, nm = -(-k // P), -(-m // P)
    out = np.zeros((nk * P, nm * P), w.dtype)
    out[:k, :m] = w
    return out.reshape(nk, P, nm, P).transpose(2, 1, 0, 3).reshape(nm, P, nk * P)


def columns(v):
    return np.ascontiguousarray(v.reshape(-1, P).T)


def lay_out(i):
    f = np.float32
    w_in = i["w_in"][0]
    o = [0, 512, 640, 768, 1792, 2304, 2816]
    gates = np.zeros((D, P), f)
    gate_b = np.zeros((P,), f)
    for n, at_row in enumerate((0, 64, 32, 96)):
        gates[:, at_row:at_row + 4] = w_in[:, o[6] + 4 * n:o[6] + 4 * n + 4]
        gate_b[at_row:at_row + 4] = i["gate_b"][0, 4 * n:4 * n + 4]
    w1 = [w_in[:, o[3]:o[4]], w_in[:, :o[3]], w_in[:, o[4]:o[6]], gates]
    w_in2 = i["w_in_2"][0]
    p = [0, 1536, 1544, 2056, 2824, 3336]
    w2 = [w_in2[:, p[3]:p[4]], w_in2[:, p[1]:p[2]], w_in2[:, p[4]:], w_in2[:, p[2]:p[3]], w_in2[:, :p[1]]]
    gu = np.stack([blocks(i["w_gate"][0]), blocks(i["w_up"][0])], 1).reshape(2 * FT, P, D)
    down = np.zeros((KT, P, 24 * P), f)
    down[:, :, :FFN] = blocks(i["w_down"][0])
    down = down.reshape(KT, P, 3, D).transpose(0, 2, 1, 3).reshape(3 * KT, P, D)
    weights = np.concatenate([blocks(x) for x in w1] + [blocks(i["w_out"][0]), gu, down]
                             + [blocks(x) for x in w2] + [blocks(i["w_out_2"][0])])
    ada = np.concatenate([i["w_ada"][0], i["w_ada_2"][0]], 1)
    ada = np.ascontiguousarray(ada.reshape(KT, P, 36, CW).transpose(2, 1, 0, 3))
    x = np.ascontiguousarray(i["x"][0].T).reshape(KT, P, T)

    small = np.zeros((P, N_SMALL), f)

    def put(name, v):
        c, n = SMALL[name]
        small[:, c:c + n] = v

    for name in ("c", "c_2", "b_ada", "b_ada_2", "norm_mix_g", "norm_ffn_g", "final_norm_g", "g_pre_2", "g_post_2",
                 "conv_b", "mlstm_norm_g"):
        put(name, columns(i[name].reshape(-1)))
    put("qk_g", np.tile(np.stack([i["q_norm_g"][0]] * 4 + [i["k_norm_g"][0]], 1), (2, 1)))
    put("conv_w", i["conv_w"][0].reshape(5, KT, P).transpose(2, 1, 0).reshape(P, 40))
    put("gate_b", gate_b[:, None])
    fg = np.zeros((P, 1), f)
    fg[:8, 0] = i["b_fgate_2"][0]
    put("b_fgate", fg)
    put("sinks", np.broadcast_to(i["sinks_2"][0][None, :], (P, 8)))
    put("eps", EPS)
    put("tiny", 1e-37)
    put("one", 1.0)
    put("half_pi", np.pi / 2)
    half = 32
    freq = (f(10000.0) ** (-np.arange(half, dtype=f) / f(half))).astype(f)
    put("inv_freq", np.tile(freq, 4)[:, None])
    put("rope_sign", np.tile(np.repeat(np.array([-1.0, 1.0], f), 32), 2)[:, None])

    r = np.arange(P)
    row, c = r[:, None], r[None, :]
    consts = np.stack([row == c, np.ones((P, P)), row // 64 == c // 64, row == c,
                       np.where(c > row, NEG, 0), np.where(c < row, NEG, 0),
                       np.where(c <= row, NEG, 0), np.where(c >= row, NEG, 0)]).astype(f)

    inv = (f(10000.0) ** (-np.arange(0, 32, 2, dtype=f) / f(32))).astype(f)
    t = np.arange(T)
    ang = np.stack([(t // 64).astype(f)[None] * inv[:, None], (t % 64).astype(f)[None] * inv[:, None]])
    cos = np.repeat(np.cos(ang)[:, None], 2, 1).reshape(64, T)
    sin = np.stack([-np.sin(ang), np.sin(ang)], 1).reshape(64, T)
    rope = np.stack([np.tile(cos, (2, 1)), np.tile(sin, (2, 1))]).astype(f)

    sel = np.zeros((P, 8, P), f)
    for k in range(8):
        at_row = (k // 4) * 32 + k % 4
        sel[[at_row, 64 + at_row], k, :] = 1.0
    sel_f = np.zeros((P, 8, P), f)
    for k in range(8):
        sel_f[[k, 32 + k], k, :] = 1.0
    return {"weights": weights, "ada": ada, "x": x, "small": small, "consts": consts, "rope": rope,
            "sel": sel, "sel_f": sel_f, "positions": np.ascontiguousarray(i["positions_2"])}


def kernel(**inputs):
    import concourse.bacc as bacc
    from concourse.bass_utils import run_bass_kernel_spmd

    nc = bacc.Bacc("TRN2", target_bir_lowering=False, num_devices=1)
    arrays = {f"in_{n}": v for n, v in lay_out({n: np.asarray(v) for n, v in inputs.items()}).items()}
    ins = {n[3:]: nc.dram_tensor(n, v.shape, mybir.dt.from_np(v.dtype), kind="ExternalInput").ap() for n, v in arrays.items()}
    out = nc.dram_tensor("out_dram", (KT, P, T), F32, kind="ExternalOutput").ap()
    build(nc, ins, out)
    r = run_bass_kernel_spmd(nc, [arrays], core_ids=[0])
    return np.ascontiguousarray(r.results[0]["out_dram"].reshape(D, T).T)[None]
```
